# Optimizing a Trainium2 kernel written in Bass

```python
import math
import jax
import jax.numpy as jnp
from jax import lax
import numpy as np

D_MODEL = 1024
BATCH = 1
SEQ = 512
DEPTH = 1
DEC_BATCH = 8
DEC_SEQ = 4
PAST_LEN = 1024
PAGE_SIZE = 128

N_HEADS = 8
N_KV_HEADS = 2
HEAD_DIM = 64
GROUP = N_HEADS // N_KV_HEADS
ATT_WIDTH = N_HEADS * HEAD_DIM
KV_WIDTH = N_KV_HEADS * HEAD_DIM
N_NSA_BRANCH = 3
CMP_BLOCK = 32
CMP_STRIDE = 16
CMP_HIDDEN = 256
SEL_BLOCK = 64
SEL_TOPK = 16
WINDOW = 512
Q_BLOCK = 128
N_BUCKETS = 32
REL_MAX_DIST = 128
SSM_WIDTH = 512
SSM_GROUP_CH = 16
N_SSM_GROUPS = SSM_WIDTH // SSM_GROUP_CH
SSM_STATE = 64
D_FF = ((8 * D_MODEL + 3 * 256 - 1) // (3 * 256)) * 256
PLE_DIM = 256
EPS = 1e-6
NEG_INF = -1e30
FORCE_SCORE = 1e9

kernel_name = 'nsa_s5_gated_hybrid_step'

def rmsnorm(x, g):
    xf = x.astype(jnp.float32)
    y = xf * lax.rsqrt(jnp.mean(xf * xf, axis=-1, keepdims=True) + EPS)
    return (y * g.astype(jnp.float32)).astype(x.dtype)

def rel_bucket(dist):
    n = jnp.maximum(dist, 0)
    exact = N_BUCKETS // 2
    nf = jnp.maximum(n, 1).astype(jnp.float32)
    large = exact + (jnp.log(nf / exact) / math.log(REL_MAX_DIST / exact) * (N_BUCKETS - exact)).astype(jnp.int32)
    return jnp.where(n < exact, n, jnp.minimum(large, N_BUCKETS - 1))

def head_bias(rel_bias, dist):
    b = rel_bias[rel_bucket(dist)].astype(jnp.float32)
    tq, nk = dist.shape
    return jnp.transpose(b, (2, 0, 1)).reshape(N_KV_HEADS, GROUP, tq, nk)

def masked_softmax(s, mask):
    s = jnp.where(mask, s, NEG_INF)
    e = jnp.exp(s - jnp.max(s, axis=-1, keepdims=True)) * mask
    return e / jnp.maximum(jnp.sum(e, axis=-1, keepdims=True), 1e-30)

def compress(rows, pe, w1, w2):
    b, length = rows.shape[:2]
    n_chunks = length // CMP_STRIDE
    r = CMP_BLOCK // CMP_STRIDE
    n_cmp = n_chunks - r + 1
    ch = rows[:, :n_chunks * CMP_STRIDE].reshape(b, n_chunks, CMP_STRIDE, N_KV_HEADS, HEAD_DIM)
    blocks = jnp.concatenate([ch[:, i:i + n_cmp] for i in range(r)], axis=2)
    blocks = blocks + pe[:, None, :]
    flat = jnp.transpose(blocks, (0, 1, 3, 2, 4)).reshape(b, n_cmp, N_KV_HEADS, CMP_BLOCK * HEAD_DIM)
    return jax.nn.gelu(flat @ w1) @ w2

def sel_blocks(rows):
    b, length = rows.shape[:2]
    n_sel = -(-length // SEL_BLOCK)
    rows = jnp.pad(rows, ((0, 0), (0, n_sel * SEL_BLOCK - length), (0, 0), (0, 0)))
    return jnp.transpose(rows.reshape(b, n_sel, SEL_BLOCK, N_KV_HEADS, HEAD_DIM), (0, 3, 1, 2, 4))

def nsa_context(kc_rows, vc_rows, ks_rows, vs_rows, lw):
    kc = compress(kc_rows, lw['cmp_pe_k'], lw['cmp_w1_k'], lw['cmp_w2_k'])
    vc = compress(vc_rows, lw['cmp_pe_v'], lw['cmp_w1_v'], lw['cmp_w2_v'])
    c_start = jnp.arange(kc.shape[1]) * CMP_STRIDE
    c_end = c_start + CMP_BLOCK - 1
    ksb = sel_blocks(ks_rows)
    vsb = sel_blocks(vs_rows)
    s_start = jnp.arange(ksb.shape[2]) * SEL_BLOCK
    overlap = ((c_start[:, None] < s_start[None, :] + SEL_BLOCK) & (c_end[:, None] >= s_start[None, :])).astype(jnp.float32)
    return kc, vc, c_end, overlap, ksb, vsb

def nsa_block(q, q_pos, kc, vc, c_end, overlap, ksb, vsb, kw, vw, w_pos, rel_bias):
    b, tq = q.shape[:2]
    n_sel = ksb.shape[2]
    scale = HEAD_DIM ** -0.5
    tcol = q_pos[:, None]
    s_c = jnp.einsum('btkgd,bnkd->bkgtn', q, kc).astype(jnp.float32) * scale + head_bias(rel_bias, tcol - c_end[None, :])
    p_c = masked_softmax(s_c, c_end[None, :] <= tcol)
    o_c = jnp.einsum('bkgtn,bnkd->btkgd', p_c.astype(vc.dtype), vc)
    imp = jnp.einsum('bkgtn,nj->bktj', p_c, overlap)
    blk = jnp.arange(n_sel)[None, :]
    cur = tcol // SEL_BLOCK
    forced = (blk == 0) | (blk == cur) | (blk == cur - 1)
    valid = blk * SEL_BLOCK <= tcol
    score = jnp.where(valid, jnp.where(forced, FORCE_SCORE, imp), NEG_INF)
    _, idx = lax.top_k(score, min(SEL_TOPK, n_sel))
    b_ar = jnp.arange(b)[:, None, None, None]
    kv_ar = jnp.arange(N_KV_HEADS)[None, :, None, None]
    kg = ksb[b_ar, kv_ar, idx]
    vg = vsb[b_ar, kv_ar, idx]
    pos_s = idx[..., None] * SEL_BLOCK + jnp.arange(SEL_BLOCK)
    tb = jnp.transpose(rel_bias.reshape(N_BUCKETS, N_KV_HEADS, GROUP), (1, 0, 2))
    bias_s = jnp.moveaxis(tb[kv_ar[..., None], rel_bucket(q_pos[:, None, None] - pos_s)], -1, 2).astype(jnp.float32)
    s_s = jnp.einsum('btkgd,bktnsd->bkgtns', q, kg).astype(jnp.float32) * scale + bias_s
    mask_s = (pos_s <= q_pos[:, None, None])[:, :, None]
    p_s = masked_softmax(s_s.reshape(b, N_KV_HEADS, GROUP, tq, -1), mask_s.reshape(b, N_KV_HEADS, 1, tq, -1)).reshape(s_s.shape)
    o_s = jnp.einsum('bkgtns,bktnsd->btkgd', p_s.astype(vg.dtype), vg)
    dw = tcol - w_pos[None, :]
    s_w = jnp.einsum('btkgd,bwkd->bkgtw', q, kw).astype(jnp.float32) * scale + head_bias(rel_bias, dw)
    p_w = masked_softmax(s_w, (dw >= 0) & (dw < WINDOW) & (w_pos[None, :] >= 0))
    o_w = jnp.einsum('bkgtw,bwkd->btkgd', p_w.astype(vw.dtype), vw)
    return o_c, o_s, o_w

def nsa_prompt(q, ctx, kw, vw, rel_bias):
    kc, vc, c_end, overlap, ksb, vsb = ctx
    b, t = q.shape[:2]
    pad = ((0, 0), (WINDOW, 0), (0, 0), (0, 0))
    kw_pad = jnp.pad(kw, pad)
    vw_pad = jnp.pad(vw, pad)
    band = WINDOW + Q_BLOCK

    def block(i):
        start = i * Q_BLOCK
        qb = lax.dynamic_slice_in_dim(q, start, Q_BLOCK, axis=1)
        kwb = lax.dynamic_slice_in_dim(kw_pad, start, band, axis=1)
        vwb = lax.dynamic_slice_in_dim(vw_pad, start, band, axis=1)
        q_pos = start + jnp.arange(Q_BLOCK)
        w_pos = start - WINDOW + jnp.arange(band)
        return nsa_block(qb, q_pos, kc, vc, c_end, overlap, ksb, vsb, kwb, vwb, w_pos, rel_bias)

    outs = lax.map(block, jnp.arange(t // Q_BLOCK))
    return tuple(jnp.swapaxes(o, 0, 1).reshape(b, t, N_KV_HEADS, GROUP, HEAD_DIM) for o in outs)

def ssm_combine(e1, e2):
    a1r, a1i, b1r, b1i = e1
    a2r, a2i, b2r, b2i = e2
    return (a2r * a1r - a2i * a1i, a2r * a1i + a2i * a1r,
            a2r * b1r - a2i * b1i + b2r, a2r * b1i + a2i * b1r + b2i)

def ssm_branch(u, h0_re, h0_im, lw):
    b, t = u.shape[:2]
    ar = lw['ssm_a_re'].astype(jnp.float32)
    ai = lw['ssm_a_im'].astype(jnp.float32)
    dt = jnp.exp(lw['ssm_log_dt'].astype(jnp.float32))[:, None]
    mag = jnp.exp(ar * dt)
    abr, abi = mag * jnp.cos(ai * dt), mag * jnp.sin(ai * dt)
    den = ar * ar + ai * ai
    nr, ni = abr - 1.0, abi
    fr, fi = (nr * ar + ni * ai) / den, (ni * ar - nr * ai) / den
    br = lw['ssm_b_re'].astype(jnp.float32)
    bi = lw['ssm_b_im'].astype(jnp.float32)
    bbr = fr[..., None] * br - fi[..., None] * bi
    bbi = fr[..., None] * bi + fi[..., None] * br
    uf = u.astype(jnp.float32)
    xr = jnp.einsum('btgc,gpc->btgp', uf, bbr)
    xi = jnp.einsum('btgc,gpc->btgp', uf, bbi)
    h0r = h0_re.astype(jnp.float32)
    h0i = h0_im.astype(jnp.float32)
    xr = xr.at[:, 0].add(abr * h0r - abi * h0i)
    xi = xi.at[:, 0].add(abr * h0i + abi * h0r)
    shp = xr.shape
    _, _, hr, hi = lax.associative_scan(ssm_combine, (jnp.broadcast_to(abr, shp), jnp.broadcast_to(abi, shp), xr, xi), axis=1)
    y = (jnp.einsum('btgp,gcp->btgc', hr, lw['ssm_c_re'].astype(jnp.float32))
         - jnp.einsum('btgp,gcp->btgc', hi, lw['ssm_c_im'].astype(jnp.float32))
         + lw['ssm_d'].astype(jnp.float32) * uf)
    z = jax.nn.gelu(y.reshape(b, t, SSM_WIDTH)).astype(u.dtype)
    out = z * jax.nn.sigmoid(z @ lw['w_glu'] + lw['b_glu'])
    return out, hr[:, -1], hi[:, -1]

def layer_front(h, lw):
    b, t = h.shape[:2]
    z = rmsnorm(h, lw['attn_norm']) @ lw['w_in']
    sizes = [ATT_WIDTH] + [KV_WIDTH] * 6 + [N_HEADS * N_NSA_BRANCH, SSM_WIDTH, 2 * D_MODEL]
    cuts = [int(c) for c in np.cumsum(sizes)[:-1]]
    q, kc, vc, ks, vs, kw, vw, ng, su, mg = jnp.split(z, cuts, axis=-1)
    kvr = (b, t, N_KV_HEADS, HEAD_DIM)
    return (q.reshape(b, t, N_KV_HEADS, GROUP, HEAD_DIM), kc.reshape(kvr), vc.reshape(kvr), ks.reshape(kvr), vs.reshape(kvr),
            kw.reshape(kvr), vw.reshape(kvr), jax.nn.sigmoid(ng).reshape(b, t, N_KV_HEADS, GROUP, N_NSA_BRANCH),
            su.reshape(b, t, N_SSM_GROUPS, SSM_GROUP_CH), jax.nn.sigmoid(mg).reshape(b, t, 2, D_MODEL))

def layer_back(h, outs, ng, so, mg, p_l, lw):
    o_c, o_s, o_w = outs
    b, t = h.shape[:2]
    o = ng[..., 0:1] * o_c + ng[..., 1:2] * o_s + ng[..., 2:3] * o_w
    a = o.reshape(b, t, ATT_WIDTH) @ lw['w_att_br']
    s = so @ lw['w_ssm_br']
    h = h + (mg[:, :, 0] * a + mg[:, :, 1] * s) @ lw['w_o']
    f = rmsnorm(h, lw['ffn_norm'])
    h = h + (jax.nn.silu(f @ lw['w_ffn_gate']) * (f @ lw['w_ffn_up'])) @ lw['w_ffn_down']
    g = jax.nn.sigmoid(rmsnorm(h, lw['ple_norm']) @ lw['w_ple_gate'])
    return h + g * (p_l @ lw['w_ple'])

def with_past(pool, page_table, new):
    rows = pool[page_table]
    bd, n_pages, page = rows.shape[:3]
    return jnp.concatenate([rows.reshape(bd, n_pages * page, N_KV_HEADS, HEAD_DIM), new], axis=1)

def setup_inputs(seed: int = 0) -> dict:
    key = jax.random.key(seed)
    keys = iter(jax.random.split(key, 64))
    nrm = lambda shape, scale=1.0: scale * jax.random.normal(next(keys), shape, jnp.float32)
    n_pages = PAST_LEN // PAGE_SIZE
    n_used = DEC_BATCH * n_pages
    n_phys = (5 * n_used + 3) // 4
    win_buf = min(WINDOW, PAST_LEN)
    paged = (DEPTH, n_phys, PAGE_SIZE, N_KV_HEADS, HEAD_DIM)
    wbuf = (DEPTH, DEC_BATCH, win_buf, N_KV_HEADS, HEAD_DIM)
    sst = (DEPTH, DEC_BATCH, N_SSM_GROUPS, SSM_STATE)
    gp = (DEPTH, N_SSM_GROUPS, SSM_STATE)
    return {
        'x_prompt': nrm((BATCH, SEQ, D_MODEL)),
        'x_sample': nrm((DEC_BATCH, DEC_SEQ, D_MODEL)),
        'cache_k_cmp': nrm(paged),
        'cache_v_cmp': nrm(paged),
        'cache_k_sel': nrm(paged),
        'cache_v_sel': nrm(paged),
        'cache_k_win': nrm(wbuf),
        'cache_v_win': nrm(wbuf),
        'state_ssm_re': nrm(sst, 0.3),
        'state_ssm_im': nrm(sst, 0.3),
        'page_table': jax.random.permutation(next(keys), n_phys)[:n_used].reshape(DEC_BATCH, n_pages).astype(jnp.int32),
        'p_prompt': nrm((DEPTH, BATCH, SEQ, PLE_DIM)),
        'p_sample': nrm((DEPTH, DEC_BATCH, DEC_SEQ, PLE_DIM)),
        'rel_bias': nrm((N_BUCKETS, N_HEADS), 0.5),
        'final_norm': 1.0 + nrm((D_MODEL,), 0.02),
        'attn_norm': 1.0 + nrm((DEPTH, D_MODEL), 0.02),
        'w_in': nrm((DEPTH, D_MODEL, ATT_WIDTH + 6 * KV_WIDTH + N_HEADS * N_NSA_BRANCH + SSM_WIDTH + 2 * D_MODEL), D_MODEL ** -0.5),
        'cmp_pe_k': nrm((DEPTH, CMP_BLOCK, HEAD_DIM), 0.1),
        'cmp_w1_k': nrm((DEPTH, CMP_BLOCK * HEAD_DIM, CMP_HIDDEN), (CMP_BLOCK * HEAD_DIM) ** -0.5),
        'cmp_w2_k': nrm((DEPTH, CMP_HIDDEN, HEAD_DIM), CMP_HIDDEN ** -0.5),
        'cmp_pe_v': nrm((DEPTH, CMP_BLOCK, HEAD_DIM), 0.1),
        'cmp_w1_v': nrm((DEPTH, CMP_BLOCK * HEAD_DIM, CMP_HIDDEN), (CMP_BLOCK * HEAD_DIM) ** -0.5),
        'cmp_w2_v': nrm((DEPTH, CMP_HIDDEN, HEAD_DIM), CMP_HIDDEN ** -0.5),
        'ssm_a_re': -0.5 + nrm(gp, 0.01),
        'ssm_a_im': jnp.pi * jnp.broadcast_to(jnp.arange(SSM_STATE, dtype=jnp.float32), gp) + nrm(gp, 0.01),
        'ssm_log_dt': jax.random.uniform(next(keys), (DEPTH, N_SSM_GROUPS), jnp.float32, math.log(1e-3), math.log(1e-1)),
        'ssm_b_re': nrm((DEPTH, N_SSM_GROUPS, SSM_STATE, SSM_GROUP_CH), (2 * SSM_GROUP_CH) ** -0.5),
        'ssm_b_im': nrm((DEPTH, N_SSM_GROUPS, SSM_STATE, SSM_GROUP_CH), (2 * SSM_GROUP_CH) ** -0.5),
        'ssm_c_re': nrm((DEPTH, N_SSM_GROUPS, SSM_GROUP_CH, SSM_STATE), (2 * SSM_STATE) ** -0.5),
        'ssm_c_im': nrm((DEPTH, N_SSM_GROUPS, SSM_GROUP_CH, SSM_STATE), (2 * SSM_STATE) ** -0.5),
        'ssm_d': nrm((DEPTH, N_SSM_GROUPS, SSM_GROUP_CH)),
        'w_glu': nrm((DEPTH, SSM_WIDTH, SSM_WIDTH), SSM_WIDTH ** -0.5),
        'b_glu': nrm((DEPTH, SSM_WIDTH), 0.01),
        'w_att_br': nrm((DEPTH, ATT_WIDTH, D_MODEL), ATT_WIDTH ** -0.5),
        'w_ssm_br': nrm((DEPTH, SSM_WIDTH, D_MODEL), SSM_WIDTH ** -0.5),
        'w_o': nrm((DEPTH, D_MODEL, D_MODEL), D_MODEL ** -0.5),
        'ffn_norm': 1.0 + nrm((DEPTH, D_MODEL), 0.02),
        'w_ffn_gate': nrm((DEPTH, D_MODEL, D_FF), D_MODEL ** -0.5),
        'w_ffn_up': nrm((DEPTH, D_MODEL, D_FF), D_MODEL ** -0.5),
        'w_ffn_down': nrm((DEPTH, D_FF, D_MODEL), D_FF ** -0.5),
        'ple_norm': 1.0 + nrm((DEPTH, D_MODEL), 0.02),
        'w_ple_gate': nrm((DEPTH, D_MODEL, D_MODEL), D_MODEL ** -0.5),
        'w_ple': nrm((DEPTH, PLE_DIM, D_MODEL), PLE_DIM ** -0.5),
    }

def reference(x_prompt, x_sample, cache_k_cmp, cache_v_cmp, cache_k_sel, cache_v_sel, cache_k_win, cache_v_win,
              state_ssm_re, state_ssm_im, page_table, p_prompt, p_sample, rel_bias, final_norm, attn_norm, w_in,
              cmp_pe_k, cmp_w1_k, cmp_w2_k, cmp_pe_v, cmp_w1_v, cmp_w2_v, ssm_a_re, ssm_a_im, ssm_log_dt,
              ssm_b_re, ssm_b_im, ssm_c_re, ssm_c_im, ssm_d, w_glu, b_glu, w_att_br, w_ssm_br, w_o,
              ffn_norm, w_ffn_gate, w_ffn_up, w_ffn_down, ple_norm, w_ple_gate, w_ple):
    b_p, t_p = x_prompt.shape[:2]
    t_s = x_sample.shape[1]
    past_len = page_table.shape[1] * cache_k_cmp.shape[2]
    win_buf = cache_k_win.shape[2]
    keep_p = min(WINDOW, t_p)
    hp, hs = x_prompt, x_sample
    rec_p, rec_s = [], []
    for l in range(DEPTH):
        lw = {'attn_norm': attn_norm[l], 'w_in': w_in[l],
              'cmp_pe_k': cmp_pe_k[l], 'cmp_w1_k': cmp_w1_k[l], 'cmp_w2_k': cmp_w2_k[l],
              'cmp_pe_v': cmp_pe_v[l], 'cmp_w1_v': cmp_w1_v[l], 'cmp_w2_v': cmp_w2_v[l],
              'ssm_a_re': ssm_a_re[l], 'ssm_a_im': ssm_a_im[l], 'ssm_log_dt': ssm_log_dt[l],
              'ssm_b_re': ssm_b_re[l], 'ssm_b_im': ssm_b_im[l], 'ssm_c_re': ssm_c_re[l], 'ssm_c_im': ssm_c_im[l],
              'ssm_d': ssm_d[l], 'w_glu': w_glu[l], 'b_glu': b_glu[l],
              'w_att_br': w_att_br[l], 'w_ssm_br': w_ssm_br[l], 'w_o': w_o[l],
              'ffn_norm': ffn_norm[l], 'w_ffn_gate': w_ffn_gate[l], 'w_ffn_up': w_ffn_up[l], 'w_ffn_down': w_ffn_down[l],
              'ple_norm': ple_norm[l], 'w_ple_gate': w_ple_gate[l], 'w_ple': w_ple[l]}
        q, kc, vc, ks, vs, kw, vw, ng, su, mg = layer_front(hp, lw)
        outs = nsa_prompt(q, nsa_context(kc, vc, ks, vs, lw), kw, vw, rel_bias)
        h0 = jnp.zeros((b_p, N_SSM_GROUPS, SSM_STATE), jnp.float32)
        so, sr, si = ssm_branch(su, h0, h0, lw)
        hp = layer_back(hp, outs, ng, so, mg, p_prompt[l], lw)
        rec_p.append((kc, vc, ks, vs, kw[:, t_p - keep_p:], vw[:, t_p - keep_p:], sr, si))
        q, kc, vc, ks, vs, kw, vw, ng, su, mg = layer_front(hs, lw)
        ctx = nsa_context(with_past(cache_k_cmp[l], page_table, kc), with_past(cache_v_cmp[l], page_table, vc),
                          with_past(cache_k_sel[l], page_table, ks), with_past(cache_v_sel[l], page_table, vs), lw)
        kw_all = jnp.concatenate([cache_k_win[l], kw], axis=1)
        vw_all = jnp.concatenate([cache_v_win[l], vw], axis=1)
        w_pos = past_len - win_buf + jnp.arange(win_buf + t_s)
        q_pos = past_len + jnp.arange(t_s)
        outs = nsa_block(q, q_pos, *ctx, kw_all, vw_all, w_pos, rel_bias)
        so, sr, si = ssm_branch(su, state_ssm_re[l], state_ssm_im[l], lw)
        hs = layer_back(hs, outs, ng, so, mg, p_sample[l], lw)
        rec_s.append((kc, vc, ks, vs, kw_all[:, t_s:], vw_all[:, t_s:], sr, si))
    y_prompt = rmsnorm(hp, final_norm)
    y_sample = rmsnorm(hs, final_norm)
    nk_cmp_p, nv_cmp_p, nk_sel_p, nv_sel_p, nk_win_p, nv_win_p, ns_re_p, ns_im_p = [jnp.stack(t) for t in zip(*rec_p)]
    nk_cmp_s, nv_cmp_s, nk_sel_s, nv_sel_s, nk_win_s, nv_win_s, ns_re_s, ns_im_s = [jnp.stack(t) for t in zip(*rec_s)]
    return (y_prompt, y_sample,
            nk_cmp_p, nv_cmp_p, nk_sel_p, nv_sel_p, nk_win_p, nv_win_p, ns_re_p, ns_im_p,
            nk_cmp_s, nv_cmp_s, nk_sel_s, nv_sel_s, nk_win_s, nv_win_s, ns_re_s, ns_im_s)


_drawn_inputs = setup_inputs


def setup_inputs(seed=0):
    import zlib

    import numpy as np

    out = dict(_drawn_inputs(seed))
    spreads = {}
    factors = {'cache_k_cmp': 3.87,
     'cache_k_sel': 4.374,
     'cache_v_sel': 3.471,
     'final_norm': 8.268,
     'attn_norm': 2.812,
     'cmp_pe_k': 8.0,
     'cmp_pe_v': 4.837,
     'ssm_a_re': 16.012,
     'b_glu': 32.388,
     'ffn_norm': 4.02,
     'ple_norm': 64.0}
    for name, (base, spread) in spreads.items():
        noise = np.random.default_rng([zlib.crc32(name.encode()), seed]).standard_normal(out[name].shape)
        drawn = base * np.exp(spread * noise) if base else spread * noise
        out[name] = jnp.asarray(drawn.astype(out[name].dtype))
    for name, factor in factors.items():
        out[name] = (out[name] * factor).astype(out[name].dtype)
    return out
```

```python
import math
from contextlib import ExitStack

import numpy as np

import concourse.bass as bass
from concourse import mybir

F32 = mybir.dt.float32
I32 = mybir.dt.int32
U32 = mybir.dt.uint32
ALU = mybir.AluOpType
ACT = mybir.ActivationFunctionType
AX = mybir.AxisListType

P = 128
D = 1024
T = 512
DB, DT = 8, 4
NS = DB * DT
TT = T + NS
HT = TT // 2
PAST = 1024
PAGE = 128
NPAGES = PAST // PAGE
HEADS, KV, HD = 8, 2, 64
G = HEADS // KV
WIN = 512
SEL = 64
NSEL = PAST // SEL + 1
CH = 16
CB_P = T // CH - 1
CB_S = PAST // CH - 1
HID = 256
SG, SC, SP_ = 32, 16, 64
FF = 2816
PLE = 256
NBUCKET = 32
KC = D // P
FC = FF // P
EPS = 1e-6
MASK = -1e30
TILES = T // P
DMAX = PAST + DT - 1
TW = 912
TBASE = DMAX - 3 * P
LINE = TBASE + TW + 1
SHIFTS = 16
LPITCH = LINE + SHIFTS
RING = 4
SLAB = 2048
C_Q, C_KV, C_NG, C_SU, C_MG = 0, 512, 1280, 1304, 1816
W_IN = C_MG + 2 * D
MAGIC = 12582912.0
TWO_PI = 2.0 * math.pi
TP_HI = float(np.float32(6.28125))
TP_LO = float(np.float32(TWO_PI - 6.28125))
K_ID, K_G, K_SM, K_WM, K_IO, K_MOD = 0, 128, 256, 320, 324, 338
K_N = 340


def bucket_table():
    n = np.arange(LINE)
    dist = DMAX - n
    d = np.maximum(dist, 0)
    exact = NBUCKET // 2
    nf = np.maximum(d, 1).astype(np.float32)
    large = exact + (np.log(nf / np.float32(exact)) / np.float32(math.log(128 / exact)) * np.float32(NBUCKET - exact)).astype(np.int32)
    b = np.where(d < exact, d, np.minimum(large, NBUCKET - 1))
    out = np.zeros((NBUCKET + 1, LINE), np.float32)
    out[b[dist >= 0], n[dist >= 0]] = 8.0
    out[NBUCKET, dist < 0] = MASK
    return out


def constants():
    c = np.zeros((P, K_N), np.float32)
    r = np.arange(P)
    c[:, K_ID:K_ID + P] = np.eye(P)
    b, kv, g, t = r // 32, r // 16 % 2, r // 4 % 4, r % 4
    same = (b[:, None] == b) & (kv[:, None] == kv) & (t[:, None] == t)
    c[:, K_G:K_G + P] = same
    for tile in range(2):
        for col in range(NS):
            c[:, K_SM + tile * NS + col] = np.where(4 * tile + b == col // DT, 0.0, MASK)
    for u in range(DT):
        c[:, K_WM + u] = np.where(u <= t, MASK, 0.0)
    c[:, K_IO:K_IO + NSEL - 3] = np.arange(1, NSEL - 2)
    c[:, K_MOD] = r % 16
    c[:, K_MOD + 1] = r % 8
    return c


def at(ap, offset, dims):
    return bass.AP(ap.tensor, ap.offset + offset, [list(ap.ap[0])] + dims)


def wide(ap, n, axis=None):
    dims = [list(x) for x in ap.ap]
    dims.insert(len(dims) if axis is None else axis, [0, n])
    return bass.AP(ap.tensor, ap.offset, dims)


def plan_gemms():
    groups, slabs = [], []

    def slab(kind, n):
        slabs.append((kind, n))
        return len(slabs) - 1

    def group(name, steps):
        groups.append((name, steps))

    group(("norm", 0), None)
    for s in range(2):
        w = slab("q", s)
        for m in range(2):
            group(("z", 2 * s + m), [(w, k * 256 + m * P, P, k) for k in range(KC)])
    for s in range(3):
        w = slab("kv", s)
        for m in range(2):
            group(("z", 4 + 2 * s + m), [(w, k * 256 + m * P, P, k) for k in range(KC)])
    for s in range(2):
        w = slab("su", s)
        for m in range(2):
            group(("z", 10 + 2 * s + m), [(w, k * 256 + m * P, P, k) for k in range(KC)])
    w = slab("ng", 0)
    group(("ng", 0), [(w, k * 24, 24, k) for k in range(KC)])
    w = slab("glu", 0)
    for m in range(4):
        group(("glu", m), [(w, k * 512 + m * P, P, k) for k in range(4)])
    for s in range(2):
        for half in range(2):
            g0, g1 = slab("mg0", 2 * s + half), slab("mg1", 2 * s + half)
            a = slab("att", 2 * s + half)
            for m in range(2):
                c = 4 * s + 2 * half + m
                group(("mg0", c), [(g0, k * 256 + m * P, P, k) for k in range(KC)])
                group(("mg1", c), [(g1, k * 256 + m * P, P, k) for k in range(KC)])
                group(("att", c), [(a, k * 256 + m * P, P, k) for k in range(4)])
                group(("ssm", c), [(a, 1024 + k * 256 + m * P, P, k) for k in range(4)])
    for s in range(4):
        w = slab("wo", s)
        for m in range(2):
            group(("wo", 2 * s + m), [(w, k * 256 + m * P, P, k) for k in range(KC)])
    for k in range(2):
        group(("pt", k), None)
    group(("norm", 1), None)
    for s in range(11):
        a, b = slab("gate", s), slab("up", s)
        for m in range(2):
            group(("gate", 2 * s + m), [(a, k * 256 + m * P, P, k) for k in range(KC)])
            group(("up", 2 * s + m), [(b, k * 256 + m * P, P, k) for k in range(KC)])
    for m in range(KC):
        a, b = slab("down", 2 * m), slab("down", 2 * m + 1)
        group(("down", m), [(a, k * P, P, k) for k in range(11)] + [(b, k * P, P, 11 + k) for k in range(11)])
    group(("norm", 2), None)
    for s in range(4):
        w = slab("pg", s)
        for m in range(2):
            group(("pg", 2 * s + m), [(w, k * 256 + m * P, P, k) for k in range(KC)])
            group(("ple", 2 * s + m), [(None, k * D + (2 * s + m) * P, P, k) for k in range(2)])
    group(("norm", 3), None)
    return groups, slabs


def build(nc, a):
    groups, slabs = plan_gemms()
    pair_of, use_of, count = {}, {}, [0] * 4
    last_use = {}
    landed_at, total = [], [0] * RING
    for n, (kind, _) in enumerate(slabs):
        total[n % RING] += 16 * {"q": 4, "att": 3}.get(kind, 1)
        landed_at.append(total[n % RING])
    for n, (name, steps) in enumerate(groups):
        pair = n % 4
        count[pair] += 1
        pair_of[name], use_of[name] = pair, count[pair]
        for st in steps or []:
            if st[0] is not None:
                last_use[st[0]] = name

    bias_line = nc.dram_tensor("bias_line", (HEADS, SHIFTS, LPITCH), F32, kind="Internal").ap()
    gate_rows = nc.dram_tensor("gate_rows", (NS, 24), F32, kind="Internal").ap()
    h_spill = nc.dram_tensor("h_spill", (P, KC * TT), F32, kind="Internal").ap()

    with ExitStack() as ctx:
        def sb(name, shape, dt=F32):
            return ctx.enter_context(nc.sbuf_tensor(name, shape, dt))

        def sem(name):
            return ctx.enter_context(nc.semaphore(name))

        kc_ = sb("consts", [P, K_N])[:, :]
        ident = kc_[:, K_ID:K_ID + P]
        ones = sb("ones", [P, P])[:, :]
        vec = sb("vec", [P, 120])[:, :]
        sp = sb("ssm_params", [P, 34, 16])
        uT = sb("uT", [P, KC, TT])
        zq = sb("zq", [P, 4, TT])
        zkv = sb("zkv", [P, 6, TT])
        zsu = sb("zsu", [P, 4, TT])
        ring = sb("ring", [P, RING, SLAB])
        vtok = sb("vtok", [P, 5, 2, P])
        kcT_s = sb("kcT_s", [P, 2, 252])
        kcT_p = sb("kcT_p", [P, 32])
        vc_s = sb("vc_s", [64, DB, P])
        vc_p = sb("vc_p", [P, HD])
        gates = sb("gates", [P, TILES + 1, 24])
        gates_s = sb("gates_s", [P, 2, 3])
        small = sb("small", [P, 96])
        idx = sb("idx", [P, 16], I32)
        pages = sb("page_rows", [16, 32], I32)
        log_dt = sb("log_dt", [16, 2])
        eps_t = sb("eps_t", [P, 1])
        AR = 28400
        arena = sb("arena", [P, AR])
        oT = zkv[:, 0:4, :]
        KS, KW = 4, 5
        ZSLOT = [0, 1, 4, 2, 5, 3]

        def ar(off, *dims):
            n = int(np.prod(dims))
            assert off + n <= AR
            v = arena[:, off:off + n]
            if len(dims) == 2:
                return v.rearrange("p (a b) -> p a b", b=dims[1])
            if len(dims) == 3:
                return v.rearrange("p (a b c) -> p a b c", b=dims[1], c=dims[2])
            if len(dims) == 4:
                return v.rearrange("p (a b c d) -> p a b c d", b=dims[1], c=dims[2], d=dims[3])
            return v

        xtok = ar(0, 5, D)
        hT0 = ar(5120, KC, TT)
        hot = arena[0:33, 20480:20480 + LINE]
        relb = arena[0:33, 22100:22100 + HEADS]
        line = arena[0:HEADS, 22120:22120 + LINE]
        nat = ar(23700, 256)[:, 0:P]
        spread = ar(25500, 3, P)
        rt0, rs0 = ar(26100, TT), ar(27200, TT)
        zng = arena[0:24, 24900:24900 + TT]
        tmp = ar(23840, 4, 16, 16)
        br_, bi_ = ar(16384, 16, 16), ar(16640, 16, 16)
        bbr, bbi = ar(16896, 16, 16), ar(17152, 16, 16)
        bt_ = ar(17408, 16, 16)
        bdr, bdi = ar(17664, 16, 32), ar(18176, 16, 32)
        cnat = ar(18688, 2, 4, P)
        h0nat = ar(19712, 2, P)
        tokst = ar(9472, 5, 512)
        BT = ar(0, 2, 4, P)
        CT = ar(1024, 2, 16, 32)
        Jt = ar(2048, 2, 16, 32)
        St = ar(3072, 2, 16, 16)
        Hs = ar(3584, 2, 16, NS)
        h0T = ar(4608, 2, P)
        rot = ar(5120, 6, T)
        Et = ar(8192, 2, 2, T)
        Hp = ar(10240, 2, 2, T)
        ptmp = ar(27136, 2, T)
        hfin = sb("hfin", [P, 2, 16])
        hfin_s = ar(26752, 2, P)
        hout = ar(27136, 4, P)
        glu_sig = ar(10240, 4, TT)
        w1 = ar(12288, 16, HID)
        XT = ar(16384, 8, KV, 256)
        raw = ar(20480, SLAB)
        raw2 = ar(22528, SLAB)
        Hh = ar(24576, 2, 504)
        XP = ar(25600, 16, 64)
        Hq = ar(26624, 2, 62)
        w2 = sb("w2", [P, 2, 2, HD])
        pb = sb("pe_bias", [P, 4])
        TZ = ar(0, HEADS, TW)
        Ssb = ar(7304, 4, T)
        Psb = ar(9352, 4, T)
        PTs = ar(11400, 4, T)
        dg = ar(13448, 4, P)
        PTc = ar(13960, TILES, 2, P)
        cs, ce = ar(14984, HEADS, 32), ar(15240, HEADS, 32)
        ksel = ar(16384, 2, 1024)
        vsel = ar(18432, 4, 1024)
        kwin = ar(22528, 4, 512)
        vwin = ar(24576, 4, 512)
        biasS = ar(26624, 1056)
        KT = ar(0, 2, 1024)
        KTw = ar(2048, 2, 512)
        bd = ar(3072, 1056)
        bw = ar(4128, 544)
        SS = ar(4672, 1056)
        SW = ar(5728, 544)
        PS_ = ar(6272, 1056)
        PW = ar(7328, 544)
        cc = ar(7872, 3, 64)
        PTS = ar(8064, 15, P)
        dgs = ar(9984, 3, P)
        Qb = ar(10368, DB, 32)
        hT = ar(0, KC, TT)
        mT = ar(KC * TT, KC, TT)
        sig = ar(8704, 4, TT)
        mid = ar(10880, FC, TT)
        sil = ar(22848, 2, TT)
        pT = ar(23936, 2, TT)
        wple = ar(25024, SLAB)
        rt, rs = ar(27136, TT), ar(27680, TT)
        ptok = ar(10880, 5, PLE)
        ytok = ar(KC * TT, 2, D)

        pair = [ctx.enter_context(nc.psum_tensor(f"pair{i}", [P, 2, 512], F32)) for i in range(4)]

        def bank(b):
            return pair[b // 2][:, b % 2, :]

        slab_landed = [sem(f"slab_landed{i}") for i in range(RING)]
        sum_done = [sem(f"sum_done{i}") for i in range(4)]
        taken = [sem(f"taken{i}") for i in range(4)]
        names = """x0 const_in hot_in nat_in ssm_in ones_set line_done line_copied line_out turned_x copied_x
            vec_turned vec_copied squares normed h_out kvt_done tokst_copied vtok_copied kv_out v_step a_step g_step p_step
            ldt theta_ready sin_done bd_ready bd_turned bd_copied c_turned c_copied h0_turned h0_copied
            gate_out gate_in gates_turned gates_copied rows_in spread_ready spread_turned idx_ready
            w1_in w2_in raw_in raw_copied raw_turned turn_copied hid_done hid_taken c2_done c2_taken xp_ready
            xs_done samples_done ys_done ys_taken x_done x_taken E_ready E_used h_ready y_done y_taken z_ready
            fin_ready fin_turned fin_copied fin_out glu_ready
            toep_in cs_done cmax_done cexp_done cnorm_done cpt_done cpt_copied
            s_done s_taken exp_done diag_ready pt_done pt_copied o_done o_taken
            kwin_in vwin_in biasS_in tb_done tb_copied qb_ready sc_done cmin_done cexps impsum_ready
            imp_done bd_seen pc_ready pc_done pc_copied ss_done ss_taken sexp sdiag so_done so_taken
            h_in p_in wple_in mixed h_new y_turned y_copied_v y_copied_a win_out fix_ready""".split()
        S = {n: sem(n) for n in names}
        ksel_in = [sem(f"ksel_in{i}") for i in range(2)]
        y_stored = [sem(f"y_stored{i}") for i in range(2)]
        vsel_in = [sem(f"vsel_in{i}") for i in range(4)]

        xp_t = a["x_prompt"].rearrange("b (t p) d -> p (b t) d", p=P)
        w_in = a["w_in"].rearrange("l (k p) n -> p (l k) n", p=P)

        def done(name):
            return sum_done[pair_of[name]], use_of[name]

        def out_of(name):
            return taken[pair_of[name]], use_of[name]

        def keys_turned(b):
            return 3 * (b + 1) + (4 if b >= 4 else 0)

        def both(pr):
            return pair[pr][:, :, 0:HT]

        def halves(v):
            return v.rearrange("p (h n) -> p h n", h=2)

        block = ctx.enter_context(nc.Block())

        @block.sync
        def _(eng):
            def wide_cols(w, c0, n, k=KC):
                return w[:, 0:k, c0:c0 + n]

            gate_w = a["w_ffn_gate"].rearrange("l (k p) n -> p (l k) n", p=P)
            up_w = a["w_ffn_up"].rearrange("l (k p) n -> p (l k) n", p=P)
            down_w = a["w_ffn_down"].rearrange("l (k p) n -> p (l k) n", p=P)
            o_w = a["w_o"].rearrange("l (k p) n -> p (l k) n", p=P)
            glu_w = a["w_glu"].rearrange("l (k p) n -> p (l k) n", p=P)
            pg_w = a["w_ple_gate"].rearrange("l (k p) n -> p (l k) n", p=P)
            ssm_w = a["w_ssm_br"].rearrange("l (k p) n -> p (l k) n", p=P)

            def load_slab(n):
                kind, s = slabs[n]
                slot = n % RING
                if n >= RING:
                    eng.wait_ge(*done(last_use[n - RING]))
                dst = ring[:, slot, :]
                landed = slab_landed[slot]
                if kind == "q":
                    v = dst.rearrange("p (k m h d) -> p k m h d", k=KC, m=2, h=2)
                    for m in range(2):
                        for h in range(2):
                            c0 = (2 * s + m + G * h) * HD
                            ins = eng.dma_start(v[:, :, m, h, :], w_in[:, :, c0:c0 + HD])
                            ins.then_inc(landed, 16)
                    return
                if kind in ("kv", "su", "mg0", "mg1", "gate", "up", "wo", "pg"):
                    src, c0 = {"kv": (w_in, C_KV), "su": (w_in, C_SU), "mg0": (w_in, C_MG), "mg1": (w_in, C_MG + D),
                               "gate": (gate_w, 0), "up": (up_w, 0), "wo": (o_w, 0), "pg": (pg_w, 0)}[kind]
                    eng.dma_start(dst.rearrange("p (k n) -> p k n", k=KC),
                                  wide_cols(src, c0 + 256 * s, 256)).then_inc(landed, 16)
                elif kind == "ng":
                    eng.dma_start(dst[:, 0:KC * 24].rearrange("p (k n) -> p k n", k=KC),
                                  wide_cols(w_in, C_NG, 24)).then_inc(landed, 16)
                elif kind == "glu":
                    eng.dma_start(dst.rearrange("p (k n) -> p k n", k=4), glu_w).then_inc(landed, 16)
                elif kind == "att":
                    v = dst[:, 0:1024].rearrange("p (k n) -> p k n", k=4)
                    for h in range(2):
                        rows = a["w_att_br"][0, h * 256:(h + 1) * 256, 256 * s:256 * s + 256]
                        eng.dma_start(v[64 * h:64 * h + 64, :, :],
                                      rows.rearrange("(k p) n -> p k n", p=HD)).then_inc(landed, 16)
                    eng.dma_start(dst[:, 1024:2048].rearrange("p (k n) -> p k n", k=4),
                                  ssm_w[:, :, 256 * s:256 * s + 256]).then_inc(landed, 16)
                elif kind == "down":
                    m, half = s // 2, s % 2
                    eng.dma_start(dst[:, 0:11 * P].rearrange("p (k n) -> p k n", k=11),
                                  down_w[:, 11 * half:11 * half + 11, m * P:(m + 1) * P]).then_inc(landed, 16)

            for t in range(TILES):
                eng.dma_start(xtok[:, t, :], xp_t[:, t, :]).then_inc(S["x0"], 16)
            eng.dma_start(xtok[0:NS, 4, :], a["x_sample"].rearrange("b t d -> (b t) d")).then_inc(S["x0"], 16)
            eng.dma_start(kc_, a["consts"]).then_inc(S["const_in"], 16)
            rows = lambda n, k: a[n].rearrange("l (r p) -> (l r) p", p=P)
            at_row = 0
            for n in ("attn_norm", "ffn_norm", "ple_norm"):
                eng.dma_start(nat[at_row:at_row + KC, :], rows(n, KC)).then_inc(S["nat_in"], 16)
                at_row += KC
            eng.dma_start(nat[24:32, :], a["final_norm"].rearrange("(r p) -> r p", p=P)).then_inc(S["nat_in"], 16)
            eng.dma_start(nat[32:36, :], rows("b_glu", 4)).then_inc(S["nat_in"], 16)
            eng.dma_start(nat[36:40, :], a["ssm_d"].rearrange("l (r g) c -> (l r) (g c)", r=4)).then_inc(S["nat_in"], 16)
            eng.dma_start(nat[40:56, :], a["ssm_a_re"].rearrange("l (j g) p -> (l j) (g p)", g=2)).then_inc(S["nat_in"], 16)
            eng.dma_start(nat[56:72, :], a["ssm_a_im"].rearrange("l (j g) p -> (l j) (g p)", g=2)).then_inc(S["nat_in"], 16)
            eng.dma_start(nat[72:88, :], a["cmp_pe_k"].rearrange("l (k r) d -> (l k) (r d)", r=2)).then_inc(S["nat_in"], 16)
            eng.dma_start(nat[88:104, :], a["cmp_pe_v"].rearrange("l (k r) d -> (l k) (r d)", r=2)).then_inc(S["nat_in"], 16)
            eng.dma_start(pages[0:8, 0:8], a["page_table"]).then_inc(S["rows_in"], 16)
            eng.dma_start(pages[0:4, 16:32], a["page_table"].rearrange("(a b) n -> a (b n)", b=2)).then_inc(S["rows_in"], 16)
            eng.dma_start(log_dt[:, :], a["ssm_log_dt"].rearrange("l (j g) -> (l j) g", g=2)).then_inc(S["rows_in"], 16)
            eng.dma_start(hot, a["buckets"]).then_inc(S["hot_in"], 16)
            eng.dma_start(relb[0:NBUCKET, :], a["rel_bias"]).then_inc(S["hot_in"], 16)
            load_slab(0)
            load_slab(1)
            for q, (src, dst) in enumerate((("ssm_b_re", br_), ("ssm_b_im", bi_))):
                eng.dma_start(dst, a[src].rearrange("l (j g) p c -> (g p) (l j) c", g=2)).then_inc(S["ssm_in"], 16)
            for q, src in enumerate(("ssm_c_re", "ssm_c_im")):
                v = a[src].rearrange("l (k g) c p -> (g c) (l k) p", k=4)
                for half in range(2):
                    eng.dma_start(cnat[:, q, :, 64 * half:64 * half + 64], v).then_inc(S["ssm_in"], 16)
            for q, src in enumerate(("state_ssm_re", "state_ssm_im")):
                eng.dma_start(h0nat[:, q, :], a[src].rearrange("l b (j g) p -> (l b j) (g p)", g=2)).then_inc(S["ssm_in"], 16)
            load_slab(2)
            rest = (WIN - DT) * KV * HD // 16
            for src, dst in (("cache_k_win", "nk_win_s"), ("cache_v_win", "nv_win_s")):
                dims = [[rest, 16], [WIN * KV * HD, DB], [1, rest]]
                eng.dma_start(bass.AP(a[dst].tensor, 0, dims),
                              bass.AP(a[src].tensor, DT * KV * HD, dims)).then_inc(S["win_out"], 16)
            eng.wait_ge(S["copied_x"], 10)
            eng.dma_start(h_spill, arena[:, 5120:5120 + KC * TT]).then_inc(S["h_out"], 16)
            eng.wait_ge(S["line_copied"], 4)
            eng.dma_start(bass.AP(bias_line.tensor, 0, [[SHIFTS * LPITCH, HEADS], [LPITCH + 1, SHIFTS], [1, LINE]]),
                          wide(line, SHIFTS, 1)).then_inc(S["line_out"], 16)
            for n in range(3, 8):
                load_slab(n)
            eng.dma_start(w1, a["cmp_w1_k"].rearrange("l (k p) n -> p (l k) n", p=P)).then_inc(S["w1_in"], 16)
            for q, src in enumerate(("cmp_w2_k", "cmp_w2_v")):
                eng.dma_start(w2[:, q, :, :], a[src].rearrange("l (k p) n -> p (l k) n", p=P)).then_inc(S["w2_in"], 16)
            eng.wait_ge(S["gates_copied"], TILES + 1)
            eng.dma_start(gate_rows, gates[0:NS, TILES, :]).then_inc(S["gate_out"], 16)
            eng.wait_ge(S["gate_out"], 16)
            for b in range(DB):
                eng.dma_start(gates_s[32 * (b % 4):32 * (b % 4) + 32, b // 4, :],
                              bass.AP(gate_rows.tensor, DT * 24 * b, [[3, HEADS], [24, DT], [1, 3]])).then_inc(S["gate_in"], 16)
            eng.wait_ge(S["tokst_copied"], 5)
            eng.wait_ge(S["vtok_copied"], 5)
            stores = [("nk_cmp", 0, None), ("nv_cmp", 1, None), ("nk_sel", 2, None), ("nk_win", 3, None),
                      ("nv_sel", None, 0), ("nv_win", None, 1)]
            for n, q, v in stores:
                src = tokst[:, 0:4, q * P:(q + 1) * P] if v is None else vtok[:, 0:4, v, :]
                eng.dma_start(a[n + "_p"].rearrange("l b (t p) k d -> p (l b t) (k d)", p=P), src).then_inc(S["kv_out"], 16)
                src = tokst[0:NS, 4, q * P:(q + 1) * P] if v is None else vtok[0:NS, 4, v, :]
                if n.endswith("win"):
                    o = a[n + "_s"]
                    eng.dma_start(bass.AP(o.tensor, (WIN - DT) * P, [[WIN * P, DB], [P, DT], [1, P]]), src).then_inc(S["kv_out"], 16)
                else:
                    eng.dma_start(a[n + "_s"].rearrange("l b t k d -> (l b t) (k d)"), src).then_inc(S["kv_out"], 16)
            load_slab(8)
            eng.wait_ge(S["hid_done"], 6)
            eng.dma_start(w1, a["cmp_w1_v"].rearrange("l (k p) n -> p (l k) n", p=P)).then_inc(S["w1_in"], 16)
            eng.wait_ge(S["fin_copied"], 4)
            for q, n in enumerate(("ns_re", "ns_im")):
                eng.dma_start(a[n + "_p"].rearrange("l b (j g) p -> (l b j) (g p)", g=2), hout[0:16, q, :]).then_inc(S["fin_out"], 16)
                eng.dma_start(a[n + "_s"].rearrange("l b (j g) p -> (l b j) (g p)", g=2), hout[:, 2 + q, :]).then_inc(S["fin_out"], 16)
            load_slab(9)
            load_slab(10)
            eng.wait_ge(S["c2_done"], 6)
            for tile in range(2):
                if tile:
                    eng.wait_ge(S["so_done"], 4)
                for n, dst, s in (("cache_k_win", kwin, "kwin_in"), ("cache_v_win", vwin, "vwin_in")):
                    eng.dma_start(dst, a[n][0, 4 * tile:4 * tile + 4].rearrange("b (p j) k d -> p b (j k d)", p=P)).then_inc(S[s], 16)
                if tile == 0:
                    eng.wait_ge(S["y_done"], 16)
                    eng.wait_ge(S["fin_turned"], 4)
                    eng.wait_ge(S["line_out"], 16)
                    eng.wait_ge(S["fin_out"], 64)
                    for p0 in range(0, P, SHIFTS):
                        for k in range(KV):
                            eng.dma_start(TZ[p0:p0 + SHIFTS, k:HEADS:KV, :],
                                          bass.AP(bias_line.tensor, k * G * SHIFTS * LPITCH + TBASE - p0,
                                                  [[LPITCH, SHIFTS], [SHIFTS * LPITCH, G], [1, TW]])).then_inc(S["toep_in"], 16)
                    for b in range(4):
                        eng.dma_start(biasS[32 * b:32 * b + 32, 0:PAST + DT],
                                      bass.AP(bias_line.tensor, DT - 1, [[SHIFTS * LPITCH, HEADS], [LPITCH, DT], [1, PAST + DT]])).then_inc(S["biasS_in"], 16)
            eng.wait_ge(S["so_taken"], 4)
            eng.wait_ge(S["h_out"], 16)
            eng.dma_start(arena[:, 0:KC * TT], h_spill).then_inc(S["h_in"], 16)
            eng.dma_start(ptok[:, 0:4, :], a["p_prompt"].rearrange("l b (t p) d -> p (l b t) d", p=P)).then_inc(S["p_in"], 16)
            eng.dma_start(ptok[0:NS, 4, :], a["p_sample"].rearrange("l b t d -> (l b t) d")).then_inc(S["p_in"], 16)
            eng.dma_start(wple.rearrange("p (k n) -> p k n", k=2), a["w_ple"].rearrange("l (k p) n -> p (l k) n", p=P)).then_inc(S["wple_in"], 16)
            for n in range(11, len(slabs)):
                load_slab(n)
            for t in range(5):
                eng.wait_ge(S["y_copied_v"], t + 1)
                eng.wait_ge(S["y_copied_a"], t + 1)
                if t < 4:
                    eng.dma_start(a["y_prompt"][0, t * P:(t + 1) * P, :], ytok[:, t % 2, :]).then_inc(y_stored[t % 2], 16)
                else:
                    eng.dma_start(a["y_sample"].rearrange("b t d -> (b t) d"), ytok[0:NS, 0, :]).then_inc(y_stored[0], 16)
            eng.wait_ge(y_stored[0], 16 * 3)
            eng.wait_ge(y_stored[1], 16 * 2)
            eng.wait_ge(S["win_out"], 32)
            eng.wait_ge(S["kv_out"], 16 * 12)
            eng.wait_ge(S["fin_out"], 16 * 4)

        @block.gpsimd
        def _(eng):
            steps = [0]

            def link(ins):
                steps[0] += 1
                ins.then_inc(S["g_step"], 1)
                eng.wait_ge(S["g_step"], steps[0])

            pools = {n: a[n] for n in ("cache_k_cmp", "cache_v_cmp", "cache_k_sel", "cache_v_sel")}

            def gather_cmp(n):
                kv, tile = n // 4, n % 4
                if n:
                    eng.wait_ge(S["raw_copied"], n)
                src = pools["cache_k_cmp" if kv == 0 else "cache_v_cmp"].rearrange("l n (c r) k d -> (l n c) (r k d)", r=CH)
                eng.indirect_dma_start(out=raw, out_offset=None, in_=src,
                                       in_offset=bass.IndirectOffsetOnAxis(ap=idx[:, 8 + tile:9 + tile].bitcast(U32), axis=0)).then_inc(S["raw_in"], 16)

            def gather_sel(which, b):
                src = pools["cache_k_sel" if which == 0 else "cache_v_sel"].rearrange("l n (c r) k d -> (l n c) (r k d)", r=8)
                dst = ksel[:, b % 2, :] if which == 0 else vsel[:, b % 4, :]
                eng.indirect_dma_start(out=dst, out_offset=None, in_=src,
                                       in_offset=bass.IndirectOffsetOnAxis(ap=idx[:, b:b + 1].bitcast(U32), axis=0)).then_inc(ksel_in[b % 2] if which == 0 else vsel_in[b % 4], 16)

            eng.wait_ge(S["idx_ready"], 2)
            eng.wait_ge(S["line_out"], 16)
            eng.wait_ge(S["vec_turned"], 1)
            gather_cmp(0)
            eng.wait_ge(S["theta_ready"], 1)
            eng.wait_ge(S["kv_out"], 16 * 12)
            eng.wait_ge(S["h_out"], 16)
            raws = 1
            for j in range(16):
                if j:
                    eng.wait_ge(S["E_ready"], j)
                if j >= 2:
                    eng.wait_ge(S["E_used"], j - 1)
                J = lambda c: wide(Jt[:, c, j, :], 16)
                Sx = lambda c: wide(St[:, c, j, :], 32, 1)
                t0 = ptmp[:, 0, :].rearrange("p (a b) -> p a b", b=16)
                t1 = ptmp[:, 1, :].rearrange("p (a b) -> p a b", b=16)
                E = lambda c: Et[:, j % 2, c, :].rearrange("p (a b) -> p a b", b=16)
                eng.tensor_tensor(t0, J(0), Sx(0), ALU.mult)
                link(eng.tensor_tensor(t1, J(1), Sx(1), ALU.mult))
                link(eng.tensor_tensor(E(0), t0, t1, ALU.subtract))
                eng.tensor_tensor(t0, J(0), Sx(1), ALU.mult)
                link(eng.tensor_tensor(t1, J(1), Sx(0), ALU.mult))
                eng.tensor_tensor(E(1), t0, t1, ALU.add).then_inc(S["E_ready"], 1)
                if j % 2 == 0 and raws < 8:
                    gather_cmp(raws)
                    raws += 1
            while raws < 8:
                gather_cmp(raws)
                raws += 1
            eng.wait_ge(S["c2_done"], 6)
            for b in range(DB):
                if b >= 2:
                    eng.wait_ge(S["tb_done"], keys_turned(b - 2))
                gather_sel(0, b)
                if b >= 4:
                    eng.wait_ge(S["so_done"], b - 3)
                gather_sel(1, b)

        def pt_copy(eng, n):
            W = P * (n // 8 + 1)
            for br in range(2):
                eng.wait_ge(S["pt_done"], 2 * n + br + 1)
                if n >= 2:
                    eng.wait_ge(S["o_done"], n - 1)
                eng.activation(PTs[:, 2 * (n % 2) + br, 0:W], bank(4 + br)[:, 0:W], ACT.Copy).then_inc(S["pt_copied"], 1)

        @block.scalar
        def _(eng):
            steps = [0]

            def link(ins):
                steps[0] += 1
                ins.then_inc(S["a_step"], 1)
                eng.wait_ge(S["a_step"], steps[0])

            def squares(n, src, gate):
                for k in range(KC):
                    gate(k)
                    eng.activation(uT[:, k, :], src[:, k, :], ACT.Square).then_inc(S["squares"], 1)

            def root(n, dst):
                eng.wait_ge(*done(("norm", n)))
                eng.activation(halves(dst), both(pair_of[("norm", n)]), ACT.Sqrt, bias=eps_t[:, :], scale=1.0 / D).then_inc(taken[pair_of[("norm", n)]], 1)

            eng.wait_ge(S["ones_set"], 2)
            squares(0, hT0, lambda k: eng.wait_ge(S["copied_x"], 10) if k == 0 else None)
            root(0, rt0)
            ldt, ar_, dt, mag = vec[:, 104:120], vec[:, 40:56], sp[:, 0, :], sp[:, 1, :]
            eng.wait_ge(S["vec_copied"], 1)
            eng.activation(dt, ldt, ACT.Exp).then_inc(S["ldt"], 1)
            eng.wait_ge(S["ldt"], 2)
            eng.activation(mag, sp[:, 2, :], ACT.Exp).then_inc(S["sin_done"], 1)
            eng.wait_ge(S["ldt"], 4)
            eng.activation(sp[:, 5, :], sp[:, 3, :], ACT.Sin).then_inc(S["sin_done"], 1)
            eng.activation(sp[:, 6, :], sp[:, 4, :], ACT.Sin).then_inc(S["sin_done"], 1)
            for m in range(14):
                name = ("z", m)
                eng.wait_ge(*done(name))
                dst = zq[:, m, :] if m < 4 else zkv[:, ZSLOT[m - 4], :] if m < 10 else zsu[:, m - 10, :]
                eng.activation(halves(dst), both(pair_of[name]), ACT.Copy).then_inc(taken[pair_of[name]], 1)
            eng.wait_ge(*done(("ng", 0)))
            eng.activation(halves(zng), pair[pair_of[("ng", 0)]][0:24, :, 0:HT], ACT.Sigmoid).then_inc(taken[pair_of[("ng", 0)]], 1)
            for t in range(5):
                n = P if t < 4 else NS
                eng.wait_ge(S["kvt_done"], 2 * t + 1)
                eng.activation(tokst[0:n, t, :], bank(2 * (t % 2))[0:n, :], ACT.Copy).then_inc(S["tokst_copied"], 1)
            eng.wait_ge(S["gate_out"], 16)
            eng.wait_ge(S["gates_turned"], 1)
            turn = hid = c2 = 0
            for kv in range(2):
                for h in range(2):
                    eng.wait_ge(S["hid_done"], hid + 1)
                    b = bank(hid % 2)
                    link(eng.activation(pb[:, 2 * kv + h:2 * kv + h + 1], b[:, 62:63], ACT.Copy))
                    eng.activation(Hq[:, h, :], b[:, 0:62], ACT.Gelu_apprx_tanh, bias=pb[:, 2 * kv + h:2 * kv + h + 1]).then_inc(S["hid_taken"], 1)
                    hid += 1
                eng.wait_ge(S["c2_done"], c2 + 1)
                if kv == 0:
                    eng.activation(kcT_p[:, 0:CB_P], bank(7)[:, 0:CB_P], ACT.Copy).then_inc(S["c2_taken"], 1)
                else:
                    for q in range(4):
                        r = slice(32 * q, 32 * q + CB_P)
                        ins = eng.activation(vc_p[r, :], bank(7)[r, 0:HD], ACT.Copy)
                    ins.then_inc(S["c2_taken"], 1)
                c2 += 1
                for bg in range(2):
                    for tt in range(2):
                        for q in range(4):
                            ckv, ph = q // 2, q % 2
                            eng.wait_ge(S["raw_turned"], turn + 1)
                            eng.activation(XT[:, 4 * ph:4 * ph + 4, ckv, tt * P:(tt + 1) * P],
                                           bank(2 + turn % 2).rearrange("p (a b) -> p a b", b=P), ACT.Copy).then_inc(S["turn_copied"], 1)
                            turn += 1
                    for h in range(2):
                        eng.wait_ge(S["hid_done"], hid + 1)
                        eng.activation(Hh[:, h, :], bank(hid % 2)[:, 0:504], ACT.Gelu_apprx_tanh,
                                       bias=pb[:, 2 * kv + h:2 * kv + h + 1]).then_inc(S["hid_taken"], 1)
                        hid += 1
                    eng.wait_ge(S["c2_done"], c2 + 1)
                    if kv == 0:
                        eng.activation(kcT_s[:, bg, :], bank(7)[:, 0:252], ACT.Copy).then_inc(S["c2_taken"], 1)
                    else:
                        eng.activation(vc_s[0:CB_S, 4 * bg:4 * bg + 4, :], bank(7)[0:CB_S, :].rearrange("p (a b) -> p a b", b=P), ACT.Copy).then_inc(S["c2_taken"], 1)
                    c2 += 1
            for c in range(4):
                eng.wait_ge(S["y_taken"], c + 1)
                eng.activation(zsu[:, c, :], zsu[:, c, :], ACT.Gelu_apprx_tanh).then_inc(S["z_ready"], 1)
            for m in range(4):
                name = ("glu", m)
                eng.wait_ge(*done(name))
                eng.activation(halves(glu_sig[:, m, :]), both(pair_of[name]), ACT.Sigmoid, bias=vec[:, 32 + m:33 + m]).then_inc(taken[pair_of[name]], 1)
            for i in range(TILES):
                eng.wait_ge(S["cmax_done"], i + 1)
                eng.activation(ce[:, :, 0:CB_P], cs[:, :, 0:CB_P], ACT.Exp, scale=0.125).then_inc(S["cexp_done"], 1)
                eng.wait_ge(S["cpt_done"], i + 1)
                eng.activation(PTc[:, i, :, :], bank(7)[:, 0:256].rearrange("p (a b) -> p a b", b=P), ACT.Copy).then_inc(S["cpt_copied"], 1)
            n = 0
            for i in range(TILES):
                W = P * (i + 1)
                for g in range(G):
                    for kv in range(KV):
                        for br in range(2):
                            q = 2 * (n % 2) + br
                            eng.wait_ge(S["s_taken"], 2 * n + br + 1)
                            if n >= 2:
                                eng.wait_ge(S["pt_done"], 2 * (n - 2) + br + 1)
                            eng.activation(Psb[:, q, 0:W], Ssb[:, q, 0:W], ACT.Exp, bias=small[:, q:q + 1], scale=-1.0,
                                           accum_out=small[:, 4 + q:5 + q]).then_inc(S["exp_done"], 1)
                        if n:
                            pt_copy(eng, n - 1)
                        n += 1
            pt_copy(eng, n - 1)
            tb = 0

            def tb_copy(dst, src):
                nonlocal tb
                eng.wait_ge(S["tb_done"], tb + 1)
                ins = eng.activation(dst, src(bank(4 + tb % 2)), ACT.Copy)
                ins.then_inc(S["tb_copied"], 1)
                tb += 1

            for tile in range(2):
                eng.wait_ge(S["cmin_done"], tile + 1)
                eng.activation(cc[:, 1, 0:CB_S], cc[:, 0, 0:CB_S], ACT.Exp, bias=small[:, 16:17], scale=-1.0, accum_out=small[:, 17:18]).then_inc(S["cexps"], 1)
                by4 = lambda x: x.rearrange("p (a b) -> p a b", b=P)
                for b in range(4 * tile, 4 * tile + 4):
                    for j0 in (0, 4):
                        tb_copy(at(KT[:, b % 2, :], j0, [[1, 4], [8, P]]), by4)
                    tb_copy(at(KTw[:, b % 2, :], 0, [[1, 4], [4, P]]), by4)
                eng.wait_ge(S["ss_taken"], 2 * tile + 1)
                eng.activation(PS_, SS, ACT.Exp, bias=small[:, 18:19], scale=-1.0, accum_out=small[:, 20:21]).then_inc(S["sexp"], 1)
                eng.wait_ge(S["ss_taken"], 2 * tile + 2)
                eng.activation(PW, SW, ACT.Exp, bias=small[:, 19:20], scale=-1.0, accum_out=small[:, 21:22]).then_inc(S["sexp"], 1)
                tb_copy(PTS[:, 0:4, :], by4)
                tb_copy(PTS[:, 4:8, :], by4)
                tb_copy(PTS[:, 9:13, :], by4)
                tb_copy(at(PTS[0:NS, 8, :], 0, [[5 * P, 2], [1, P]]), lambda x: x[0:NS, 0:256].rearrange("p (a b) -> p a b", b=P))
            for c in range(KC):
                for q, nm in enumerate(("mg0", "mg1")):
                    name = (nm, c)
                    eng.wait_ge(*done(name))
                    if c >= 2:
                        eng.wait_ge(S["mixed"], c - 1)
                    eng.activation(halves(sig[:, 2 * (c % 2) + q, :]), both(pair_of[name]), ACT.Sigmoid).then_inc(taken[pair_of[name]], 1)
            squares(1, hT, lambda k: eng.wait_ge(*out_of(("wo", k))))
            root(1, rt)
            for c in range(FC):
                name = ("gate", c)
                eng.wait_ge(*done(name))
                if c >= 2:
                    eng.wait_ge(*out_of(("up", c - 2)))
                eng.activation(halves(sil[:, c % 2, :]), both(pair_of[name]), ACT.Silu).then_inc(taken[pair_of[name]], 1)
            squares(2, hT, lambda k: eng.wait_ge(*out_of(("down", k))))
            root(2, rt)
            for c in range(KC):
                name = ("pg", c)
                eng.wait_ge(*done(name))
                if c >= 2:
                    eng.wait_ge(S["h_new"], c - 1)
                eng.activation(halves(sig[:, c % 2, :]), both(pair_of[name]), ACT.Sigmoid).then_inc(taken[pair_of[name]], 1)
            eng.wait_ge(*done(("pg", KC - 1)))
            squares(3, hT, lambda k: eng.wait_ge(S["h_new"], k + 1))
            root(3, rt)
            for t in range(5):
                n = P if t < 4 else NS
                eng.wait_ge(S["y_turned"], 2 * t + 2)
                if t >= 2:
                    eng.wait_ge(y_stored[t % 2], 16 * (t // 2))
                eng.activation(ytok[0:n, t % 2, 512:1024], bank(2 * (t % 2) + 1)[0:n, :], ACT.Copy).then_inc(S["y_copied_a"], 1)

        @block.vector
        def _(eng):
            steps = [0]

            def link(ins):
                steps[0] += 1
                ins.then_inc(S["v_step"], 1)
                eng.wait_ge(S["v_step"], steps[0])

            def tt(o, x, y, op):
                return eng.tensor_tensor(o, x, y, op)

            def normalise(n, src, col, rt_, rs_):
                eng.wait_ge(*out_of(("norm", n)))
                link(eng.reciprocal(rs_, rt_))
                for k in range(KC):
                    eng.scalar_tensor_tensor(uT[:, k, :], src[:, k, :], vec[:, col + k:col + k + 1], rs_, ALU.mult, ALU.mult).then_inc(S["normed"], 1)

            def xp_fill(kv):
                if kv:
                    eng.wait_ge(S["hid_done"], 2)
                for par in range(2):
                    for k in range(KV):
                        src = zkv[64 * k:64 * k + 64, ZSLOT[kv], 0:T].rearrange("p (c q r) -> p q c r", q=8, r=2)[:, :, :, par]
                        for half in range(2):
                            eng.tensor_copy(XP[64 * par:64 * par + 64, 8 * half:8 * half + 8, CB_P * k:CB_P * (k + 1)],
                                            src[:, :, half:half + CB_P])
                eng.tensor_copy(XP[:, :, 62:63], vec[:, 72 + 16 * kv:88 + 16 * kv].rearrange("p (a b) -> p a b", b=1)).then_inc(S["xp_ready"], 1)

            def raw_copy(n):
                eng.wait_ge(S["raw_in"], 16 * (n + 1))
                if n:
                    eng.wait_ge(S["raw_turned"], 4 * n)
                for par in range(2):
                    ins = eng.tensor_copy(raw2.rearrange("p (q k r d) -> p q k r d", k=KV, r=2, d=HD)[:, :, :, par, :],
                                          raw.rearrange("p (q r k d) -> p q r k d", r=2, k=KV, d=HD)[:, :, par, :, :])
                ins.then_inc(S["raw_copied"], 1)

            def y_out(c):
                eng.wait_ge(S["y_done"], 4 * c + 4)
                eng.scalar_tensor_tensor(zsu[:, c, 0:T], zsu[:, c, 0:T], vec[:, 36 + c:37 + c], bank(6), ALU.mult, ALU.add).then_inc(S["y_taken"], 1)

            def diag(n):
                q0, i, h = 2 * (n % 2), n // 8, n % 8
                head = (h % KV) * G + h // KV
                eng.wait_ge(S["exp_done"], 2 * n + 2)
                if n >= 2:
                    eng.wait_ge(S["pt_done"], 2 * (n - 1))
                link(eng.tensor_scalar(small[:, 8 + q0:10 + q0], small[:, 4 + q0:6 + q0], 1e-30, None, ALU.max))
                link(eng.reciprocal(small[:, 8 + q0:10 + q0], small[:, 8 + q0:10 + q0]))
                for br in range(2):
                    gc = 3 * head + 1 + br
                    eng.tensor_scalar(dg[:, q0 + br, :], ident, small[:, 8 + q0 + br:9 + q0 + br], gates[:, i, gc:gc + 1], ALU.mult, ALU.mult).then_inc(S["diag_ready"], 1)

            def take_o(i):
                eng.tensor_copy(oT[:, :, i * P:(i + 1) * P], bank(6).rearrange("p (a b) -> p a b", b=P)).then_inc(S["o_taken"], 1)

            eng.memset(ones, 1.0).then_inc(S["ones_set"], 1)
            eng.memset(eps_t[:, :], EPS).then_inc(S["ones_set"], 1)
            eng.memset(relb[NBUCKET:NBUCKET + 1, :], 1.0).then_inc(S["ones_set"], 1)
            eng.wait_ge(S["rows_in"], 48)
            for q, (src, n) in enumerate(((pages[0:8, 0:8], 16), (pages[0:4, 16:32], 8), (log_dt[:, :], SP_))):
                rows = src.ap[0][1]
                eng.tensor_copy(spread[0:rows, q, :].rearrange("p (a b) -> p a b", b=n), wide(src, n)).then_inc(S["spread_ready"], 1)
            eng.wait_ge(S["vec_turned"], 1)
            eng.tensor_copy(vec[:, 0:104], bank(2)[:, 0:104])
            eng.wait_ge(S["spread_turned"], 1)
            eng.tensor_copy(vec[:, 104:120], bank(3)[:, 32:48]).then_inc(S["vec_copied"], 1)
            for q in range(10):
                t, kk = q // 2, q % 2
                n = P if t < 4 else NS
                eng.wait_ge(S["turned_x"], q + 1)
                eng.tensor_copy(hT0[:, 4 * kk:4 * kk + 4, t * P:t * P + n],
                                bank(q % 2).rearrange("p (a b) -> p a b", b=P)[:, :, 0:n]).then_inc(S["copied_x"], 1)
            for q in range(4):
                eng.wait_ge(S["line_done"], q + 1)
                n = LINE // 4
                eng.tensor_copy(line[:, q * n:(q + 1) * n], bank(4 + q)[0:HEADS, 0:n]).then_inc(S["line_copied"], 1)
            eng.tensor_scalar(idx[:, 0:8], bank(3)[:, 0:8], 16.0, kc_[:, K_MOD:K_MOD + 1], ALU.mult, ALU.add).then_inc(S["idx_ready"], 1)
            eng.tensor_scalar(idx[:, 8:12], bank(3)[:, 16:20], 8.0, kc_[:, K_MOD + 1:K_MOD + 2], ALU.mult, ALU.add).then_inc(S["idx_ready"], 1)
            normalise(0, hT0, 0, rt0, rs0)
            v = lambda q: sp[:, q, :]
            are, aim = vec[:, 40:56], vec[:, 56:72]
            DTc, MAG, AD, TH, TH2, SN, CS, ABR, ABI, FR, FI, T0, T1, T2, T3 = range(15)
            eng.wait_ge(S["ldt"], 1)
            tt(v(AD), are, v(DTc), ALU.mult).then_inc(S["ldt"], 1)
            link(tt(v(T0), aim, v(DTc), ALU.mult))
            for q, shift in ((TH, 0.0), (TH2, math.pi / 2)):
                link(eng.tensor_scalar(v(T1), v(T0), shift, None, ALU.add))
                link(eng.tensor_scalar(v(T2), v(T1), 1.0 / TWO_PI, MAGIC, ALU.mult, ALU.add))
                link(eng.tensor_scalar(v(T2), v(T2), -MAGIC, None, ALU.add))
                link(eng.scalar_tensor_tensor(v(T3), v(T2), -TP_HI, v(T1), ALU.mult, ALU.add))
                link(eng.scalar_tensor_tensor(v(T3), v(T2), -TP_LO, v(T3), ALU.mult, ALU.add))
                eng.tensor_scalar(v(q), v(T3), math.pi * (1 - 1e-7), -math.pi * (1 - 1e-7), ALU.min, ALU.max).then_inc(S["ldt"], 1)
            eng.wait_ge(S["sin_done"], 3)
            tt(v(ABR), v(MAG), v(CS), ALU.mult)
            tt(v(ABI), v(MAG), v(SN), ALU.mult)
            tt(v(T0), are, are, ALU.mult)
            link(tt(v(T1), aim, aim, ALU.mult))
            link(tt(v(T0), v(T0), v(T1), ALU.add))
            link(eng.reciprocal(v(T1), v(T0)))
            link(eng.tensor_scalar(v(T0), v(ABR), -1.0, None, ALU.add))
            tt(v(T2), v(T0), are, ALU.mult)
            link(tt(v(T3), v(ABI), aim, ALU.mult))
            link(tt(v(T2), v(T2), v(T3), ALU.add))
            link(tt(v(FR), v(T2), v(T1), ALU.mult))
            tt(v(T2), v(ABI), are, ALU.mult)
            link(tt(v(T3), v(T0), aim, ALU.mult))
            link(tt(v(T2), v(T2), v(T3), ALU.subtract))
            link(tt(v(FI), v(T2), v(T1), ALU.mult))
            eng.wait_ge(S["ssm_in"], 16 * 8)
            eng.memset(bdr, 0.0)
            eng.memset(bdi, 0.0)
            fr, fi = wide(v(FR), 16), wide(v(FI), 16)
            link(tt(bbr, br_, fr, ALU.mult))
            link(tt(bt_, bi_, fi, ALU.mult))
            link(tt(bbr, bbr, bt_, ALU.subtract))
            link(tt(bbi, bi_, fr, ALU.mult))
            link(tt(bt_, br_, fi, ALU.mult))
            link(tt(bbi, bbi, bt_, ALU.add))
            for src, dst in ((bbr, bdr), (bbi, bdi)):
                for half in range(2):
                    r = slice(64 * half, 64 * half + 64)
                    eng.tensor_copy(dst[r, :, 16 * half:16 * half + 16], src[r, :, :]).then_inc(S["bd_ready"], 1)
            eng.wait_ge(S["turned_x"], 10)
            pw = [sp[:, 16 + 2 * q:18 + 2 * q, :] for q in range(6)]

            def cmul(o, x, y, n):
                t = [tmp[:, q, :, 0:n] for q in range(4)]
                link(tt(t[0], x[0], y[0], ALU.mult))
                tt(t[1], x[1], y[1], ALU.mult)
                tt(t[2], x[0], y[1], ALU.mult)
                link(tt(t[3], x[1], y[0], ALU.mult))
                tt(o[0], t[0], t[1], ALU.subtract)
                link(tt(o[1], t[2], t[3], ALU.add))

            col = lambda q: [sp[:, 16 + 2 * q + c, :] for c in range(2)]
            flat = lambda c: at(c, 0, [list(c.ap[-1]), [1, 1]])
            eng.tensor_copy(col(0)[0], v(CS))
            link(eng.tensor_copy(col(0)[1], v(SN)))
            cur = 0
            for table, top in ((St, 16), (Jt, 32)):
                eng.memset(table[:, 0, :, 0:1], 1.0)
                link(eng.memset(table[:, 1, :, 0:1], 0.0))
                n = 1
                while n < top:
                    p_ = [wide(c, n) for c in col(cur)]
                    cmul([table[:, c, :, n:2 * n] for c in range(2)], [table[:, c, :, 0:n] for c in range(2)], p_, n)
                    if (table is St) or n * 2 < top:
                        x = [flat(c) for c in col(cur)]
                        cmul([flat(c) for c in col(1 - cur)], x, x, 1)
                        cur = 1 - cur
                    n *= 2
            link(eng.memset(Hs[:, :, :, :].rearrange("p a b c -> p (a b c)"), 0.0))
            eng.memset(CT[:, :, :, :].rearrange("p a b c -> p (a b c)"), 0.0).then_inc(S["theta_ready"], 1)
            for q in range(2):
                eng.wait_ge(S["bd_turned"], q + 1)
                eng.tensor_copy(BT[:, q, :, :], bank(4 + q).rearrange("p (a b) -> p a b", b=P)).then_inc(S["bd_copied"], 1)
            eng.wait_ge(S["theta_ready"], 1)
            for q in range(2):
                eng.wait_ge(S["c_turned"], q + 1)
                for half in range(2):
                    r = slice(64 * half, 64 * half + 64)
                    src = bank(6 + q)[r, :].rearrange("p (j g c) -> p j g c", g=2, c=16)[:, :, half, :]
                    eng.tensor_scalar(CT[r, q, :, 16 * half:16 * half + 16], src, -1.0 if q else 1.0, None, ALU.mult).then_inc(S["c_copied"], 1)
            eng.wait_ge(S["h0_turned"], 1)
            eng.tensor_copy(h0T[:, :, :], bank(4)[:, 0:256].rearrange("p (a b) -> p a b", b=P)).then_inc(S["h0_copied"], 1)
            for t in range(5):
                n = P if t < 4 else NS
                eng.wait_ge(S["kvt_done"], 2 * t + 2)
                eng.tensor_copy(vtok[0:n, t, :, :], bank(2 * (t % 2) + 1)[0:n, 0:256].rearrange("p (a b) -> p a b", b=P)).then_inc(S["vtok_copied"], 1)
            eng.wait_ge(S["gates_turned"], 1)
            for t in range(TILES + 1):
                n = P if t < TILES else NS
                eng.tensor_copy(gates[0:n, t, :], bank(5)[0:n, 32 * t:32 * t + 24]).then_inc(S["gates_copied"], 1)
            eng.wait_ge(S["h_out"], 16)
            xp_fill(0)
            raw_copy(0)
            eng.wait_ge(S["xs_done"], 4)
            eng.wait_ge(S["h0_copied"], 1)
            abr, abi = wide(v(ABR), DB), wide(v(ABI), DB)
            rx = [at(rot, q * T, [[8, 16], [1, 8]]) for q in range(4)]
            for t in range(DT):
                if t == 0:
                    hr, hi = [h0T[:, c, :].rearrange("p (b j) -> p j b", j=16) for c in range(2)]
                else:
                    hr, hi = [Hs[:, c, :, :].rearrange("p j (b t) -> p j b t", t=DT)[:, :, :, t - 1] for c in range(2)]
                xr, xi = [bank(4 + c).rearrange("p (j b t) -> p j b t", b=DB, t=DT)[:, :, :, t] for c in range(2)]
                orr, oii = [Hs[:, c, :, :].rearrange("p j (b t) -> p j b t", t=DT)[:, :, :, t] for c in range(2)]
                tt(rx[0], hr, abr, ALU.mult)
                tt(rx[1], hi, abi, ALU.mult)
                tt(rx[2], hi, abr, ALU.mult)
                link(tt(rx[3], hr, abi, ALU.mult))
                tt(rx[0], rx[0], rx[1], ALU.subtract)
                link(tt(rx[2], rx[2], rx[3], ALU.add))
                tt(orr, rx[0], xr, ALU.add)
                ins = tt(oii, rx[2], xi, ALU.add)
                if t < DT - 1:
                    link(ins)
                else:
                    ins.then_inc(S["samples_done"], 1)
            eng.wait_ge(S["samples_done"], 1)
            for c in range(2):
                eng.tensor_copy(hfin_s[:, c, :].rearrange("p (b j) -> p b j", j=16),
                                Hs[:, c, :, :].rearrange("p j (b t) -> p b j t", t=DT)[:, :, :, DT - 1]).then_inc(S["fin_ready"], 1)
            eng.wait_ge(S["ys_done"], 1)
            for c in range(4):
                eng.scalar_tensor_tensor(zsu[:, c, T:TT], zsu[:, c, T:TT], vec[:, 36 + c:37 + c], bank(7)[:, c * NS:(c + 1) * NS], ALU.mult, ALU.add).then_inc(S["ys_taken"], 1)
            for j in range(16):
                e = [Et[:, j % 2, c, :] for c in range(2)]
                R = [rot[:, q, :] for q in range(6)]
                eng.wait_ge(S["E_ready"], j + 1)
                eng.wait_ge(S["x_done"], j + 1)
                xr, xi = bank(4), bank(5)
                tt(R[0], xr, e[0], ALU.mult)
                tt(R[1], xi, e[1], ALU.mult)
                tt(R[2], xi, e[0], ALU.mult)
                ins = tt(R[3], xr, e[1], ALU.mult)
                ins.then_inc(S["x_taken"], 1)
                eng.wait_ge(S["x_taken"], j + 1)
                tt(R[0], R[0], R[1], ALU.add)
                link(tt(R[2], R[2], R[3], ALU.subtract))
                decay = at(v(MAG), j, [[0, T]])
                eng.tensor_tensor_scan(R[1], decay, R[0], 0.0, ALU.mult, ALU.add)
                link(eng.tensor_tensor_scan(R[3], decay, R[2], 0.0, ALU.mult, ALU.add))
                tt(R[0], R[1], e[0], ALU.mult)
                tt(R[2], R[3], e[1], ALU.mult)
                tt(R[4], R[1], e[1], ALU.mult)
                ins = tt(R[5], R[3], e[0], ALU.mult)
                ins.then_inc(S["E_used"], 1)
                eng.wait_ge(S["E_used"], j + 1)
                if j >= 2:
                    eng.wait_ge(S["y_done"], j - 1)
                tt(Hp[:, j % 2, 0, :], R[0], R[2], ALU.subtract)
                tt(Hp[:, j % 2, 1, :], R[4], R[5], ALU.add).then_inc(S["h_ready"], 1)
                eng.wait_ge(S["h_ready"], j + 1)
                eng.tensor_copy(hfin[:, 0, j:j + 1], Hp[:, j % 2, 0, T - 1:T])
                ins = eng.tensor_copy(hfin[:, 1, j:j + 1], Hp[:, j % 2, 1, T - 1:T])
                if j == 15:
                    ins.then_inc(S["fin_ready"], 1)
                if j % 4 == 0 and j:
                    y_out(j // 4 - 1)
                if j == 0:
                    raw_copy(1)
                if j % 4 == 1 and j < 13:
                    raw_copy((j + 3) // 2)
                if j % 4 == 3 and j < 15:
                    raw_copy((j + 3) // 2)
                if j == 3:
                    xp_fill(1)
            y_out(3)
            eng.wait_ge(S["fin_turned"], 4)
            for q in range(4):
                n = 16 if q < 2 else P
                eng.tensor_copy(hout[0:n, q, :], bank(6)[0:n, q * P:(q + 1) * P]).then_inc(S["fin_copied"], 1)
            eng.wait_ge(*done(("glu", 3)))
            for m in range(4):
                eng.wait_ge(*out_of(("glu", m)))
                eng.tensor_tensor(zsu[:, m, :], zsu[:, m, :], glu_sig[:, m, :], ALU.mult).then_inc(S["glu_ready"], 1)
            eng.memset(ce[:, :, CB_P:32], 0.0).then_inc(S["fix_ready"], 1)
            eng.wait_ge(S["toep_in"], 16 * KV * P // SHIFTS)
            mx, sm = small[:, 24:32], small[:, 32:40]
            for i in range(TILES):
                eng.wait_ge(S["cs_done"], i + 1)
                c0 = 3 * P - P * i + 2 * CH - 1
                link(tt(cs[:, :, 0:CB_P], bank(7)[:, 0:248].rearrange("p (a b) -> p a b", b=CB_P), TZ[:, :, c0:c0 + CH * (CB_P - 1) + 1:CH], ALU.add))
                link(eng.tensor_reduce(mx, cs[:, :, 0:CB_P], AX.X, ALU.max))
                link(eng.tensor_scalar(mx, mx, 0.1 * MASK, None, ALU.max))
                tt(cs[:, :, 0:CB_P], cs[:, :, 0:CB_P], wide(mx, CB_P), ALU.subtract).then_inc(S["cmax_done"], 1)
                eng.wait_ge(S["cexp_done"], i + 1)
                link(eng.tensor_reduce(sm, ce[:, :, 0:CB_P], AX.X, ALU.add))
                link(eng.tensor_scalar(sm, sm, 1e-30, None, ALU.max))
                link(eng.reciprocal(sm, sm))
                gt = gates[:, i, :].rearrange("p (k g r) -> p g k r", k=KV, r=3)[:, :, :, 0]
                link(tt(sm.rearrange("p (g k) -> p g k", k=KV), sm.rearrange("p (g k) -> p g k", k=KV), gt, ALU.mult))
                tt(ce[:, :, 0:CB_P], ce[:, :, 0:CB_P], wide(sm, CB_P), ALU.mult).then_inc(S["cnorm_done"], 1)
            n = 0
            for i in range(TILES):
                W = P * (i + 1)
                for g in range(G):
                    for kv in range(KV):
                        for br in range(2):
                            q = 2 * (n % 2) + br
                            eng.wait_ge(S["s_done"], 2 * n + br + 1)
                            if n >= 2:
                                eng.wait_ge(S["exp_done"], 2 * (n - 2) + br + 1)
                            eng.tensor_tensor_reduce(Ssb[:, q, 0:W], bank(q)[:, 0:W], TZ[:, 2 * g + kv, (3 - i) * P:T], -0.125, 3e38,
                                                     ALU.add, ALU.min, small[:, q:q + 1]).then_inc(S["s_taken"], 1)
                        if n:
                            diag(n - 1)
                        if n % 8 == 1 and n > 1:
                            eng.wait_ge(S["o_done"], n - 1)
                            take_o(i - 1)
                        n += 1
            diag(n - 1)
            eng.wait_ge(S["o_done"], 32)
            take_o(TILES - 1)
            eng.memset(Qb[:, :, :].rearrange("p a b -> p (a b)"), 0.0).then_inc(S["v_step"], 1)
            steps[0] += 1
            eng.wait_ge(S["v_step"], steps[0])
            for kv in range(KV):
                r = slice(64 * kv, 64 * kv + 64)
                eng.tensor_copy(Qb[r, :, 16 * kv:16 * kv + 16].rearrange("p b (g t) -> p b g t", t=DT),
                                zq[r, :, T:TT].rearrange("p g (b t) -> p b g t", t=DT)).then_inc(S["qb_ready"], 1)
            eng.wait_ge(S["biasS_in"], 64)
            eng.wait_ge(S["gate_in"], 16 * DB)
            link(eng.memset(cc[:, 2, CB_S:64], 0.0))
            IO = kc_[:, K_IO:K_IO + NSEL - 3]
            for tile in range(2):
                eng.wait_ge(S["sc_done"], tile + 1)
                eng.tensor_tensor_reduce(cc[:, 0, 0:CB_S], bank(6)[:, 0:CB_S], biasS[:, 2 * CH - 1:2 * CH - 1 + CH * (CB_S - 1) + 1:CH], -0.125, 3e38,
                                         ALU.add, ALU.min, small[:, 16:17]).then_inc(S["cmin_done"], 1)
                eng.wait_ge(S["cexps"], tile + 1)
                link(eng.tensor_scalar(small[:, 76:77], small[:, 17:18], 1e-30, None, ALU.max))
                link(eng.reciprocal(small[:, 76:77], small[:, 76:77]))
                link(eng.tensor_scalar(cc[:, 2, 0:CB_S], cc[:, 1, 0:CB_S], small[:, 76:77], None, ALU.mult))
                link(eng.tensor_reduce(small[:, 40:54], cc[:, 2, 4:60].rearrange("p (a b) -> p a b", b=4), AX.X, ALU.add))
                tt(small[:, 40:54], small[:, 40:54], cc[:, 2, 3:56:4], ALU.add).then_inc(S["impsum_ready"], 1)
                eng.tensor_scalar(cc[:, 0, 0:CB_S], cc[:, 2, 0:CB_S], gates_s[:, tile, 0:1], None, ALU.mult).then_inc(S["pc_ready"], 1)
                eng.wait_ge(S["imp_done"], tile + 1)
                eng.tensor_copy(small[:, 40:54], bank(6)[:, 64:78]).then_inc(S["bd_seen"], 1)
                eng.wait_ge(S["bd_seen"], tile + 1)
                link(eng.tensor_reduce(small[:, 72:73], small[:, 40:54], AX.X, ALU.min))
                link(eng.scalar_tensor_tensor(small[:, 56:70], small[:, 40:54], small[:, 72:73], IO, ALU.is_equal, ALU.mult))
                link(eng.tensor_reduce(small[:, 73:74], small[:, 56:70], AX.X, ALU.max))
                link(eng.tensor_scalar(small[:, 56:70], IO, small[:, 73:74], MASK, ALU.is_equal, ALU.mult))
                tt(bd[:, SEL:PAST - SEL].rearrange("p (a b) -> p a b", b=SEL), biasS[:, SEL:PAST - SEL].rearrange("p (a b) -> p a b", b=SEL),
                   wide(small[:, 56:70], SEL), ALU.add)
                eng.tensor_copy(bd[:, 0:SEL], biasS[:, 0:SEL])
                eng.tensor_copy(bd[:, PAST - SEL:PAST], biasS[:, PAST - SEL:PAST])
                own = kc_[:, K_SM + NS * tile:K_SM + NS * tile + NS].rearrange("p (b t) -> p b t", t=DT)
                tt(bd[:, PAST:PAST + NS].rearrange("p (b t) -> p b t", t=DT), wide(biasS[:, PAST:PAST + DT], DB, 1), own, ALU.add)
                tt(bw[:, WIN:WIN + NS].rearrange("p (b t) -> p b t", t=DT), wide(biasS[:, PAST:PAST + DT], DB, 1), own, ALU.add)
                eng.tensor_copy(bw[:, DT:WIN], biasS[:, PAST - WIN + DT:PAST])
                link(tt(bw[:, 0:DT], biasS[:, PAST - WIN:PAST - WIN + DT], kc_[:, K_WM:K_WM + DT], ALU.add))
                eng.wait_ge(S["pc_done"], tile + 1)
                eng.tensor_copy(PTS[0:CB_S, 14, :], bank(6)[0:CB_S, P:2 * P]).then_inc(S["pc_copied"], 1)
                eng.wait_ge(S["ss_done"], 4 * tile + 4)
                sel = pair[0][:, :, :].rearrange("p a b -> p (a b)")
                link(eng.tensor_tensor_reduce(SS[:, 0:PAST], sel, bd[:, 0:PAST], -0.125, 3e38, ALU.add, ALU.min, small[:, 77:78]))
                eng.tensor_tensor_reduce(SS[:, PAST:PAST + NS], bank(3)[:, 0:NS], bd[:, PAST:PAST + NS], -0.125, small[:, 77:78],
                                         ALU.add, ALU.min, small[:, 18:19]).then_inc(S["ss_taken"], 1)
                link(eng.tensor_tensor_reduce(SW[:, 0:WIN], bank(2), bw[:, 0:WIN], -0.125, 3e38, ALU.add, ALU.min, small[:, 78:79]))
                eng.tensor_tensor_reduce(SW[:, WIN:WIN + NS], bank(3)[:, NS:2 * NS], bw[:, WIN:WIN + NS], -0.125, small[:, 78:79],
                                         ALU.add, ALU.min, small[:, 19:20]).then_inc(S["ss_taken"], 1)
                eng.wait_ge(S["sexp"], 2 * tile + 2)
                link(eng.tensor_scalar(small[:, 74:76], small[:, 20:22], 1e-30, None, ALU.max))
                link(eng.reciprocal(small[:, 74:76], small[:, 74:76]))
                for br in range(2):
                    eng.tensor_scalar(dgs[:, br, :], ident, small[:, 74 + br:75 + br], gates_s[:, tile, 1 + br:2 + br], ALU.mult, ALU.mult).then_inc(S["sdiag"], 1)
                eng.wait_ge(S["so_done"], 4 * tile + 4)
                for kv in range(KV):
                    r = slice(64 * kv, 64 * kv + 64)
                    src = bank(7)[r, P * tile:P * tile + P].rearrange("p (b k g t) -> p b k g t", k=KV, g=G, t=DT)[:, :, kv, :, :]
                    dst = oT[r, :, T + 16 * tile:T + 16 * tile + 16].rearrange("p g (b t) -> p b g t", t=DT)
                    eng.tensor_copy(dst, src).then_inc(S["so_taken"], 1)
            for c in range(KC):
                for q, nm in enumerate(("att", "ssm")):
                    eng.wait_ge(*out_of((("mg0", "mg1")[q], c)))
                    eng.wait_ge(*done((nm, c)))
                    eng.tensor_tensor(halves(sig[:, 2 * (c % 2) + q, :]), halves(sig[:, 2 * (c % 2) + q, :]), both(pair_of[(nm, c)]), ALU.mult).then_inc(taken[pair_of[(nm, c)]], 1)
                eng.wait_ge(*out_of(("ssm", c)))
                tt(mT[:, c, :], sig[:, 2 * (c % 2), :], sig[:, 2 * (c % 2) + 1, :], ALU.add).then_inc(S["mixed"], 1)
            eng.wait_ge(S["h_in"], 16)
            for c in range(KC):
                eng.wait_ge(*done(("wo", c)))
                eng.tensor_tensor(halves(hT[:, c, :]), halves(hT[:, c, :]), both(pair_of[("wo", c)]), ALU.add).then_inc(taken[pair_of[("wo", c)]], 1)
            for k in range(2):
                eng.wait_ge(*done(("pt", k)))
                eng.tensor_copy(pT[:, k, :], pair[pair_of[("pt", k)]][:, :, :].rearrange("p a b -> p (a b)")[:, 0:TT]).then_inc(taken[pair_of[("pt", k)]], 1)
            normalise(1, hT, 8, rt, rs)
            for c in range(FC):
                eng.wait_ge(*out_of(("gate", c)))
                eng.wait_ge(*done(("up", c)))
                eng.tensor_tensor(halves(mid[:, c, :]), halves(sil[:, c % 2, :]), both(pair_of[("up", c)]), ALU.mult).then_inc(taken[pair_of[("up", c)]], 1)
            for c in range(KC):
                eng.wait_ge(*done(("down", c)))
                eng.tensor_tensor(halves(hT[:, c, :]), halves(hT[:, c, :]), both(pair_of[("down", c)]), ALU.add).then_inc(taken[pair_of[("down", c)]], 1)
            normalise(2, hT, 16, rt, rs)
            for c in range(KC):
                eng.wait_ge(*out_of(("pg", c)))
                eng.wait_ge(*done(("ple", c)))
                eng.tensor_tensor(halves(sig[:, c % 2, :]), halves(sig[:, c % 2, :]), both(pair_of[("ple", c)]), ALU.mult).then_inc(taken[pair_of[("ple", c)]], 1)
                eng.wait_ge(*out_of(("ple", c)))
                tt(hT[:, c, :], hT[:, c, :], sig[:, c % 2, :], ALU.add).then_inc(S["h_new"], 1)
            normalise(3, hT, 24, rt, rs)
            for t in range(5):
                n = P if t < 4 else NS
                eng.wait_ge(S["y_turned"], 2 * t + 1)
                if t >= 2:
                    eng.wait_ge(y_stored[t % 2], 16 * (t // 2))
                eng.tensor_copy(ytok[0:n, t % 2, 0:512], bank(2 * (t % 2))[0:n, :]).then_inc(S["y_copied_v"], 1)

        @block.tensor
        def _(eng):
            rhs_of = {"z": uT, "ng": uT, "mg0": uT, "mg1": uT, "glu": zsu, "att": oT, "ssm": zsu, "wo": mT,
                      "gate": uT, "up": uT, "down": mid, "pg": uT, "ple": pT}
            step_of = dict(groups)
            steps_p = [0]

            def link(ins):
                steps_p[0] += 1
                ins.then_inc(S["p_step"], 1)
                eng.wait_ge(S["p_step"], steps_p[0])

            def gemm(name, ready=None):
                pr, use = pair_of[name], use_of[name]
                if use > 1:
                    eng.wait_ge(taken[pr], use - 1)
                steps = step_of[name]
                src = rhs_of[name[0]]
                seen = set()
                for n, (w, off, m, k) in enumerate(steps):
                    if w is None:
                        lhsT = wple[:, off:off + m]
                    else:
                        if w not in seen:
                            eng.wait_ge(slab_landed[w % RING], landed_at[w])
                            seen.add(w)
                        lhsT = ring[:, w % RING, off:off + m]
                    if ready:
                        eng.wait_ge(*ready(k))
                    for h in range(2):
                        ins = eng.matmul(pair[pr][0:m, h, 0:HT], lhsT, src[:, k, h * HT:(h + 1) * HT], start=n == 0, stop=n == len(steps) - 1)
                ins.then_inc(sum_done[pr], 1)

            def norm(n):
                pr, use = pair_of[("norm", n)], use_of[("norm", n)]
                if use > 1:
                    eng.wait_ge(taken[pr], use - 1)
                for k in range(KC):
                    eng.wait_ge(S["squares"], KC * n + k + 1)
                    for h in range(2):
                        ins = eng.matmul(pair[pr][:, h, 0:HT], ones, uT[:, k, h * HT:(h + 1) * HT], start=k == 0, stop=k == KC - 1)
                ins.then_inc(sum_done[pr], 1)

            normed = lambda n: lambda k: (S["normed"], KC * n + k + 1)

            def ssm_maps():
                eng.wait_ge(S["bd_ready"], 4)
                for q, src in enumerate((bdr, bdi)):
                    for k in range(4):
                        ins = eng.transpose(bank(4 + q)[:, k * P:(k + 1) * P], src[:, 4 * k:4 * k + 4, :].rearrange("p a b -> p (a b)"), ident)
                    ins.then_inc(S["bd_turned"], 1)
                eng.wait_ge(S["ssm_in"], 16 * 8)
                for q in range(2):
                    for k in range(4):
                        ins = eng.transpose(bank(6 + q)[:, k * P:(k + 1) * P], cnat[:, q, k, :], ident)
                    ins.then_inc(S["c_turned"], 1)
                eng.wait_ge(S["bd_copied"], 1)
                for q in range(2):
                    ins = eng.transpose(bank(4)[:, q * P:(q + 1) * P], h0nat[:, q, :], ident)
                ins.then_inc(S["h0_turned"], 1)

            eng.wait_ge(S["const_in"], 16)
            eng.wait_ge(S["nat_in"], 16 * 10)
            eng.transpose(bank(2)[:, 0:104], nat[0:104, :], ident[0:104, 0:104]).then_inc(S["vec_turned"], 1)
            eng.wait_ge(S["spread_ready"], 3)
            for q, rows in enumerate((8, 4, 16)):
                ins = eng.transpose(bank(3)[:, 16 * q:16 * q + rows], spread[0:rows, q, :], ident[0:rows, 0:rows])
            ins.then_inc(S["spread_turned"], 1)
            eng.wait_ge(S["x0"], 16 * 5)
            for q in range(10):
                t, kk = q // 2, q % 2
                n = P if t < 4 else NS
                if q >= 2:
                    eng.wait_ge(S["copied_x"], q - 1)
                for c in range(4):
                    k = 4 * kk + c
                    ins = eng.transpose(bank(q % 2)[:, c * P:c * P + n], xtok[0:n, t, k * P:(k + 1) * P], ident[0:n, 0:n])
                ins.then_inc(S["turned_x"], 1)
            eng.wait_ge(S["hot_in"], 32)
            eng.wait_ge(S["ones_set"], 3)
            n = LINE // 4
            for q in range(4):
                eng.matmul(bank(4 + q)[0:HEADS, 0:n], relb, hot[:, q * n:(q + 1) * n], start=True, stop=True).then_inc(S["line_done"], 1)
            eng.wait_ge(S["copied_x"], 10)
            norm(0)
            eng.wait_ge(S["vec_copied"], 1)
            for m in range(14):
                if m == 1:
                    eng.wait_ge(S["line_copied"], 4)
                gemm(("z", m), normed(0) if m == 0 else None)
            gemm(("ng", 0))
            for t in range(5):
                n = P if t < 4 else NS
                if t == 0:
                    for m in range(10, 14):
                        eng.wait_ge(*out_of(("z", m)))
                    eng.wait_ge(*out_of(("ng", 0)))
                if t >= 2:
                    eng.wait_ge(S["tokst_copied"], t - 1)
                    eng.wait_ge(S["vtok_copied"], t - 1)
                for q, slot in enumerate((0, 1, KS, KW)):
                    ins = eng.transpose(bank(2 * (t % 2))[0:n, q * P:(q + 1) * P], zkv[:, slot, t * P:t * P + n], ident)
                ins.then_inc(S["kvt_done"], 1)
                for q, slot in enumerate((2, 3)):
                    ins = eng.transpose(bank(2 * (t % 2) + 1)[0:n, q * P:(q + 1) * P], zkv[:, slot, t * P:t * P + n], ident)
                ins.then_inc(S["kvt_done"], 1)
                if t == 0:
                    ssm_maps()
            eng.wait_ge(S["bd_copied"], 2)
            for t in range(TILES):
                eng.transpose(bank(5)[:, 32 * t:32 * t + 24], zng[:, t * P:(t + 1) * P], ident[0:24, 0:24])
            ins = eng.transpose(bank(5)[0:NS, 32 * TILES:32 * TILES + 24], zng[:, T:TT], ident[0:24, 0:24])
            ins.then_inc(S["gates_turned"], 1)
            eng.wait_ge(S["h0_copied"], 1)
            eng.wait_ge(S["gates_copied"], TILES + 1)
            for rg in range(4):
                r = slice(32 * rg, 32 * rg + 32)
                for c in range(2):
                    for j in range(rg, 16, 4):
                        ins = eng.matmul(bank(4 + c)[:, j * NS:(j + 1) * NS], BT[r, c, j // 4, :], zsu[r, j // 4, T:TT], start=True, stop=True)
                ins.then_inc(S["xs_done"], 1)
                if rg < 3:
                    eng.wait_ge(S["xs_done"], rg + 1)
            eng.wait_ge(S["samples_done"], 1)
            eng.wait_ge(S["c_copied"], 4)
            for cg in range(4):
                for j in range(cg, 16, 4):
                    for c in range(2):
                        ins = eng.matmul(bank(7)[32 * cg:32 * cg + 32, NS * (j // 4):NS * (j // 4) + NS], CT[:, c, j, :], Hs[:, c, j, :], start=c == 0, stop=c == 1)
            ins.then_inc(S["ys_done"], 1)
            turn = hid = c2 = 0

            def x_in(j):
                if j:
                    eng.wait_ge(S["x_taken"], j)
                r = slice(32 * (j % 4), 32 * (j % 4) + 32)
                for c in range(2):
                    ins = eng.matmul(bank(4 + c), BT[r, c, j // 4, :], zsu[r, j // 4, 0:T], start=True, stop=True)
                ins.then_inc(S["x_done"], 1)

            def y_sum(j):
                eng.wait_ge(S["h_ready"], j + 1)
                if j >= 4 and j % 4 == 0:
                    eng.wait_ge(S["y_taken"], j // 4)
                for c in range(2):
                    ins = eng.matmul(bank(6)[32 * (j % 4):32 * (j % 4) + 32, :], CT[:, c, j, :], Hp[:, j % 2, c, :], start=c == 0, stop=c == 1)
                ins.then_inc(S["y_done"], 1)

            def turns():
                nonlocal turn
                eng.wait_ge(S["raw_copied"], turn // 4 + 1)
                for q in range(4):
                    ckv, ph = q // 2, q % 2
                    if turn >= 2:
                        eng.wait_ge(S["turn_copied"], turn - 1)
                    for c in range(4):
                        col = (4 * ph + c) * 256 + ckv * P
                        ins = eng.transpose(bank(2 + turn % 2)[:, c * P:(c + 1) * P], raw2[:, col:col + P], ident)
                    ins.then_inc(S["raw_turned"], 1)
                    turn += 1

            def hidden(h, half, batch):
                nonlocal hid
                if half == 0 and hid >= 2:
                    eng.wait_ge(S["hid_taken"], hid - 1)
                if half == 0 and h == 0:
                    eng.wait_ge(S["turn_copied"], 8 * (batch + 1))
                out = bank(hid % 2)[:, 0:504].rearrange("p (k b c) -> p k b c", k=KV, c=CB_S)
                for q in range(8):
                    rhs = XT[:, q, :, :].rearrange("p k (b c) -> p k b c", c=64)[:, :, :, half:half + CB_S]
                    ins = eng.matmul(out, w1[:, 8 * half + q, h * P:(h + 1) * P], rhs, start=half == 0 and q == 0, stop=half == 1 and q == 7)
                if half:
                    ins.then_inc(S["hid_done"], 1)
                    hid += 1

            def second(kv):
                nonlocal c2
                eng.wait_ge(S["hid_taken"], hid)
                if c2:
                    eng.wait_ge(S["c2_taken"], c2)
                if c2 % 3 == 0:
                    for quad in range(2 if kv == 0 else 4):
                        for h in range(2):
                            k = quad % 2
                            x = Hq[:, h, CB_P * k:CB_P * (k + 1)]
                            if kv == 0:
                                ins = eng.matmul(bank(7)[64 * k:64 * k + 64, 0:CB_P], w2[:, 0, h, :], x, start=h == 0, stop=h == 1)
                            else:
                                ins = eng.matmul(bank(7)[32 * quad:32 * quad + CB_P, 0:HD], x, w2[:, 1, h, :], start=h == 0, stop=h == 1)
                elif kv == 0:
                    for k in range(KV):
                        for h in range(2):
                            ins = eng.matmul(bank(7)[64 * k:64 * k + 64, 0:252], w2[:, 0, h, :], Hh[:, h, 252 * k:252 * k + 252], start=h == 0, stop=h == 1)
                else:
                    for b in range(4):
                        for k in range(KV):
                            for h in range(2):
                                x = Hh[:, h, 252 * k + CB_S * b:252 * k + CB_S * (b + 1)]
                                ins = eng.matmul(bank(7)[0:CB_S, P * b + HD * k:P * b + HD * (k + 1)], x, w2[:, 1, h, :], start=h == 0, stop=h == 1)
                ins.then_inc(S["c2_done"], 1)
                c2 += 1

            def prompt_hidden(kv):
                nonlocal hid
                eng.wait_ge(S["w1_in"], 16 * (kv + 1))
                eng.wait_ge(S["xp_ready"], kv + 1)
                for h in range(2):
                    if hid >= 2:
                        eng.wait_ge(S["hid_taken"], hid - 1)
                    for q in range(16):
                        ins = eng.matmul(bank(hid % 2)[:, 0:63], w1[:, q, h * P:(h + 1) * P], XP[:, q, 0:63], start=q == 0, stop=q == 15)
                    ins.then_inc(S["hid_done"], 1)
                    hid += 1
                eng.wait_ge(S["w2_in"], 32)
                second(kv)

            eng.wait_ge(S["ys_taken"], 4)
            eng.wait_ge(S["tokst_copied"], 5)
            eng.wait_ge(S["vtok_copied"], 5)
            for j in range(16):
                if j:
                    y_sum(j - 1)
                x_in(j)
                batch = j // 4
                if j % 4 == 0:
                    if batch % 2 == 0:
                        prompt_hidden(batch // 2)
                    turns()
                    turns()
                hidden(j // 2 % 2, j % 2, batch)
                if j % 4 == 3:
                    second(batch // 2)
            y_sum(15)
            eng.wait_ge(S["fin_ready"], 3)
            eng.wait_ge(S["y_taken"], 4)
            for q in range(2):
                eng.transpose(bank(6)[0:16, q * P:(q + 1) * P], hfin[:, q, :], ident).then_inc(S["fin_turned"], 1)
            for q in range(2):
                eng.transpose(bank(6)[:, (2 + q) * P:(3 + q) * P], hfin_s[:, q, :], ident).then_inc(S["fin_turned"], 1)
            eng.wait_ge(S["hid_taken"], 12)
            eng.wait_ge(S["fin_copied"], 4)
            eng.wait_ge(S["c2_taken"], 6)
            eng.wait_ge(S["x_taken"], 16)
            for m in range(4):
                gemm(("glu", m), (lambda k: (S["z_ready"], k + 1)) if m == 0 else None)
            for m in range(4):
                eng.wait_ge(*out_of(("glu", m)))
            for i in range(TILES):
                if i:
                    eng.wait_ge(S["cpt_copied"], i)
                for k, g in [(k, g) for k in range(KV) for g in range(G)]:
                    h = KV * g + k
                    r = slice(64 * k, 64 * k + 64)
                    if g == 0 and k:
                        link(ins)
                    ins = eng.matmul(bank(7)[:, h * CB_P:(h + 1) * CB_P], zq[r, g, i * P:(i + 1) * P], kcT_p[r, 0:CB_P], start=True, stop=True)
                ins.then_inc(S["cs_done"], 1)
                eng.wait_ge(S["cnorm_done"], i + 1)
                eng.wait_ge(S["fix_ready"], 1)
                for half in range(2):
                    ins = eng.transpose(bank(7)[:, half * P:(half + 1) * P], ce[:, 4 * half:4 * half + 4, :].rearrange("p a b -> p (a b)"), ident)
                ins.then_inc(S["cpt_done"], 1)

            def scores(n):
                i, h = n // 8, n % 8
                g, k, W = h // KV, h % KV, P * (i + 1)
                r = slice(64 * k, 64 * k + 64)
                for br in range(2):
                    if n >= 2:
                        eng.wait_ge(S["s_taken"], 2 * (n - 2) + br + 1)
                    eng.matmul(bank(2 * (n % 2) + br)[:, 0:W], zq[r, g, i * P:(i + 1) * P], zkv[r, (KS, KW)[br], 0:W], start=True, stop=True).then_inc(S["s_done"], 1)

            def turn_probs(n):
                i = n // 8
                for br in range(2):
                    q = 2 * (n % 2) + br
                    eng.wait_ge(S["diag_ready"], 2 * n + br + 1)
                    if n:
                        eng.wait_ge(S["pt_copied"], 2 * (n - 1) + br + 1)
                    for c in range(i + 1):
                        ins = eng.matmul(bank(4 + br)[:, c * P:(c + 1) * P], Psb[:, q, c * P:(c + 1) * P], dg[:, q, :], start=True, stop=True)
                    ins.then_inc(S["pt_done"], 1)

            def values(n):
                i, h = n // 8, n % 8
                g, k = h // KV, h % KV
                if n % 8 == 0 and i:
                    eng.wait_ge(S["o_taken"], i)
                out = bank(6)[64 * k:64 * k + 64, g * P:(g + 1) * P]
                quad = (g % 2) * 2 + k
                r = slice(32 * quad, 32 * quad + CB_P)
                eng.wait_ge(S["cpt_copied"], i + 1)
                if n >= 2:
                    eng.wait_ge(S["o_done"], n - 1)
                eng.matmul(out, vc_p[r, :], PTc[r, i, g // 2, :], start=True, stop=False)
                eng.wait_ge(S["pt_copied"], 2 * n + 2)
                for br in range(2):
                    for c in range(i + 1):
                        last = br == 1 and c == i
                        ins = eng.matmul(out, vtok[:, c, br, 64 * k:64 * k + 64], PTs[:, 2 * (n % 2) + br, c * P:(c + 1) * P], start=False, stop=last)
                ins.then_inc(S["o_done"], 1)

            scores(0)
            for n in range(32):
                if n + 1 < 32:
                    scores(n + 1)
                turn_probs(n)
                if n:
                    values(n - 1)
            values(31)
            tb = 0

            def tb_bank():
                if tb >= 2:
                    eng.wait_ge(S["tb_copied"], tb - 1)
                return bank(4 + tb % 2)

            eng.wait_ge(S["qb_ready"], 2)
            eng.wait_ge(S["pt_copied"], 64)
            eng.wait_ge(S["o_taken"], 4)
            for tile in range(2):
                if tile:
                    eng.wait_ge(S["pc_copied"], tile)
                for b in range(4):
                    ins = eng.matmul(bank(6)[32 * b:32 * b + 32, 0:CB_S], Qb[:, 4 * tile + b, :], kcT_s[:, tile, CB_S * b:CB_S * (b + 1)], start=True, stop=True)
                ins.then_inc(S["sc_done"], 1)
                eng.wait_ge(S["kwin_in"], 16 * (tile + 1))
                for b in range(4 * tile, 4 * tile + 4):
                    eng.wait_ge(ksel_in[b % 2], 16 * (b // 2 + 1))
                    for j0 in (0, 4):
                        bk = tb_bank()
                        for c in range(4):
                            ins = eng.transpose(bk[:, c * P:(c + 1) * P], ksel[:, b % 2, (j0 + c) * P:(j0 + c + 1) * P], ident)
                        ins.then_inc(S["tb_done"], 1)
                        tb += 1
                    bk = tb_bank()
                    for c in range(4):
                        ins = eng.transpose(bk[:, c * P:(c + 1) * P], kwin[:, b % 4, c * P:(c + 1) * P], ident)
                    ins.then_inc(S["tb_done"], 1)
                    tb += 1
                    eng.wait_ge(S["tb_copied"], tb)
                    if tile and b == 4:
                        eng.wait_ge(S["ss_taken"], 2)
                    r = slice(32 * (b % 4), 32 * (b % 4) + 32)
                    q = Qb[:, b, :]
                    eng.matmul(bank(0)[r, :], q, KT[:, b % 2, 0:512], start=True, stop=True)
                    eng.matmul(bank(1)[r, :], q, KT[:, b % 2, 512:1024], start=True, stop=True)
                    eng.matmul(bank(2)[r, :], q, KTw[:, b % 2, :], start=True, stop=True)
                    eng.matmul(bank(3)[r, 0:NS], q, zkv[:, KS, T:TT], start=True, stop=True)
                    eng.matmul(bank(3)[r, NS:2 * NS], q, zkv[:, KW, T:TT], start=True, stop=True).then_inc(S["ss_done"], 1)
                    if b % 4 == 0:
                        eng.wait_ge(S["impsum_ready"], tile + 1)
                        eng.matmul(bank(6)[:, 64:78], kc_[:, K_G:K_G + P], small[:, 40:54], start=True, stop=True).then_inc(S["imp_done"], 1)
                    if b % 4 == 1:
                        eng.wait_ge(S["pc_ready"], tile + 1)
                        eng.wait_ge(S["bd_seen"], tile + 1)
                        eng.transpose(bank(6)[0:CB_S, P:2 * P], cc[:, 0, 0:CB_S], ident).then_inc(S["pc_done"], 1)
                eng.wait_ge(S["sdiag"], 2 * tile + 2)
                for j0 in (0, 4):
                    bk = tb_bank()
                    for c in range(4):
                        ins = eng.matmul(bk[:, c * P:(c + 1) * P], PS_[:, j0 + c:j0 + c + 8 * (P - 1) + 1:8], dgs[:, 0, :], start=True, stop=True)
                    ins.then_inc(S["tb_done"], 1)
                    tb += 1
                bk = tb_bank()
                for c in range(4):
                    ins = eng.matmul(bk[:, c * P:(c + 1) * P], PW[:, c:c + 4 * (P - 1) + 1:4], dgs[:, 1, :], start=True, stop=True)
                ins.then_inc(S["tb_done"], 1)
                tb += 1
                bk = tb_bank()
                eng.matmul(bk[0:NS, 0:P], PS_[:, PAST:PAST + NS], dgs[:, 0, :], start=True, stop=True)
                eng.matmul(bk[0:NS, P:2 * P], PW[:, WIN:WIN + NS], dgs[:, 1, :], start=True, stop=True).then_inc(S["tb_done"], 1)
                tb += 1
                eng.wait_ge(S["tb_copied"], tb)
                eng.wait_ge(S["pc_copied"], tile + 1)
                eng.wait_ge(S["vwin_in"], 16 * (tile + 1))
                if tile:
                    eng.wait_ge(S["so_taken"], 2)
                for b in range(4 * tile, 4 * tile + 4):
                    bl = b % 4
                    c = slice(32 * bl, 32 * bl + 32)
                    out = bank(7)[:, 32 * b:32 * b + 32]
                    eng.wait_ge(vsel_in[b % 4], 16 * (b // 4 + 1))
                    eng.matmul(out, vc_s[0:CB_S, b, :], PTS[0:CB_S, 14, c], start=True, stop=False)
                    for j in range(8):
                        eng.matmul(out, vsel[:, bl, j * P:(j + 1) * P], PTS[:, j, c], start=False, stop=False)
                    for j in range(4):
                        eng.matmul(out, vwin[:, bl, j * P:(j + 1) * P], PTS[:, 9 + j, c], start=False, stop=False)
                    eng.matmul(out, vtok[0:NS, 4, 0, :], PTS[0:NS, 8, c], start=False, stop=False)
                    eng.matmul(out, vtok[0:NS, 4, 1, :], PTS[0:NS, 13, c], start=False, stop=True).then_inc(S["so_done"], 1)
            eng.wait_ge(S["so_taken"], 4)
            eng.wait_ge(S["glu_ready"], 4)
            for c in range(KC):
                for nm in ("mg0", "mg1", "att", "ssm"):
                    gemm((nm, c))
            for c in range(KC):
                gemm(("wo", c), (lambda k: (S["mixed"], k + 1)) if c == 0 else None)
            eng.wait_ge(S["p_in"], 32)
            for k in range(2):
                pr, use = pair_of[("pt", k)], use_of[("pt", k)]
                eng.wait_ge(taken[pr], use - 1)
                flat = pair[pr][:, :, :].rearrange("p a b -> p (a b)")
                for t in range(5):
                    n = P if t < 4 else NS
                    ins = eng.transpose(flat[:, t * P:t * P + n], ptok[0:n, t, k * P:(k + 1) * P], ident[0:n, 0:n])
                ins.then_inc(sum_done[pr], 1)
            norm(1)
            for c in range(FC):
                gemm(("gate", c), normed(1) if c == 0 else None)
                gemm(("up", c))
            for c in range(KC):
                gemm(("down", c), (lambda k: out_of(("up", k))) if c == 0 else None)
            norm(2)
            eng.wait_ge(S["wple_in"], 16)
            for c in range(KC):
                gemm(("pg", c), normed(2) if c == 0 else None)
                gemm(("ple", c))
            norm(3)
            eng.wait_ge(*out_of(("norm", 3)))
            eng.wait_ge(*out_of(("ple", KC - 1)))
            for t in range(5):
                n = P if t < 4 else NS
                if t == 0:
                    eng.wait_ge(S["normed"], 4 * KC)
                for half in range(2):
                    if t >= 2:
                        eng.wait_ge(S["y_copied_a" if half else "y_copied_v"], t - 1)
                    for c in range(4):
                        ins = eng.transpose(bank(2 * (t % 2) + half)[0:n, c * P:(c + 1) * P], uT[:, 4 * half + c, t * P:t * P + n], ident)
                    ins.then_inc(S["y_turned"], 1)


_INS = """x_prompt x_sample cache_k_cmp cache_v_cmp cache_k_sel cache_v_sel cache_k_win cache_v_win state_ssm_re state_ssm_im
page_table p_prompt p_sample rel_bias final_norm attn_norm w_in cmp_pe_k cmp_w1_k cmp_w2_k cmp_pe_v cmp_w1_v cmp_w2_v ssm_a_re
ssm_a_im ssm_log_dt ssm_b_re ssm_b_im ssm_c_re ssm_c_im ssm_d w_glu b_glu w_att_br w_ssm_br w_o ffn_norm w_ffn_gate w_ffn_up
w_ffn_down ple_norm w_ple_gate w_ple""".split()
_KVP, _KVS, _WINS = (1, 1, T, KV, HD), (1, DB, DT, KV, HD), (1, DB, WIN, KV, HD)
_OUTS = [("y_prompt", (1, T, D)), ("y_sample", (DB, DT, D)),
         ("nk_cmp_p", _KVP), ("nv_cmp_p", _KVP), ("nk_sel_p", _KVP), ("nv_sel_p", _KVP), ("nk_win_p", _KVP), ("nv_win_p", _KVP),
         ("ns_re_p", (1, 1, SG, SP_)), ("ns_im_p", (1, 1, SG, SP_)),
         ("nk_cmp_s", _KVS), ("nv_cmp_s", _KVS), ("nk_sel_s", _KVS), ("nv_sel_s", _KVS), ("nk_win_s", _WINS), ("nv_win_s", _WINS),
         ("ns_re_s", (1, DB, SG, SP_)), ("ns_im_s", (1, DB, SG, SP_))]


def kernel(**inputs):
    import concourse.bacc as bacc
    from concourse.bass_utils import run_bass_kernel_spmd

    nc = bacc.Bacc("TRN2", target_bir_lowering=False, num_devices=1)
    arrays = {n: np.ascontiguousarray(inputs[n]) for n in _INS}
    arrays["consts"] = constants()
    arrays["buckets"] = bucket_table()
    a = {n: nc.dram_tensor("in_" + n, v.shape, mybir.dt.from_np(v.dtype), kind="ExternalInput").ap() for n, v in arrays.items()}
    for n, shape in _OUTS:
        a[n] = nc.dram_tensor("out_" + n, shape, F32, kind="ExternalOutput").ap()
    build(nc, a)
    r = run_bass_kernel_spmd(nc, [{"in_" + n: v for n, v in arrays.items()}], core_ids=[0])
    return tuple(r.results[0]["out_" + n] for n, _ in _OUTS)
```

```python
import math
from contextlib import ExitStack

import numpy as np

import concourse.bass as bass
from concourse import mybir

F32 = mybir.dt.float32
F32R = mybir.dt.float32r
I32 = mybir.dt.int32
U32 = mybir.dt.uint32
ALU = mybir.AluOpType
ACT = mybir.ActivationFunctionType
AX = mybir.AxisListType

P = 128
D = 1024
T = 512
DB, DT = 8, 4
NS = DB * DT
TT = T + NS
HT = TT // 2
PAST = 1024
PAGE = 128
NPAGES = PAST // PAGE
HEADS, KV, HD = 8, 2, 64
G = HEADS // KV
WIN = 512
SEL = 64
NSEL = PAST // SEL + 1
CH = 16
CB_P = T // CH - 1
CB_S = PAST // CH - 1
HID = 256
SG, SC, SP_ = 32, 16, 64
FF = 2816
PLE = 256
NBUCKET = 32
KC = D // P
FC = FF // P
EPS = 1e-6
MASK = -1e30
TILES = T // P
DMAX = PAST + DT - 1
TW = 912
TBASE = DMAX - 3 * P
LINE = TBASE + TW + 1
SHIFTS = 16
LPITCH = LINE + SHIFTS
SLAB = 1024
RING = 5
HI_RING = 3
C_Q, C_KV, C_NG, C_SU, C_MG = 0, 512, 1280, 1304, 1816
W_IN = C_MG + 2 * D
MAGIC = 12582912.0
TWO_PI = 2.0 * math.pi
TP_HI = float(np.float32(6.28125))
TP_LO = float(np.float32(TWO_PI - 6.28125))
K_ID, K_G, K_SM, K_WM, K_IO, K_MOD = 0, 128, 256, 320, 324, 338
K_N = 340


def bucket_table():
    n = np.arange(LINE)
    dist = DMAX - n
    d = np.maximum(dist, 0)
    exact = NBUCKET // 2
    nf = np.maximum(d, 1).astype(np.float32)
    large = exact + (np.log(nf / np.float32(exact)) / np.float32(math.log(128 / exact)) * np.float32(NBUCKET - exact)).astype(np.int32)
    b = np.where(d < exact, d, np.minimum(large, NBUCKET - 1))
    out = np.zeros((NBUCKET + 1, LINE), np.float32)
    out[b[dist >= 0], n[dist >= 0]] = 8.0
    out[NBUCKET, dist < 0] = MASK
    return out


def constants():
    c = np.zeros((P, K_N), np.float32)
    r = np.arange(P)
    c[:, K_ID:K_ID + P] = np.eye(P)
    b, kv, g, t = r // 32, r // 16 % 2, r // 4 % 4, r % 4
    same = (b[:, None] == b) & (kv[:, None] == kv) & (t[:, None] == t)
    c[:, K_G:K_G + P] = same
    for tile in range(2):
        for col in range(NS):
            c[:, K_SM + tile * NS + col] = np.where(4 * tile + b == col // DT, 0.0, MASK)
    for u in range(DT):
        c[:, K_WM + u] = np.where(u <= t, MASK, 0.0)
    c[:, K_IO:K_IO + NSEL - 3] = np.arange(1, NSEL - 2)
    c[:, K_MOD] = r % 16
    c[:, K_MOD + 1] = r % 8
    return c


def at(ap, offset, dims):
    return bass.AP(ap.tensor, ap.offset + offset, [list(ap.ap[0])] + dims)


def wide(ap, n, axis=None):
    dims = [list(x) for x in ap.ap]
    dims.insert(len(dims) if axis is None else axis, [0, n])
    return bass.AP(ap.tensor, ap.offset, dims)


def plan_gemms():
    groups, slabs = [], []

    def slab(kind, n, split=True):
        slabs.append((kind, n, split))
        return len(slabs) - 1

    def group(name, steps):
        groups.append((name, steps))

    def plain_steps(w, count, k0=0, m=P):
        return [(w, k * m, m, k0 + k) for k in range(count)]

    group(("norm", 0), None)
    for m in range(14):
        group(("z", m), plain_steps(slab("z", m), KC))
    group(("ng", 0), plain_steps(slab("ng", 0), KC, m=24))
    for s in range(2):
        w = slab("glu", s, False)
        for m in range(2):
            group(("glu", 2 * s + m), [(w, k * 256 + m * P, P, k) for k in range(4)])
    for c in range(KC):
        for kind in ("mg0", "mg1"):
            group((kind, c), plain_steps(slab(kind, c), KC))
        w = slab("att", c, False)
        group(("att", c), plain_steps(w, 4))
        group(("ssm", c), [(w, 512 + k * P, P, k) for k in range(4)])
    for c in range(KC):
        group(("wo", c), plain_steps(slab("wo", c), KC))
    group(("norm", 1), None)
    for c in range(FC):
        for kind in ("gate", "up"):
            group((kind, c), plain_steps(slab(kind, c), KC))
    for m in range(KC):
        steps = []
        for part in range(3):
            k0 = KC * part
            steps += plain_steps(slab("down", 3 * m + part), min(KC, FC - k0), k0)
        group(("down", m), steps)
    group(("norm", 2), None)
    for k in range(2):
        group(("pt", k), None)
    for c in range(KC):
        group(("pg", c), plain_steps(slab("pg", c), KC))
        group(("ple", c), [(None, k * D + c * P, P, k) for k in range(2)])
    group(("norm", 3), None)
    return groups, slabs


def build(nc, a):
    groups, slabs = plan_gemms()
    pair_of, use_of, count = {}, {}, [0] * 4
    last_use = {}
    landed_at, total = [], [0] * RING
    split_index = {}
    for n, (kind, m, split) in enumerate(slabs):
        total[n % RING] += 16 * (3 if kind == "att" else 2 if kind == "z" and m < 4 else 1)
        if split:
            split_index[n] = len(split_index)
        landed_at.append(total[n % RING])
    split_slab = list(split_index)
    for n, (name, steps) in enumerate(groups):
        pair = n % 4
        count[pair] += 1
        pair_of[name], use_of[name] = pair, count[pair]
        for st in steps or []:
            if st[0] is not None:
                last_use[st[0]] = name

    bias_line = nc.dram_tensor("bias_line", (HEADS, SHIFTS, LPITCH), F32, kind="Internal").ap()
    gate_rows = nc.dram_tensor("gate_rows", (NS, 24), F32, kind="Internal").ap()
    u_spill = nc.dram_tensor("u_spill", (P, KC * TT), F32, kind="Internal").ap()
    h_spill = nc.dram_tensor("h_spill", (P, KC * TT), F32, kind="Internal").ap()

    AR = 28400
    with ExitStack() as ctx:
        def sb(name, shape, dt=F32):
            return ctx.enter_context(nc.sbuf_tensor(name, shape, dt))

        def sem(name):
            return ctx.enter_context(nc.semaphore(name))

        kc_ = sb("consts", [P, K_N])[:, :]
        ident = kc_[:, K_ID:K_ID + P]
        ones = sb("ones", [P, P])[:, :]
        vec = sb("vec", [P, 120])[:, :]
        sp = sb("ssm_params", [P, 34, 16])
        shapes = [("uT", [P, KC, TT]), ("zT", [P, 14, TT]), ("ring", [P, RING + HI_RING, SLAB]), ("arena", [P, AR])]
        with ExitStack() as plain:
            uT, zT, ring, arena = [plain.enter_context(nc.sbuf_tensor(n, sh, F32)) for n, sh in shapes]
        uT_r, zT_r, ring_r = [sb(n + "_r", sh, F32R) for n, sh in shapes[:3]]
        cuts = [0, 10880, 22848, AR]
        pieces = [sb(f"arena_r{i}", [P, cuts[i + 1] - cuts[i]], F32R) for i in range(3)]
        zq = zT[:, 0:4, :]
        zkv = zT[:, 4:10, :]
        zsu = zT[:, 10:14, :]
        vtok = sb("vtok", [P, 5, 2, P])
        kcT_s = sb("kcT_s", [P, 2, 252])
        kcT_p = sb("kcT_p", [P, 32])
        vc_s = sb("vc_s", [64, DB, P])
        vc_p = sb("vc_p", [P, HD])
        gates = sb("gates", [P, TILES + 1, 24])
        gates_s = sb("gates_s", [P, 2, 3])
        small = sb("small", [P, 96])
        idx = sb("idx", [P, 16], I32)
        pages = sb("page_rows", [16, 32], I32)
        log_dt = sb("log_dt", [16, 2])
        eps_t = sb("eps_t", [P, 1])
        oT = zkv[:, 0:4, :]
        KS, KW = 4, 5
        ZSLOT = [0, 1, 4, 2, 5, 3]

        def ar(off, *dims):
            n = int(np.prod(dims))
            assert off + n <= AR
            v = arena[:, off:off + n]
            if len(dims) == 2:
                return v.rearrange("p (a b) -> p a b", b=dims[1])
            if len(dims) == 3:
                return v.rearrange("p (a b c) -> p a b c", b=dims[1], c=dims[2])
            if len(dims) == 4:
                return v.rearrange("p (a b c d) -> p a b c d", b=dims[1], c=dims[2], d=dims[3])
            return v

        def ar_r(off, a_, b_):
            i = max(i for i in range(3) if cuts[i] <= off)
            assert off + a_ * b_ <= cuts[i + 1]
            off -= cuts[i]
            return pieces[i][:, off:off + a_ * b_].rearrange("p (a b) -> p a b", b=b_)

        u_hi0 = ar_r(10880, KC, TT)
        xtok = ar(0, 5, D)
        hT0 = ar(5120, KC, TT)
        hot = arena[0:33, 20480:20480 + LINE]
        relb = arena[0:33, 22100:22100 + HEADS]
        line = arena[0:HEADS, 22120:22120 + LINE]
        nat = ar(23700, 256)[:, 0:P]
        spread = ar(25500, 3, P)
        rt0, rs0 = ar(26100, TT), ar(27200, TT)
        zng = arena[0:24, 24900:24900 + TT]
        tmp = ar(23840, 4, 16, 16)
        br_, bi_ = ar(16384, 16, 16), ar(16640, 16, 16)
        bbr, bbi = ar(16896, 16, 16), ar(17152, 16, 16)
        bt_ = ar(17408, 16, 16)
        bdr, bdi = ar(17664, 16, 32), ar(18176, 16, 32)
        cnat = ar(18688, 2, 4, P)
        h0nat = ar(19712, 2, P)
        tokst = ar(9472, 5, 512)
        BT = ar(0, 2, 4, P)
        CT = ar(1024, 2, 16, 32)
        Jt = ar(2048, 2, 16, 32)
        St = ar(3072, 2, 16, 16)
        Hs = ar(3584, 2, 16, NS)
        h0T = ar(4608, 2, P)
        rot = ar(5120, 6, T)
        Et = ar(8192, 2, 2, T)
        Hp = ar(10240, 2, 2, T)
        ptmp = ar(27136, 2, T)
        hfin = sb("hfin", [P, 2, 16])
        hfin_s = ar(26752, 2, P)
        hout = ar(27136, 4, P)
        glu_sig = ar(10240, 4, TT)
        w1 = ar(12288, 16, HID)
        XT = ar(16384, 8, KV, 256)
        raw = ar(20480, 2048)
        raw2 = ar(22528, 2048)
        Hh = ar(24576, 2, 504)
        XP = ar(25600, 16, 64)
        Hq = ar(26624, 2, 62)
        w2 = sb("w2", [P, 2, 2, HD])
        pb = sb("pe_bias", [P, 4])
        TZ = ar(0, HEADS, TW)
        Ssb = ar(7304, 4, T)
        Psb = [ar(9352, 4, T)[:, q, :] for q in range(4)] + [ar(15048, 2, T)[:, q, :] for q in range(2)]
        PTs = ar(11400, 4, T)
        dg = [ar(13448, 4, P)[:, q, :] for q in range(4)] + [ar(16072, 2, P)[:, q, :] for q in range(2)]
        PTc = ar(13960, TILES, 2, P)
        cs, ce = ar(7304, TILES * HEADS, 32), ar(8328, TILES * HEADS, 32)
        csum = ar(14984, 64)
        ksel = ar(16384, 2, 1024)
        vsel = ar(18432, 4, 1024)
        kwin = ar(22528, 4, 512)
        vwin = ar(24576, 4, 512)
        biasS = ar(26624, 1056)
        KT = ar(0, 2, 1024)
        KTw = ar(2048, 2, 512)
        bd = ar(3072, 1056)
        bw = ar(4128, 544)
        SS = ar(4672, 1056)
        SW = ar(5728, 544)
        PS_ = ar(6272, 1056)
        PW = ar(7328, 544)
        cc = ar(7872, 3, 64)
        PTS = ar(8064, 16, P)
        dgs = ar(10112, 2, P)
        Qb = ar(10368, DB, 32)
        hT = ar(0, KC, TT)
        mT = ar(KC * TT, KC, TT)
        sig = ar(8704, 4, TT)
        mid = ar(10880, FC, TT)
        sil = ar(22848, 2, TT)
        u_back = ar(10880, KC, TT)
        u_hi_mix = ar_r(10880, KC, TT)
        u_hi = ar_r(KC * TT, KC, TT)
        mT_lo, mT_hi = ar_r(KC * TT, KC, TT), ar_r(15232, KC, TT)
        mid_lo = ar_r(10880, FC, TT)
        mid_hi = [zT_r[:, c, :] for c in range(14)] + [ar_r(8704, 4, TT)[:, c, :] for c in range(4)] + \
                 [ar_r(23936, 4, TT)[:, c, :] for c in range(4)]
        pT = ar(10880, 2, TT)
        wple = ar(11968, 2048)
        rt, rs = ar(27136, TT), ar(27680, TT)
        ptok = vtok[:, :, :, :].rearrange("p t a b -> p t (a b)")
        ytok = ar(KC * TT, 2, D)

        pair = [ctx.enter_context(nc.psum_tensor(f"pair{i}", [P, 2, 512], F32)) for i in range(4)]

        def bank(b):
            return pair[b // 2][:, b % 2, :]

        slab_landed = [sem(f"slab_landed{i}") for i in range(RING)]
        sum_done = [sem(f"sum_done{i}") for i in range(4)]
        taken = [sem(f"taken{i}") for i in range(4)]
        names = """x0 const_in hot_in nat_in ssm_in ones_set line_done line_copied line_out turned_x copied_x
            vec_turned vec_copied squares normed h_out kvt_done tokst_copied vtok_copied kv_out v_step a_step g_step p_step
            ldt theta_ready sin_done bd_ready bd_turned bd_copied c_turned c_copied h0_turned h0_copied
            gate_out gate_in gates_turned gates_copied rows_in spread_ready spread_turned idx_ready
            w1_in w2_in raw_in raw_copied raw_turned turn_copied hid_done hid_taken c2_done c2_taken xp_ready
            xs_done samples_done ys_done ys_taken x_done x_taken E_ready E_used h_ready y_done y_taken z_ready
            fin_ready fin_turned fin_copied fin_out glu_ready
            toep_in cs_done cmax_done cexp_done cnorm_done cpt_done cpt_copied
            s_done s_taken exp_done diag_ready pt_done pt_copied o_done o_taken
            kwin_in vwin_in biasS_in tb_done tb_copied qb_ready sc_done cmin_done cexps impsum_ready
            imp_done bd_seen pc_ready pc_done pc_copied ss_done ss_taken sexp sdiag so_done so_taken
            h_in p_in wple_in mixed h_new y_turned y_copied_v y_copied_a win_out slab_high slab_split part_done u_new u_high uhi_out uhi_in u_returned mix_high mix_split mid_high mid_split fix_ready""".split()
        S = {n: sem(n) for n in names}
        ksel_in = [sem(f"ksel_in{i}") for i in range(2)]
        y_stored = [sem(f"y_stored{i}") for i in range(2)]
        vsel_in = [sem(f"vsel_in{i}") for i in range(4)]

        xp_t = a["x_prompt"].rearrange("b (t p) d -> p (b t) d", p=P)
        w_in = a["w_in"].rearrange("l (k p) n -> p (l k) n", p=P)

        def done(name):
            return sum_done[pair_of[name]], use_of[name]

        def slab_size(n):
            kind, m, _ = slabs[n]
            return KC * 24 if kind == "ng" else P * min(KC, FC - KC * (m % 3)) if kind == "down" else SLAB

        def used(n):
            kind, m, _ = slabs[n]
            if kind == "down" and m % 3 < 2:
                return S["part_done"], 2 * (m // 3) + m % 3 + 1
            return done(last_use[n])

        def out_of(name):
            return taken[pair_of[name]], use_of[name]

        def keys_turned(b):
            return 3 * (b + 1)

        def both(pr):
            return pair[pr][:, :, 0:HT]

        def halves(v):
            return v.rearrange("p (h n) -> p h n", h=2)

        block = ctx.enter_context(nc.Block())

        @block.sync
        def _(eng):
            gate_w = a["w_ffn_gate"].rearrange("l (k p) n -> p (l k) n", p=P)
            up_w = a["w_ffn_up"].rearrange("l (k p) n -> p (l k) n", p=P)
            down_w = a["w_ffn_down"].rearrange("l (k p) n -> p (l k) n", p=P)
            o_w = a["w_o"].rearrange("l (k p) n -> p (l k) n", p=P)
            glu_w = a["w_glu"].rearrange("l (k p) n -> p (l k) n", p=P)
            pg_w = a["w_ple_gate"].rearrange("l (k p) n -> p (l k) n", p=P)
            ssm_w = a["w_ssm_br"].rearrange("l (k p) n -> p (l k) n", p=P)

            def load_slab(n):
                kind, s, _ = slabs[n]
                slot = n % RING
                if n >= RING:
                    eng.wait_ge(*used(n - RING))
                dst = ring[:, slot, :]
                landed = slab_landed[slot]
                by_chunk = dst.rearrange("p (k n) -> p k n", k=KC)
                if kind == "z" and s < 4:
                    for h in range(2):
                        c0 = (s + G * h) * HD
                        eng.dma_start(by_chunk[:, :, HD * h:HD * h + HD], w_in[:, :, c0:c0 + HD]).then_inc(landed, 16)
                elif kind == "z":
                    c0 = C_KV + P * (s - 4) if s < 10 else C_SU + P * (s - 10)
                    eng.dma_start(by_chunk, w_in[:, :, c0:c0 + P]).then_inc(landed, 16)
                elif kind in ("mg0", "mg1", "gate", "up", "wo", "pg"):
                    src, c0 = {"mg0": (w_in, C_MG), "mg1": (w_in, C_MG + D), "gate": (gate_w, 0), "up": (up_w, 0),
                               "wo": (o_w, 0), "pg": (pg_w, 0)}[kind]
                    eng.dma_start(by_chunk, src[:, :, c0 + P * s:c0 + P * s + P]).then_inc(landed, 16)
                elif kind == "ng":
                    eng.dma_start(dst[:, 0:KC * 24].rearrange("p (k n) -> p k n", k=KC),
                                  w_in[:, :, C_NG:C_NG + 24]).then_inc(landed, 16)
                elif kind == "glu":
                    eng.dma_start(dst.rearrange("p (k n) -> p k n", k=4), glu_w[:, :, 256 * s:256 * s + 256]).then_inc(landed, 16)
                elif kind == "att":
                    v = dst[:, 0:512].rearrange("p (k n) -> p k n", k=4)
                    for h in range(2):
                        rows = a["w_att_br"][0, h * 256:(h + 1) * 256, P * s:P * s + P]
                        eng.dma_start(v[64 * h:64 * h + 64, :, :],
                                      rows.rearrange("(k p) n -> p k n", p=HD)).then_inc(landed, 16)
                    eng.dma_start(dst[:, 512:1024].rearrange("p (k n) -> p k n", k=4),
                                  ssm_w[:, :, P * s:P * s + P]).then_inc(landed, 16)
                elif kind == "down":
                    m, k0 = s // 3, KC * (s % 3)
                    n_k = min(KC, FC - k0)
                    eng.dma_start(by_chunk[:, 0:n_k, :], down_w[:, k0:k0 + n_k, m * P:(m + 1) * P]).then_inc(landed, 16)

            for t in range(TILES):
                eng.dma_start(xtok[:, t, :], xp_t[:, t, :]).then_inc(S["x0"], 16)
            eng.dma_start(xtok[0:NS, 4, :], a["x_sample"].rearrange("b t d -> (b t) d")).then_inc(S["x0"], 16)
            eng.dma_start(kc_, a["consts"]).then_inc(S["const_in"], 16)
            rows = lambda n, k: a[n].rearrange("l (r p) -> (l r) p", p=P)
            at_row = 0
            for n in ("attn_norm", "ffn_norm", "ple_norm"):
                eng.dma_start(nat[at_row:at_row + KC, :], rows(n, KC)).then_inc(S["nat_in"], 16)
                at_row += KC
            eng.dma_start(nat[24:32, :], a["final_norm"].rearrange("(r p) -> r p", p=P)).then_inc(S["nat_in"], 16)
            eng.dma_start(nat[32:36, :], rows("b_glu", 4)).then_inc(S["nat_in"], 16)
            eng.dma_start(nat[36:40, :], a["ssm_d"].rearrange("l (r g) c -> (l r) (g c)", r=4)).then_inc(S["nat_in"], 16)
            eng.dma_start(nat[40:56, :], a["ssm_a_re"].rearrange("l (j g) p -> (l j) (g p)", g=2)).then_inc(S["nat_in"], 16)
            eng.dma_start(nat[56:72, :], a["ssm_a_im"].rearrange("l (j g) p -> (l j) (g p)", g=2)).then_inc(S["nat_in"], 16)
            eng.dma_start(nat[72:88, :], a["cmp_pe_k"].rearrange("l (k r) d -> (l k) (r d)", r=2)).then_inc(S["nat_in"], 16)
            eng.dma_start(nat[88:104, :], a["cmp_pe_v"].rearrange("l (k r) d -> (l k) (r d)", r=2)).then_inc(S["nat_in"], 16)
            eng.dma_start(pages[0:8, 0:8], a["page_table"]).then_inc(S["rows_in"], 16)
            eng.dma_start(pages[0:4, 16:32], a["page_table"].rearrange("(a b) n -> a (b n)", b=2)).then_inc(S["rows_in"], 16)
            eng.dma_start(log_dt[:, :], a["ssm_log_dt"].rearrange("l (j g) -> (l j) g", g=2)).then_inc(S["rows_in"], 16)
            eng.dma_start(hot, a["buckets"]).then_inc(S["hot_in"], 16)
            eng.dma_start(relb[0:NBUCKET, :], a["rel_bias"]).then_inc(S["hot_in"], 16)
            load_slab(0)
            load_slab(1)
            for q, (src, dst) in enumerate((("ssm_b_re", br_), ("ssm_b_im", bi_))):
                eng.dma_start(dst, a[src].rearrange("l (j g) p c -> (g p) (l j) c", g=2)).then_inc(S["ssm_in"], 16)
            for q, src in enumerate(("ssm_c_re", "ssm_c_im")):
                v = a[src].rearrange("l (k g) c p -> (g c) (l k) p", k=4)
                for half in range(2):
                    eng.dma_start(cnat[:, q, :, 64 * half:64 * half + 64], v).then_inc(S["ssm_in"], 16)
            for q, src in enumerate(("state_ssm_re", "state_ssm_im")):
                eng.dma_start(h0nat[:, q, :], a[src].rearrange("l b (j g) p -> (l b j) (g p)", g=2)).then_inc(S["ssm_in"], 16)
            for n in range(2, RING):
                load_slab(n)
            rest = (WIN - DT) * KV * HD // 16
            for src, dst in (("cache_k_win", "nk_win_s"), ("cache_v_win", "nv_win_s")):
                dims = [[rest, 16], [WIN * KV * HD, DB], [1, rest]]
                eng.dma_start(bass.AP(a[dst].tensor, 0, dims),
                              bass.AP(a[src].tensor, DT * KV * HD, dims)).then_inc(S["win_out"], 16)
            eng.wait_ge(S["copied_x"], 10)
            eng.dma_start(h_spill, arena[:, 5120:5120 + KC * TT]).then_inc(S["h_out"], 16)
            eng.wait_ge(S["line_copied"], 4)
            eng.dma_start(bass.AP(bias_line.tensor, 0, [[SHIFTS * LPITCH, HEADS], [LPITCH + 1, SHIFTS], [1, LINE]]),
                          wide(line, SHIFTS, 1)).then_inc(S["line_out"], 16)
            for n in range(RING, 7):
                load_slab(n)
            eng.wait_ge(S["u_high"], KC)
            eng.dma_start(u_spill, u_hi0.rearrange("p a b -> p (a b)").bitcast(F32)).then_inc(S["uhi_out"], 16)
            for n in range(7, 20):
                load_slab(n)
            eng.wait_ge(*done(("ng", 0)))
            eng.wait_ge(S["uhi_out"], 16)
            eng.dma_start(w1, a["cmp_w1_k"].rearrange("l (k p) n -> p (l k) n", p=P)).then_inc(S["w1_in"], 16)
            for q, src in enumerate(("cmp_w2_k", "cmp_w2_v")):
                eng.dma_start(w2[:, q, :, :], a[src].rearrange("l (k p) n -> p (l k) n", p=P)).then_inc(S["w2_in"], 16)
            eng.wait_ge(S["gates_copied"], TILES + 1)
            eng.dma_start(gate_rows, gates[0:NS, TILES, :]).then_inc(S["gate_out"], 16)
            eng.wait_ge(S["gate_out"], 16)
            for b in range(DB):
                eng.dma_start(gates_s[32 * (b % 4):32 * (b % 4) + 32, b // 4, :],
                              bass.AP(gate_rows.tensor, DT * 24 * b, [[3, HEADS], [24, DT], [1, 3]])).then_inc(S["gate_in"], 16)
            eng.wait_ge(S["tokst_copied"], 5)
            eng.wait_ge(S["vtok_copied"], 5)
            stores = [("nk_cmp", 0, None), ("nv_cmp", 1, None), ("nk_sel", 2, None), ("nk_win", 3, None),
                      ("nv_sel", None, 0), ("nv_win", None, 1)]
            for n, q, v in stores:
                src = tokst[:, 0:4, q * P:(q + 1) * P] if v is None else vtok[:, 0:4, v, :]
                eng.dma_start(a[n + "_p"].rearrange("l b (t p) k d -> p (l b t) (k d)", p=P), src).then_inc(S["kv_out"], 16)
                src = tokst[0:NS, 4, q * P:(q + 1) * P] if v is None else vtok[0:NS, 4, v, :]
                if n.endswith("win"):
                    o = a[n + "_s"]
                    eng.dma_start(bass.AP(o.tensor, (WIN - DT) * P, [[WIN * P, DB], [P, DT], [1, P]]), src).then_inc(S["kv_out"], 16)
                else:
                    eng.dma_start(a[n + "_s"].rearrange("l b t k d -> (l b t) (k d)"), src).then_inc(S["kv_out"], 16)
            eng.wait_ge(S["hid_done"], 6)
            eng.dma_start(w1, a["cmp_w1_v"].rearrange("l (k p) n -> p (l k) n", p=P)).then_inc(S["w1_in"], 16)
            eng.wait_ge(S["fin_copied"], 4)
            for q, n in enumerate(("ns_re", "ns_im")):
                eng.dma_start(a[n + "_p"].rearrange("l b (j g) p -> (l b j) (g p)", g=2), hout[0:16, q, :]).then_inc(S["fin_out"], 16)
                eng.dma_start(a[n + "_s"].rearrange("l b (j g) p -> (l b j) (g p)", g=2), hout[:, 2 + q, :]).then_inc(S["fin_out"], 16)
            eng.wait_ge(S["c2_done"], 6)
            def window(n, dst, tile, s):
                eng.dma_start(dst, a[n][0, 4 * tile:4 * tile + 4].rearrange("b (p j) k d -> p b (j k d)", p=P)).then_inc(S[s], 16)

            window("cache_k_win", kwin, 0, "kwin_in")
            window("cache_v_win", vwin, 0, "vwin_in")
            eng.wait_ge(S["y_done"], 16)
            eng.wait_ge(S["fin_turned"], 4)
            eng.wait_ge(S["line_out"], 16)
            eng.wait_ge(S["fin_out"], 64)
            for p0 in range(0, P, SHIFTS):
                for k in range(KV):
                    eng.dma_start(TZ[p0:p0 + SHIFTS, k:HEADS:KV, :],
                                  bass.AP(bias_line.tensor, k * G * SHIFTS * LPITCH + TBASE - p0,
                                          [[LPITCH, SHIFTS], [SHIFTS * LPITCH, G], [1, TW]])).then_inc(S["toep_in"], 16)
            for b in range(4):
                eng.dma_start(biasS[32 * b:32 * b + 32, 0:PAST + DT],
                              bass.AP(bias_line.tensor, DT - 1, [[SHIFTS * LPITCH, HEADS], [LPITCH, DT], [1, PAST + DT]])).then_inc(S["biasS_in"], 16)
            load_slab(20)
            load_slab(21)
            eng.wait_ge(S["o_taken"], TILES)
            eng.dma_start(arena[:, 10880:10880 + KC * TT], u_spill).then_inc(S["uhi_in"], 16)
            eng.wait_ge(S["tb_done"], keys_turned(3))
            window("cache_k_win", kwin, 1, "kwin_in")
            eng.wait_ge(S["so_done"], 4)
            window("cache_v_win", vwin, 1, "vwin_in")
            eng.wait_ge(S["so_taken"], 4)
            eng.wait_ge(S["h_out"], 16)
            eng.dma_start(arena[:, 0:KC * TT], h_spill).then_inc(S["h_in"], 16)
            eng.wait_ge(S["kv_out"], 16 * 12)
            eng.dma_start(ptok[:, 0:4, :], a["p_prompt"].rearrange("l b (t p) d -> p (l b t) d", p=P)).then_inc(S["p_in"], 16)
            eng.dma_start(ptok[0:NS, 4, :], a["p_sample"].rearrange("l b t d -> (l b t) d")).then_inc(S["p_in"], 16)
            for n in range(22, len(slabs)):
                load_slab(n)
                if n == len(slabs) - KC + 3:
                    eng.wait_ge(*done(("down", KC - 1)))
                    eng.dma_start(wple.rearrange("p (k n) -> p k n", k=2), a["w_ple"].rearrange("l (k p) n -> p (l k) n", p=P)).then_inc(S["wple_in"], 16)
            for t in range(5):
                eng.wait_ge(S["y_copied_v"], t + 1)
                eng.wait_ge(S["y_copied_a"], t + 1)
                if t < 4:
                    eng.dma_start(a["y_prompt"][0, t * P:(t + 1) * P, :], ytok[:, t % 2, :]).then_inc(y_stored[t % 2], 16)
                else:
                    eng.dma_start(a["y_sample"].rearrange("b t d -> (b t) d"), ytok[0:NS, 0, :]).then_inc(y_stored[0], 16)
            eng.wait_ge(y_stored[0], 16 * 3)
            eng.wait_ge(y_stored[1], 16 * 2)
            eng.wait_ge(S["win_out"], 32)
            eng.wait_ge(S["kv_out"], 16 * 12)
            eng.wait_ge(S["fin_out"], 16 * 4)

        @block.gpsimd
        def _(eng):
            steps = [0]

            def link(ins):
                steps[0] += 1
                ins.then_inc(S["g_step"], 1)
                eng.wait_ge(S["g_step"], steps[0])

            pools = {n: a[n] for n in ("cache_k_cmp", "cache_v_cmp", "cache_k_sel", "cache_v_sel")}

            def gather_cmp(n):
                kv, tile = n // 4, n % 4
                if n:
                    eng.wait_ge(S["raw_copied"], n)
                src = pools["cache_k_cmp" if kv == 0 else "cache_v_cmp"].rearrange("l n (c r) k d -> (l n c) (r k d)", r=CH)
                eng.indirect_dma_start(out=raw, out_offset=None, in_=src,
                                       in_offset=bass.IndirectOffsetOnAxis(ap=idx[:, 8 + tile:9 + tile].bitcast(U32), axis=0)).then_inc(S["raw_in"], 16)

            def gather_sel(which, b):
                src = pools["cache_k_sel" if which == 0 else "cache_v_sel"].rearrange("l n (c r) k d -> (l n c) (r k d)", r=8)
                dst = ksel[:, b % 2, :] if which == 0 else vsel[:, b % 4, :]
                eng.indirect_dma_start(out=dst, out_offset=None, in_=src,
                                       in_offset=bass.IndirectOffsetOnAxis(ap=idx[:, b:b + 1].bitcast(U32), axis=0)).then_inc(ksel_in[b % 2] if which == 0 else vsel_in[b % 4], 16)

            def split(n):
                q = split_index[n]
                eng.wait_ge(S["slab_high"], q + 1)
                hi = ring_r[:, RING + q % HI_RING, 0:slab_size(n)].bitcast(F32)
                eng.tensor_tensor(ring_r[:, n % RING, 0:slab_size(n)], ring[:, n % RING, 0:slab_size(n)], hi, ALU.subtract).then_inc(S["slab_split"], 1)

            for n in range(15):
                split(n)
            eng.wait_ge(S["idx_ready"], 2)
            eng.wait_ge(S["line_out"], 16)
            eng.wait_ge(S["vec_turned"], 1)
            gather_cmp(0)
            eng.wait_ge(S["theta_ready"], 1)
            eng.wait_ge(S["kv_out"], 16 * 12)
            eng.wait_ge(S["h_out"], 16)
            raws = 1
            for j in range(16):
                if j:
                    eng.wait_ge(S["E_ready"], j)
                if j >= 2:
                    eng.wait_ge(S["E_used"], j - 1)
                J = lambda c: wide(Jt[:, c, j, :], 16)
                Sx = lambda c: wide(St[:, c, j, :], 32, 1)
                t0 = ptmp[:, 0, :].rearrange("p (a b) -> p a b", b=16)
                t1 = ptmp[:, 1, :].rearrange("p (a b) -> p a b", b=16)
                E = lambda c: Et[:, j % 2, c, :].rearrange("p (a b) -> p a b", b=16)
                eng.tensor_tensor(t0, J(0), Sx(0), ALU.mult)
                link(eng.tensor_tensor(t1, J(1), Sx(1), ALU.mult))
                link(eng.tensor_tensor(E(0), t0, t1, ALU.subtract))
                eng.tensor_tensor(t0, J(0), Sx(1), ALU.mult)
                link(eng.tensor_tensor(t1, J(1), Sx(0), ALU.mult))
                eng.tensor_tensor(E(1), t0, t1, ALU.add).then_inc(S["E_ready"], 1)
                if j % 2 == 0 and raws < 8:
                    gather_cmp(raws)
                    raws += 1
            while raws < 8:
                gather_cmp(raws)
                raws += 1
            split(17)
            split(18)
            eng.wait_ge(S["c2_done"], 6)
            for which, b in [(0, 0), (0, 1)] + [(1, b) for b in range(4)] + [(0, b) for b in range(2, DB)] + [(1, b) for b in range(4, DB)]:
                if which == 0 and b >= 2:
                    eng.wait_ge(S["tb_done"], keys_turned(b - 2))
                if which == 1 and b >= 4:
                    eng.wait_ge(S["so_done"], b - 3)
                gather_sel(which, b)
            for n in range(19, len(slabs)):
                if n in split_index:
                    split(n)

        def pt_copy(eng, n):
            W = P * (n // 8 + 1)
            for br in range(2):
                eng.wait_ge(S["pt_done"], 2 * n + br + 1)
                if n >= 2:
                    eng.wait_ge(S["o_done"], n - 1)
                eng.activation(PTs[:, 2 * (n % 2) + br, 0:W], bank(4 + br)[:, 0:W], ACT.Copy).then_inc(S["pt_copied"], 1)

        @block.scalar
        def _(eng):
            steps = [0]

            def link(ins):
                steps[0] += 1
                ins.then_inc(S["a_step"], 1)
                eng.wait_ge(S["a_step"], steps[0])

            def squares(n, src, gate, after=None):
                for k in range(KC):
                    gate(k)
                    eng.activation(uT[:, k, :], src[:, k, :], ACT.Square).then_inc(S["squares"], 1)
                    if after:
                        high_after((after, k))

            def root(n, dst):
                eng.wait_ge(*done(("norm", n)))
                eng.activation(halves(dst), both(pair_of[("norm", n)]), ACT.Sqrt, bias=eps_t[:, :], scale=1.0 / D).then_inc(taken[pair_of[("norm", n)]], 1)

            def high_after(name, part=2):
                slab = [st[0] for st in dict(groups)[name]][KC * part if name[0] == "down" else 0]
                weights_high(split_index[slab] + HI_RING)

            def weights_high(q):
                if q >= len(split_slab):
                    return
                n = split_slab[q]
                if q >= HI_RING:
                    eng.wait_ge(*used(split_slab[q - HI_RING]))
                eng.wait_ge(slab_landed[n % RING], landed_at[n])
                eng.activation(ring_r[:, RING + q % HI_RING, 0:slab_size(n)], ring[:, n % RING, 0:slab_size(n)], ACT.Copy).then_inc(S["slab_high"], 1)

            def high(n, dst):
                for k in range(KC):
                    eng.wait_ge(S["u_new"], KC * n + k + 1)
                    eng.activation(dst[:, k, :], uT[:, k, :], ACT.Copy).then_inc(S["u_high"], 1)

            for q in range(HI_RING):
                weights_high(q)
            eng.wait_ge(S["ones_set"], 2)
            squares(0, hT0, lambda k: eng.wait_ge(S["copied_x"], 10) if k == 0 else None)
            root(0, rt0)
            high(0, u_hi0)
            ldt, ar_, dt, mag = vec[:, 104:120], vec[:, 40:56], sp[:, 0, :], sp[:, 1, :]
            eng.wait_ge(S["vec_copied"], 1)
            eng.activation(dt, ldt, ACT.Exp).then_inc(S["ldt"], 1)
            eng.wait_ge(S["ldt"], 2)
            eng.activation(mag, sp[:, 2, :], ACT.Exp).then_inc(S["sin_done"], 1)
            eng.wait_ge(S["ldt"], 4)
            eng.activation(sp[:, 5, :], sp[:, 3, :], ACT.Sin).then_inc(S["sin_done"], 1)
            eng.activation(sp[:, 6, :], sp[:, 4, :], ACT.Sin).then_inc(S["sin_done"], 1)
            for m in range(14):
                name = ("z", m)
                eng.wait_ge(*done(name))
                dst = zq[:, m, :] if m < 4 else zkv[:, ZSLOT[m - 4], :] if m < 10 else zsu[:, m - 10, :]
                eng.activation(halves(dst), both(pair_of[name]), ACT.Copy).then_inc(taken[pair_of[name]], 1)
                if m < 12:
                    high_after(name)
            eng.wait_ge(*done(("ng", 0)))
            eng.activation(halves(zng), pair[pair_of[("ng", 0)]][0:24, :, 0:HT], ACT.Sigmoid).then_inc(taken[pair_of[("ng", 0)]], 1)
            eng.wait_ge(S["uhi_out"], 16)
            for t in range(5):
                n = P if t < 4 else NS
                eng.wait_ge(S["kvt_done"], 2 * t + 1)
                eng.activation(tokst[0:n, t, :], bank(2 * (t % 2))[0:n, :], ACT.Copy).then_inc(S["tokst_copied"], 1)
            high_after(("z", 12))
            high_after(("z", 13))
            eng.wait_ge(S["gate_out"], 16)
            eng.wait_ge(S["gates_turned"], 1)
            turn = hid = c2 = 0
            for kv in range(2):
                for h in range(2):
                    eng.wait_ge(S["hid_done"], hid + 1)
                    b = bank(hid % 2)
                    link(eng.activation(pb[:, 2 * kv + h:2 * kv + h + 1], b[:, 62:63], ACT.Copy))
                    eng.activation(Hq[:, h, :], b[:, 0:62], ACT.Gelu_apprx_tanh, bias=pb[:, 2 * kv + h:2 * kv + h + 1]).then_inc(S["hid_taken"], 1)
                    hid += 1
                eng.wait_ge(S["c2_done"], c2 + 1)
                if kv == 0:
                    eng.activation(kcT_p[:, 0:CB_P], bank(7)[:, 0:CB_P], ACT.Copy).then_inc(S["c2_taken"], 1)
                else:
                    for q in range(4):
                        r = slice(32 * q, 32 * q + CB_P)
                        ins = eng.activation(vc_p[r, :], bank(7)[r, 0:HD], ACT.Copy)
                    ins.then_inc(S["c2_taken"], 1)
                c2 += 1
                for bg in range(2):
                    for tt in range(2):
                        for q in range(4):
                            ckv, ph = q // 2, q % 2
                            eng.wait_ge(S["raw_turned"], turn + 1)
                            eng.activation(XT[:, 4 * ph:4 * ph + 4, ckv, tt * P:(tt + 1) * P],
                                           bank(2 + turn % 2).rearrange("p (a b) -> p a b", b=P), ACT.Copy).then_inc(S["turn_copied"], 1)
                            turn += 1
                    for h in range(2):
                        eng.wait_ge(S["hid_done"], hid + 1)
                        eng.activation(Hh[:, h, :], bank(hid % 2)[:, 0:504], ACT.Gelu_apprx_tanh,
                                       bias=pb[:, 2 * kv + h:2 * kv + h + 1]).then_inc(S["hid_taken"], 1)
                        hid += 1
                    eng.wait_ge(S["c2_done"], c2 + 1)
                    if kv == 0:
                        eng.activation(kcT_s[:, bg, :], bank(7)[:, 0:252], ACT.Copy).then_inc(S["c2_taken"], 1)
                    else:
                        eng.activation(vc_s[0:CB_S, 4 * bg:4 * bg + 4, :], bank(7)[0:CB_S, :].rearrange("p (a b) -> p a b", b=P), ACT.Copy).then_inc(S["c2_taken"], 1)
                    c2 += 1
            for c in range(4):
                eng.wait_ge(S["y_taken"], c + 1)
                eng.activation(zsu[:, c, :], zsu[:, c, :], ACT.Gelu_apprx_tanh).then_inc(S["z_ready"], 1)
            for m in range(4):
                name = ("glu", m)
                eng.wait_ge(*done(name))
                eng.activation(halves(glu_sig[:, m, :]), both(pair_of[name]), ACT.Sigmoid, bias=vec[:, 32 + m:33 + m]).then_inc(taken[pair_of[name]], 1)
            eng.wait_ge(S["cmax_done"], 1)
            eng.activation(ce[:, :, 0:CB_P], cs[:, :, 0:CB_P], ACT.Exp, scale=0.125).then_inc(S["cexp_done"], 1)
            for half in range(2):
                eng.wait_ge(S["cpt_done"], half + 1)
                eng.activation(PTc[:, 2 * half:2 * half + 2, :, :].rearrange("p i a b -> p (i a) b"),
                               bank(4 + half).rearrange("p (a b) -> p a b", b=P), ACT.Copy).then_inc(S["cpt_copied"], 1)
            n = 0
            for i in range(TILES):
                W = P * (i + 1)
                for g in range(G):
                    for kv in range(KV):
                        for br in range(2):
                            q = 2 * (n % 3) + br
                            eng.wait_ge(S["s_taken"], 2 * n + br + 1)
                            if n >= 3:
                                eng.wait_ge(S["pt_done"], 2 * (n - 3) + br + 1)
                            eng.activation(Psb[q][:, 0:W], Ssb[:, 2 * (n % 2) + br, 0:W], ACT.Exp, bias=small[:, q:q + 1], scale=-1.0,
                                           accum_out=small[:, 24 + q:25 + q]).then_inc(S["exp_done"], 1)
                        if n >= 2:
                            pt_copy(eng, n - 2)
                        n += 1
            pt_copy(eng, n - 2)
            pt_copy(eng, n - 1)
            tb = 0

            def tb_copy(dst, src):
                nonlocal tb
                eng.wait_ge(S["tb_done"], tb + 1)
                ins = eng.activation(dst, src(bank(4 + tb % 2)), ACT.Copy)
                ins.then_inc(S["tb_copied"], 1)
                tb += 1

            by4 = lambda x: x.rearrange("p (a b) -> p a b", b=P)

            def keys_out(tile):
                eng.wait_ge(S["cmin_done"], tile + 1)
                eng.activation(cc[:, 1, 0:CB_S], cc[:, 0, 0:CB_S], ACT.Exp, bias=small[:, 16:17], scale=-1.0, accum_out=small[:, 17:18]).then_inc(S["cexps"], 1)
                for b in range(4 * tile, 4 * tile + 4):
                    for j0 in (0, 4):
                        tb_copy(at(KT[:, b % 2, :], j0, [[1, 4], [8, P]]), by4)
                    tb_copy(at(KTw[:, b % 2, :], 0, [[1, 4], [4, P]]), by4)

            def exps(tile):
                eng.wait_ge(S["ss_taken"], 2 * tile + 1)
                eng.activation(PS_, SS, ACT.Exp, bias=small[:, 18:19], scale=-1.0, accum_out=small[:, 20:21]).then_inc(S["sexp"], 1)
                eng.wait_ge(S["ss_taken"], 2 * tile + 2)
                eng.activation(PW, SW, ACT.Exp, bias=small[:, 19:20], scale=-1.0, accum_out=small[:, 21:22]).then_inc(S["sexp"], 1)

            def probs_out():
                tb_copy(PTS[:, 0:4, :], by4)
                tb_copy(PTS[:, 4:8, :], by4)
                tb_copy(PTS[:, 9:13, :], by4)
                tb_copy(at(PTS[0:NS, 8, :], 0, [[5 * P, 2], [1, P]]), lambda x: x[0:NS, 0:256].rearrange("p (a b) -> p a b", b=P))

            keys_out(0)
            exps(0)
            keys_out(1)
            probs_out()
            exps(1)
            eng.wait_ge(S["so_done"], 4)
            probs_out()
            def mix_high(c):
                eng.wait_ge(S["mixed"], c + 1)
                eng.activation(mT_hi[:, c, :], mT[:, c, :], ACT.Copy).then_inc(S["mix_high"], 1)

            def mid_part(c):
                eng.wait_ge(*out_of(("up", c)))
                eng.activation(mid_hi[c], mid[:, c, :], ACT.Copy).then_inc(S["mid_high"], 1)

            eng.wait_ge(S["uhi_in"], 16)
            for k in range(KC):
                eng.activation(u_hi_mix[:, k, :], u_back[:, k, :], ACT.Copy).then_inc(S["u_returned"], 1)
            high_after(("ng", 0))
            for c in range(KC):
                for q, nm in enumerate(("mg0", "mg1")):
                    name = (nm, c)
                    eng.wait_ge(*done(name))
                    if c >= 2:
                        eng.wait_ge(S["mixed"], c - 1)
                    eng.activation(halves(sig[:, 2 * (c % 2) + q, :]), both(pair_of[name]), ACT.Sigmoid).then_inc(taken[pair_of[name]], 1)
                    high_after(name)
                if c:
                    mix_high(c - 1)
            mix_high(KC - 1)
            squares(1, hT, lambda k: eng.wait_ge(*out_of(("wo", k))), "wo")
            root(1, rt)
            high(1, u_hi)
            for c in range(FC):
                name = ("gate", c)
                eng.wait_ge(*done(name))
                if c >= 2:
                    eng.wait_ge(*out_of(("up", c - 2)))
                eng.activation(halves(sil[:, c % 2, :]), both(pair_of[name]), ACT.Silu).then_inc(taken[pair_of[name]], 1)
                if c:
                    mid_part(c - 1)
                    high_after(("up", c - 1))
                high_after(name)
            mid_part(FC - 1)
            high_after(("up", FC - 1))
            def down_taken(k):
                high_after(("down", k), 0)
                high_after(("down", k), 1)
                eng.wait_ge(*out_of(("down", k)))

            squares(2, hT, down_taken, "down")
            root(2, rt)
            high(2, u_hi)
            for c in range(KC):
                name = ("pg", c)
                eng.wait_ge(*done(name))
                if c >= 2:
                    eng.wait_ge(S["h_new"], c - 1)
                eng.activation(halves(sig[:, c % 2, :]), both(pair_of[name]), ACT.Sigmoid).then_inc(taken[pair_of[name]], 1)
                high_after(name)
            eng.wait_ge(*done(("pg", KC - 1)))
            squares(3, hT, lambda k: eng.wait_ge(S["h_new"], k + 1))
            root(3, rt)
            for t in range(5):
                n = P if t < 4 else NS
                eng.wait_ge(S["y_turned"], 2 * t + 2)
                if t >= 2:
                    eng.wait_ge(y_stored[t % 2], 16 * (t // 2))
                eng.activation(ytok[0:n, t % 2, 512:1024], bank(2 * (t % 2) + 1)[0:n, :], ACT.Copy).then_inc(S["y_copied_a"], 1)

        @block.vector
        def _(eng):
            steps = [0]

            def link(ins):
                steps[0] += 1
                ins.then_inc(S["v_step"], 1)
                eng.wait_ge(S["v_step"], steps[0])

            def f32(x):
                return x.bitcast(F32)

            def tt(o, x, y, op):
                return eng.tensor_tensor(o, x, y, op)

            def low(n, k, hi):
                eng.wait_ge(S["u_high"], KC * n + k + 1)
                tt(uT_r[:, k, :], uT[:, k, :], f32(hi[:, k, :]), ALU.subtract).then_inc(S["normed"], 1)

            def mix_low(c):
                eng.wait_ge(S["mix_high"], c + 1)
                tt(mT_lo[:, c, :], mT[:, c, :], f32(mT_hi[:, c, :]), ALU.subtract).then_inc(S["mix_split"], 1)

            def mid_low(c):
                eng.wait_ge(S["mid_high"], c + 1)
                tt(mid_lo[:, c, :], mid[:, c, :], f32(mid_hi[c]), ALU.subtract).then_inc(S["mid_split"], 1)

            def normalise(n, src, col, rt_, rs_, hi=None):
                eng.wait_ge(*out_of(("norm", n)))
                link(eng.reciprocal(rs_, rt_))
                for k in range(KC):
                    eng.scalar_tensor_tensor(uT[:, k, :], src[:, k, :], vec[:, col + k:col + k + 1], rs_, ALU.mult, ALU.mult).then_inc(S["u_new"], 1)
                    if hi is not None and k:
                        low(n, k - 1, hi)
                if hi is not None:
                    low(n, KC - 1, hi)

            def xp_fill(kv):
                if kv:
                    eng.wait_ge(S["hid_done"], 2)
                for par in range(2):
                    for k in range(KV):
                        src = zkv[64 * k:64 * k + 64, ZSLOT[kv], 0:T].rearrange("p (c q r) -> p q c r", q=8, r=2)[:, :, :, par]
                        for half in range(2):
                            eng.tensor_copy(XP[64 * par:64 * par + 64, 8 * half:8 * half + 8, CB_P * k:CB_P * (k + 1)],
                                            src[:, :, half:half + CB_P])
                eng.tensor_copy(XP[:, :, 62:63], vec[:, 72 + 16 * kv:88 + 16 * kv].rearrange("p (a b) -> p a b", b=1)).then_inc(S["xp_ready"], 1)

            def raw_copy(n):
                eng.wait_ge(S["raw_in"], 16 * (n + 1))
                if n:
                    eng.wait_ge(S["raw_turned"], 4 * n)
                for par in range(2):
                    ins = eng.tensor_copy(raw2.rearrange("p (q k r d) -> p q k r d", k=KV, r=2, d=HD)[:, :, :, par, :],
                                          raw.rearrange("p (q r k d) -> p q r k d", r=2, k=KV, d=HD)[:, :, par, :, :])
                ins.then_inc(S["raw_copied"], 1)

            def y_out(c):
                eng.wait_ge(S["y_done"], 4 * c + 4)
                eng.scalar_tensor_tensor(zsu[:, c, 0:T], zsu[:, c, 0:T], vec[:, 36 + c:37 + c], bank(6), ALU.mult, ALU.add).then_inc(S["y_taken"], 1)

            def diag(n):
                q0, i, h = 2 * (n % 3), n // 8, n % 8
                head = (h % KV) * G + h // KV
                inv = small[:, 32 + q0:34 + q0]
                eng.wait_ge(S["exp_done"], 2 * n + 2)
                if n >= 3:
                    eng.wait_ge(S["pt_done"], 2 * (n - 2))
                link(eng.tensor_scalar(inv, small[:, 24 + q0:26 + q0], 1e-30, None, ALU.max))
                link(eng.reciprocal(inv, inv))
                for br in range(2):
                    gc = 3 * head + 1 + br
                    eng.tensor_scalar(dg[q0 + br], ident, inv[:, br:br + 1], gates[:, i, gc:gc + 1], ALU.mult, ALU.mult).then_inc(S["diag_ready"], 1)

            def take_o(i):
                eng.tensor_copy(oT[:, :, i * P:(i + 1) * P], bank(6).rearrange("p (a b) -> p a b", b=P)).then_inc(S["o_taken"], 1)

            eng.memset(ones, 1.0).then_inc(S["ones_set"], 1)
            eng.memset(eps_t[:, :], EPS).then_inc(S["ones_set"], 1)
            eng.memset(relb[NBUCKET:NBUCKET + 1, :], 1.0).then_inc(S["ones_set"], 1)
            eng.wait_ge(S["rows_in"], 48)
            for q, (src, n) in enumerate(((pages[0:8, 0:8], 16), (pages[0:4, 16:32], 8), (log_dt[:, :], SP_))):
                rows = src.ap[0][1]
                eng.tensor_copy(spread[0:rows, q, :].rearrange("p (a b) -> p a b", b=n), wide(src, n)).then_inc(S["spread_ready"], 1)
            eng.wait_ge(S["vec_turned"], 1)
            eng.tensor_copy(vec[:, 0:104], bank(2)[:, 0:104])
            eng.wait_ge(S["spread_turned"], 1)
            eng.tensor_copy(vec[:, 104:120], bank(3)[:, 32:48]).then_inc(S["vec_copied"], 1)
            for q in range(10):
                t, kk = q // 2, q % 2
                n = P if t < 4 else NS
                eng.wait_ge(S["turned_x"], q + 1)
                eng.tensor_copy(hT0[:, 4 * kk:4 * kk + 4, t * P:t * P + n],
                                bank(q % 2).rearrange("p (a b) -> p a b", b=P)[:, :, 0:n]).then_inc(S["copied_x"], 1)
            for q in range(4):
                eng.wait_ge(S["line_done"], q + 1)
                n = LINE // 4
                eng.tensor_copy(line[:, q * n:(q + 1) * n], bank(4 + q)[0:HEADS, 0:n]).then_inc(S["line_copied"], 1)
            eng.tensor_scalar(idx[:, 0:8], bank(3)[:, 0:8], 16.0, kc_[:, K_MOD:K_MOD + 1], ALU.mult, ALU.add).then_inc(S["idx_ready"], 1)
            eng.tensor_scalar(idx[:, 8:12], bank(3)[:, 16:20], 8.0, kc_[:, K_MOD + 1:K_MOD + 2], ALU.mult, ALU.add).then_inc(S["idx_ready"], 1)
            normalise(0, hT0, 0, rt0, rs0, u_hi0)
            v = lambda q: sp[:, q, :]
            are, aim = vec[:, 40:56], vec[:, 56:72]
            DTc, MAG, AD, TH, TH2, SN, CS, ABR, ABI, FR, FI, T0, T1, T2, T3 = range(15)
            eng.wait_ge(S["ldt"], 1)
            tt(v(AD), are, v(DTc), ALU.mult).then_inc(S["ldt"], 1)
            link(tt(v(T0), aim, v(DTc), ALU.mult))
            for q, shift in ((TH, 0.0), (TH2, math.pi / 2)):
                link(eng.tensor_scalar(v(T1), v(T0), shift, None, ALU.add))
                link(eng.tensor_scalar(v(T2), v(T1), 1.0 / TWO_PI, MAGIC, ALU.mult, ALU.add))
                link(eng.tensor_scalar(v(T2), v(T2), -MAGIC, None, ALU.add))
                link(eng.scalar_tensor_tensor(v(T3), v(T2), -TP_HI, v(T1), ALU.mult, ALU.add))
                link(eng.scalar_tensor_tensor(v(T3), v(T2), -TP_LO, v(T3), ALU.mult, ALU.add))
                eng.tensor_scalar(v(q), v(T3), math.pi * (1 - 1e-7), -math.pi * (1 - 1e-7), ALU.min, ALU.max).then_inc(S["ldt"], 1)
            eng.wait_ge(S["sin_done"], 3)
            tt(v(ABR), v(MAG), v(CS), ALU.mult)
            tt(v(ABI), v(MAG), v(SN), ALU.mult)
            tt(v(T0), are, are, ALU.mult)
            link(tt(v(T1), aim, aim, ALU.mult))
            link(tt(v(T0), v(T0), v(T1), ALU.add))
            link(eng.reciprocal(v(T1), v(T0)))
            link(eng.tensor_scalar(v(T0), v(ABR), -1.0, None, ALU.add))
            tt(v(T2), v(T0), are, ALU.mult)
            link(tt(v(T3), v(ABI), aim, ALU.mult))
            link(tt(v(T2), v(T2), v(T3), ALU.add))
            link(tt(v(FR), v(T2), v(T1), ALU.mult))
            tt(v(T2), v(ABI), are, ALU.mult)
            link(tt(v(T3), v(T0), aim, ALU.mult))
            link(tt(v(T2), v(T2), v(T3), ALU.subtract))
            link(tt(v(FI), v(T2), v(T1), ALU.mult))
            eng.wait_ge(S["ssm_in"], 16 * 8)
            eng.memset(bdr, 0.0)
            eng.memset(bdi, 0.0)
            fr, fi = wide(v(FR), 16), wide(v(FI), 16)
            link(tt(bbr, br_, fr, ALU.mult))
            link(tt(bt_, bi_, fi, ALU.mult))
            link(tt(bbr, bbr, bt_, ALU.subtract))
            link(tt(bbi, bi_, fr, ALU.mult))
            link(tt(bt_, br_, fi, ALU.mult))
            link(tt(bbi, bbi, bt_, ALU.add))
            for src, dst in ((bbr, bdr), (bbi, bdi)):
                for half in range(2):
                    r = slice(64 * half, 64 * half + 64)
                    eng.tensor_copy(dst[r, :, 16 * half:16 * half + 16], src[r, :, :]).then_inc(S["bd_ready"], 1)
            eng.wait_ge(S["turned_x"], 10)
            pw = [sp[:, 16 + 2 * q:18 + 2 * q, :] for q in range(6)]

            def cmul(o, x, y, n):
                t = [tmp[:, q, :, 0:n] for q in range(4)]
                link(tt(t[0], x[0], y[0], ALU.mult))
                tt(t[1], x[1], y[1], ALU.mult)
                tt(t[2], x[0], y[1], ALU.mult)
                link(tt(t[3], x[1], y[0], ALU.mult))
                tt(o[0], t[0], t[1], ALU.subtract)
                link(tt(o[1], t[2], t[3], ALU.add))

            col = lambda q: [sp[:, 16 + 2 * q + c, :] for c in range(2)]
            flat = lambda c: at(c, 0, [list(c.ap[-1]), [1, 1]])
            eng.tensor_copy(col(0)[0], v(CS))
            link(eng.tensor_copy(col(0)[1], v(SN)))
            cur = 0
            for table, top in ((St, 16), (Jt, 32)):
                eng.memset(table[:, 0, :, 0:1], 1.0)
                link(eng.memset(table[:, 1, :, 0:1], 0.0))
                n = 1
                while n < top:
                    p_ = [wide(c, n) for c in col(cur)]
                    cmul([table[:, c, :, n:2 * n] for c in range(2)], [table[:, c, :, 0:n] for c in range(2)], p_, n)
                    if (table is St) or n * 2 < top:
                        x = [flat(c) for c in col(cur)]
                        cmul([flat(c) for c in col(1 - cur)], x, x, 1)
                        cur = 1 - cur
                    n *= 2
            link(eng.memset(Hs[:, :, :, :].rearrange("p a b c -> p (a b c)"), 0.0))
            eng.memset(CT[:, :, :, :].rearrange("p a b c -> p (a b c)"), 0.0).then_inc(S["theta_ready"], 1)
            for q in range(2):
                eng.wait_ge(S["bd_turned"], q + 1)
                eng.tensor_copy(BT[:, q, :, :], bank(4 + q).rearrange("p (a b) -> p a b", b=P)).then_inc(S["bd_copied"], 1)
            eng.wait_ge(S["theta_ready"], 1)
            for q in range(2):
                eng.wait_ge(S["c_turned"], q + 1)
                for half in range(2):
                    r = slice(64 * half, 64 * half + 64)
                    src = bank(6 + q)[r, :].rearrange("p (j g c) -> p j g c", g=2, c=16)[:, :, half, :]
                    eng.tensor_scalar(CT[r, q, :, 16 * half:16 * half + 16], src, -1.0 if q else 1.0, None, ALU.mult).then_inc(S["c_copied"], 1)
            eng.wait_ge(S["h0_turned"], 1)
            eng.tensor_copy(h0T[:, :, :], bank(4)[:, 0:256].rearrange("p (a b) -> p a b", b=P)).then_inc(S["h0_copied"], 1)
            for t in range(5):
                n = P if t < 4 else NS
                eng.wait_ge(S["kvt_done"], 2 * t + 2)
                eng.tensor_copy(vtok[0:n, t, :, :], bank(2 * (t % 2) + 1)[0:n, 0:256].rearrange("p (a b) -> p a b", b=P)).then_inc(S["vtok_copied"], 1)
            eng.wait_ge(S["gates_turned"], 1)
            for t in range(TILES + 1):
                n = P if t < TILES else NS
                eng.tensor_copy(gates[0:n, t, :], bank(5)[0:n, 32 * t:32 * t + 24]).then_inc(S["gates_copied"], 1)
            eng.wait_ge(S["h_out"], 16)
            xp_fill(0)
            raw_copy(0)
            eng.wait_ge(S["xs_done"], 4)
            eng.wait_ge(S["h0_copied"], 1)
            abr, abi = wide(v(ABR), DB), wide(v(ABI), DB)
            rx = [at(rot, q * T, [[8, 16], [1, 8]]) for q in range(4)]
            for t in range(DT):
                if t == 0:
                    hr, hi = [h0T[:, c, :].rearrange("p (b j) -> p j b", j=16) for c in range(2)]
                else:
                    hr, hi = [Hs[:, c, :, :].rearrange("p j (b t) -> p j b t", t=DT)[:, :, :, t - 1] for c in range(2)]
                xr, xi = [bank(4 + c).rearrange("p (j b t) -> p j b t", b=DB, t=DT)[:, :, :, t] for c in range(2)]
                orr, oii = [Hs[:, c, :, :].rearrange("p j (b t) -> p j b t", t=DT)[:, :, :, t] for c in range(2)]
                tt(rx[0], hr, abr, ALU.mult)
                tt(rx[1], hi, abi, ALU.mult)
                tt(rx[2], hi, abr, ALU.mult)
                link(tt(rx[3], hr, abi, ALU.mult))
                tt(rx[0], rx[0], rx[1], ALU.subtract)
                link(tt(rx[2], rx[2], rx[3], ALU.add))
                tt(orr, rx[0], xr, ALU.add)
                ins = tt(oii, rx[2], xi, ALU.add)
                if t < DT - 1:
                    link(ins)
                else:
                    ins.then_inc(S["samples_done"], 1)
            eng.wait_ge(S["samples_done"], 1)
            for c in range(2):
                eng.tensor_copy(hfin_s[:, c, :].rearrange("p (b j) -> p b j", j=16),
                                Hs[:, c, :, :].rearrange("p j (b t) -> p b j t", t=DT)[:, :, :, DT - 1]).then_inc(S["fin_ready"], 1)
            eng.wait_ge(S["ys_done"], 1)
            for c in range(4):
                eng.scalar_tensor_tensor(zsu[:, c, T:TT], zsu[:, c, T:TT], vec[:, 36 + c:37 + c], bank(7)[:, c * NS:(c + 1) * NS], ALU.mult, ALU.add).then_inc(S["ys_taken"], 1)
            for j in range(16):
                e = [Et[:, j % 2, c, :] for c in range(2)]
                R = [rot[:, q, :] for q in range(6)]
                eng.wait_ge(S["E_ready"], j + 1)
                eng.wait_ge(S["x_done"], j + 1)
                xr, xi = bank(4), bank(5)
                tt(R[0], xr, e[0], ALU.mult)
                tt(R[1], xi, e[1], ALU.mult)
                tt(R[2], xi, e[0], ALU.mult)
                ins = tt(R[3], xr, e[1], ALU.mult)
                ins.then_inc(S["x_taken"], 1)
                eng.wait_ge(S["x_taken"], j + 1)
                tt(R[0], R[0], R[1], ALU.add)
                link(tt(R[2], R[2], R[3], ALU.subtract))
                decay = at(v(MAG), j, [[0, T]])
                eng.tensor_tensor_scan(R[1], decay, R[0], 0.0, ALU.mult, ALU.add)
                link(eng.tensor_tensor_scan(R[3], decay, R[2], 0.0, ALU.mult, ALU.add))
                tt(R[0], R[1], e[0], ALU.mult)
                tt(R[2], R[3], e[1], ALU.mult)
                tt(R[4], R[1], e[1], ALU.mult)
                ins = tt(R[5], R[3], e[0], ALU.mult)
                ins.then_inc(S["E_used"], 1)
                eng.wait_ge(S["E_used"], j + 1)
                if j >= 2:
                    eng.wait_ge(S["y_done"], j - 1)
                tt(Hp[:, j % 2, 0, :], R[0], R[2], ALU.subtract)
                tt(Hp[:, j % 2, 1, :], R[4], R[5], ALU.add).then_inc(S["h_ready"], 1)
                eng.wait_ge(S["h_ready"], j + 1)
                eng.tensor_copy(hfin[:, 0, j:j + 1], Hp[:, j % 2, 0, T - 1:T])
                ins = eng.tensor_copy(hfin[:, 1, j:j + 1], Hp[:, j % 2, 1, T - 1:T])
                if j == 15:
                    ins.then_inc(S["fin_ready"], 1)
                if j % 4 == 0 and j:
                    y_out(j // 4 - 1)
                if j == 0:
                    raw_copy(1)
                if j % 4 == 1 and j < 13:
                    raw_copy((j + 3) // 2)
                if j % 4 == 3 and j < 15:
                    raw_copy((j + 3) // 2)
                if j == 3:
                    xp_fill(1)
            y_out(3)
            eng.wait_ge(S["fin_turned"], 4)
            for q in range(4):
                n = 16 if q < 2 else P
                eng.tensor_copy(hout[0:n, q, :], bank(6)[0:n, q * P:(q + 1) * P]).then_inc(S["fin_copied"], 1)
            eng.wait_ge(*done(("glu", 3)))
            for m in range(4):
                eng.wait_ge(*out_of(("glu", m)))
                eng.tensor_tensor(zsu[:, m, :], zsu[:, m, :], glu_sig[:, m, :], ALU.mult).then_inc(S["glu_ready"], 1)
            eng.memset(ce[:, :, CB_P:32], 0.0).then_inc(S["fix_ready"], 1)
            eng.wait_ge(S["toep_in"], 16 * KV * P // SHIFTS)
            mx, sm = csum[:, 0:32], csum[:, 32:64]
            eng.wait_ge(S["cs_done"], 1)
            for i in range(TILES):
                c0 = 3 * P - P * i + 2 * CH - 1
                src = bank(6 + i // 2)[:, 248 * (i % 2):248 * (i % 2) + 248]
                ins = tt(cs[:, HEADS * i:HEADS * (i + 1), 0:CB_P], src.rearrange("p (a b) -> p a b", b=CB_P),
                         TZ[:, :, c0:c0 + CH * (CB_P - 1) + 1:CH], ALU.add)
            link(ins)
            link(eng.tensor_reduce(mx, cs[:, :, 0:CB_P], AX.X, ALU.max))
            link(eng.tensor_scalar(mx, mx, 0.1 * MASK, None, ALU.max))
            tt(cs[:, :, 0:CB_P], cs[:, :, 0:CB_P], wide(mx, CB_P), ALU.subtract).then_inc(S["cmax_done"], 1)
            eng.wait_ge(S["cexp_done"], 1)
            link(eng.tensor_reduce(sm, ce[:, :, 0:CB_P], AX.X, ALU.add))
            link(eng.tensor_scalar(sm, sm, 1e-30, None, ALU.max))
            link(eng.reciprocal(sm, sm))
            for i in range(TILES):
                by_head = sm[:, HEADS * i:HEADS * (i + 1)].rearrange("p (g k) -> p g k", k=KV)
                ins = tt(by_head, by_head, gates[:, i, :].rearrange("p (k g r) -> p g k r", k=KV, r=3)[:, :, :, 0], ALU.mult)
            link(ins)
            for half in range(2):
                hs = slice(16 * half, 16 * half + 16)
                tt(ce[:, hs, 0:CB_P], ce[:, hs, 0:CB_P], wide(sm[:, hs], CB_P), ALU.mult).then_inc(S["cnorm_done"], 1)
            eng.wait_ge(S["cpt_done"], 2)
            n = 0
            for i in range(TILES):
                W = P * (i + 1)
                for g in range(G):
                    for kv in range(KV):
                        for br in range(2):
                            q = 2 * (n % 2) + br
                            eng.wait_ge(S["s_done"], 2 * n + br + 1)
                            if n >= 2:
                                eng.wait_ge(S["exp_done"], 2 * (n - 2) + br + 1)
                            eng.tensor_tensor_reduce(Ssb[:, q, 0:W], bank(q)[:, 0:W], TZ[:, 2 * g + kv, (3 - i) * P:T], -0.125, 3e38,
                                                     ALU.add, ALU.min, small[:, 2 * (n % 3) + br:2 * (n % 3) + br + 1]).then_inc(S["s_taken"], 1)
                        if n:
                            diag(n - 1)
                        if n % 8 == 1 and n > 1:
                            eng.wait_ge(S["o_done"], n - 1)
                            take_o(i - 1)
                        n += 1
            diag(n - 1)
            eng.wait_ge(S["o_done"], 32)
            take_o(TILES - 1)
            eng.memset(Qb[:, :, :].rearrange("p a b -> p (a b)"), 0.0).then_inc(S["v_step"], 1)
            steps[0] += 1
            eng.wait_ge(S["v_step"], steps[0])
            for kv in range(KV):
                r = slice(64 * kv, 64 * kv + 64)
                eng.tensor_copy(Qb[r, :, 16 * kv:16 * kv + 16].rearrange("p b (g t) -> p b g t", t=DT),
                                zq[r, :, T:TT].rearrange("p g (b t) -> p b g t", t=DT)).then_inc(S["qb_ready"], 1)
            eng.wait_ge(S["biasS_in"], 64)
            eng.wait_ge(S["gate_in"], 16 * DB)
            link(eng.memset(cc[:, 2, CB_S:64], 0.0))
            IO = kc_[:, K_IO:K_IO + NSEL - 3]

            def sample_scores(tile):
                eng.wait_ge(S["sc_done"], tile + 1)
                eng.tensor_tensor_reduce(cc[:, 0, 0:CB_S], bank(6)[:, 0:CB_S], biasS[:, 2 * CH - 1:2 * CH - 1 + CH * (CB_S - 1) + 1:CH], -0.125, 3e38,
                                         ALU.add, ALU.min, small[:, 16:17]).then_inc(S["cmin_done"], 1)
                eng.wait_ge(S["cexps"], tile + 1)
                link(eng.tensor_scalar(small[:, 76:77], small[:, 17:18], 1e-30, None, ALU.max))
                link(eng.reciprocal(small[:, 76:77], small[:, 76:77]))
                link(eng.tensor_scalar(cc[:, 2, 0:CB_S], cc[:, 1, 0:CB_S], small[:, 76:77], None, ALU.mult))
                link(eng.tensor_reduce(small[:, 40:54], cc[:, 2, 4:60].rearrange("p (a b) -> p a b", b=4), AX.X, ALU.add))
                tt(small[:, 40:54], small[:, 40:54], cc[:, 2, 3:56:4], ALU.add).then_inc(S["impsum_ready"], 1)
                eng.tensor_scalar(cc[:, 0, 0:CB_S], cc[:, 2, 0:CB_S], gates_s[:, tile, 0:1], None, ALU.mult).then_inc(S["pc_ready"], 1)
                eng.wait_ge(S["imp_done"], tile + 1)
                eng.tensor_copy(small[:, 40:54], bank(6)[:, 64:78]).then_inc(S["bd_seen"], 1)
                eng.wait_ge(S["bd_seen"], tile + 1)
                link(eng.tensor_reduce(small[:, 72:73], small[:, 40:54], AX.X, ALU.min))
                link(eng.scalar_tensor_tensor(small[:, 56:70], small[:, 40:54], small[:, 72:73], IO, ALU.is_equal, ALU.mult))
                link(eng.tensor_reduce(small[:, 73:74], small[:, 56:70], AX.X, ALU.max))
                link(eng.tensor_scalar(small[:, 56:70], IO, small[:, 73:74], MASK, ALU.is_equal, ALU.mult))
                tt(bd[:, SEL:PAST - SEL].rearrange("p (a b) -> p a b", b=SEL), biasS[:, SEL:PAST - SEL].rearrange("p (a b) -> p a b", b=SEL),
                   wide(small[:, 56:70], SEL), ALU.add)
                eng.tensor_copy(bd[:, 0:SEL], biasS[:, 0:SEL])
                eng.tensor_copy(bd[:, PAST - SEL:PAST], biasS[:, PAST - SEL:PAST])
                own = kc_[:, K_SM + NS * tile:K_SM + NS * tile + NS].rearrange("p (b t) -> p b t", t=DT)
                tt(bd[:, PAST:PAST + NS].rearrange("p (b t) -> p b t", t=DT), wide(biasS[:, PAST:PAST + DT], DB, 1), own, ALU.add)
                tt(bw[:, WIN:WIN + NS].rearrange("p (b t) -> p b t", t=DT), wide(biasS[:, PAST:PAST + DT], DB, 1), own, ALU.add)
                eng.tensor_copy(bw[:, DT:WIN], biasS[:, PAST - WIN + DT:PAST])
                link(tt(bw[:, 0:DT], biasS[:, PAST - WIN:PAST - WIN + DT], kc_[:, K_WM:K_WM + DT], ALU.add))
                eng.wait_ge(S["pc_done"], tile + 1)
                eng.tensor_copy(PTS[0:CB_S, 14 + tile, :], bank(6)[0:CB_S, P:2 * P]).then_inc(S["pc_copied"], 1)
                eng.wait_ge(S["ss_done"], 4 * tile + 4)
                sel = pair[0][:, :, :].rearrange("p a b -> p (a b)")
                link(eng.tensor_tensor_reduce(SS[:, 0:PAST], sel, bd[:, 0:PAST], -0.125, 3e38, ALU.add, ALU.min, small[:, 77:78]))
                eng.tensor_tensor_reduce(SS[:, PAST:PAST + NS], bank(3)[:, 0:NS], bd[:, PAST:PAST + NS], -0.125, small[:, 77:78],
                                         ALU.add, ALU.min, small[:, 18:19]).then_inc(S["ss_taken"], 1)
                link(eng.tensor_tensor_reduce(SW[:, 0:WIN], bank(2), bw[:, 0:WIN], -0.125, 3e38, ALU.add, ALU.min, small[:, 78:79]))
                eng.tensor_tensor_reduce(SW[:, WIN:WIN + NS], bank(3)[:, NS:2 * NS], bw[:, WIN:WIN + NS], -0.125, small[:, 78:79],
                                         ALU.add, ALU.min, small[:, 19:20]).then_inc(S["ss_taken"], 1)

            def sample_sums(tile):
                eng.wait_ge(S["sexp"], 2 * tile + 2)
                if tile:
                    eng.wait_ge(S["tb_done"], 28)
                link(eng.tensor_scalar(small[:, 74:76], small[:, 20:22], 1e-30, None, ALU.max))
                link(eng.reciprocal(small[:, 74:76], small[:, 74:76]))
                for br in range(2):
                    eng.tensor_scalar(dgs[:, br, :], ident, small[:, 74 + br:75 + br], gates_s[:, tile, 1 + br:2 + br], ALU.mult, ALU.mult).then_inc(S["sdiag"], 1)

            def sample_out(tile):
                eng.wait_ge(S["so_done"], 4 * tile + 4)
                for kv in range(KV):
                    r = slice(64 * kv, 64 * kv + 64)
                    src = bank(7)[r, P * tile:P * tile + P].rearrange("p (b k g t) -> p b k g t", k=KV, g=G, t=DT)[:, :, kv, :, :]
                    dst = oT[r, :, T + 16 * tile:T + 16 * tile + 16].rearrange("p g (b t) -> p b g t", t=DT)
                    eng.tensor_copy(dst, src).then_inc(S["so_taken"], 1)

            sample_scores(0)
            sample_sums(0)
            sample_scores(1)
            sample_out(0)
            sample_sums(1)
            sample_out(1)
            for c in range(KC):
                for q, nm in enumerate(("att", "ssm")):
                    eng.wait_ge(*out_of((("mg0", "mg1")[q], c)))
                    eng.wait_ge(*done((nm, c)))
                    eng.tensor_tensor(halves(sig[:, 2 * (c % 2) + q, :]), halves(sig[:, 2 * (c % 2) + q, :]), both(pair_of[(nm, c)]), ALU.mult).then_inc(taken[pair_of[(nm, c)]], 1)
                eng.wait_ge(*out_of(("ssm", c)))
                tt(mT[:, c, :], sig[:, 2 * (c % 2), :], sig[:, 2 * (c % 2) + 1, :], ALU.add).then_inc(S["mixed"], 1)
                if c:
                    mix_low(c - 1)
            mix_low(KC - 1)
            eng.wait_ge(S["h_in"], 16)
            for c in range(KC):
                eng.wait_ge(*done(("wo", c)))
                eng.tensor_tensor(halves(hT[:, c, :]), halves(hT[:, c, :]), both(pair_of[("wo", c)]), ALU.add).then_inc(taken[pair_of[("wo", c)]], 1)
            normalise(1, hT, 8, rt, rs, u_hi)
            for c in range(FC):
                eng.wait_ge(*out_of(("gate", c)))
                eng.wait_ge(*done(("up", c)))
                eng.tensor_tensor(halves(mid[:, c, :]), halves(sil[:, c % 2, :]), both(pair_of[("up", c)]), ALU.mult).then_inc(taken[pair_of[("up", c)]], 1)
                if c:
                    mid_low(c - 1)
            mid_low(FC - 1)
            for c in range(KC):
                eng.wait_ge(*done(("down", c)))
                eng.tensor_tensor(halves(hT[:, c, :]), halves(hT[:, c, :]), both(pair_of[("down", c)]), ALU.add).then_inc(taken[pair_of[("down", c)]], 1)
            normalise(2, hT, 16, rt, rs, u_hi)
            for k in range(2):
                eng.wait_ge(*done(("pt", k)))
                eng.tensor_copy(pT[:, k, :], pair[pair_of[("pt", k)]][:, :, :].rearrange("p a b -> p (a b)")[:, 0:TT]).then_inc(taken[pair_of[("pt", k)]], 1)
            for c in range(KC):
                eng.wait_ge(*out_of(("pg", c)))
                eng.wait_ge(*done(("ple", c)))
                eng.tensor_tensor(halves(sig[:, c % 2, :]), halves(sig[:, c % 2, :]), both(pair_of[("ple", c)]), ALU.mult).then_inc(taken[pair_of[("ple", c)]], 1)
                eng.wait_ge(*out_of(("ple", c)))
                tt(hT[:, c, :], hT[:, c, :], sig[:, c % 2, :], ALU.add).then_inc(S["h_new"], 1)
            normalise(3, hT, 24, rt, rs)
            for t in range(5):
                n = P if t < 4 else NS
                eng.wait_ge(S["y_turned"], 2 * t + 1)
                if t >= 2:
                    eng.wait_ge(y_stored[t % 2], 16 * (t // 2))
                eng.tensor_copy(ytok[0:n, t % 2, 0:512], bank(2 * (t % 2))[0:n, :]).then_inc(S["y_copied_v"], 1)

        @block.tensor
        def _(eng):
            rhs_of = {"z": uT, "ng": uT, "mg0": uT, "mg1": uT, "glu": zsu, "att": oT, "ssm": zsu, "wo": mT,
                      "gate": uT, "up": uT, "down": mid, "pg": uT, "ple": pT}
            step_of = dict(groups)
            steps_p = [0]

            def link(ins):
                steps_p[0] += 1
                ins.then_inc(S["p_step"], 1)
                eng.wait_ge(S["p_step"], steps_p[0])

            def gemm(name, ready=None):
                pr, use = pair_of[name], use_of[name]
                if use > 1:
                    eng.wait_ge(taken[pr], use - 1)
                steps = step_of[name]
                src = rhs_of[name[0]]
                seen = set()
                for n, (w, off, m, k) in enumerate(steps):
                    if w is None:
                        lhsT = wple[:, off:off + m]
                    else:
                        if w not in seen:
                            if w in split_index:
                                eng.wait_ge(S["slab_split"], split_index[w] + 1)
                            else:
                                eng.wait_ge(slab_landed[w % RING], landed_at[w])
                            seen.add(w)
                        lhsT = ring[:, w % RING, off:off + m]
                    if ready:
                        eng.wait_ge(*ready(k))
                    if w in split_index:
                        w_hi = ring_r[:, RING + split_index[w] % HI_RING, off:off + m]
                        w_lo = ring_r[:, w % RING, off:off + m]
                        x_hi, x_lo = parts_of(name)
                        for h in range(2):
                            out, cols = pair[pr][0:m, h, 0:HT], slice(h * HT, (h + 1) * HT)
                            eng.matmul(out, w_hi, x_hi(k)[:, cols], start=n == 0, stop=False)
                            eng.matmul(out, w_hi, x_lo(k)[:, cols], start=False, stop=False)
                            ins = eng.matmul(out, w_lo, x_hi(k)[:, cols], start=False, stop=n == len(steps) - 1)
                        if n < len(steps) - 1 and steps[n + 1][0] != w:
                            ins.then_inc(S["part_done"], 1)
                        continue
                    for h in range(2):
                        ins = eng.matmul(pair[pr][0:m, h, 0:HT], lhsT, src[:, k, h * HT:(h + 1) * HT], start=n == 0, stop=n == len(steps) - 1)
                ins.then_inc(sum_done[pr], 1)

            def parts_of(name):
                kind = name[0]
                if kind == "wo":
                    return (lambda k: mT_hi[:, k, :]), (lambda k: mT_lo[:, k, :])
                if kind == "down":
                    return (lambda k: mid_hi[k]), (lambda k: mid_lo[:, k, :])
                hi = u_hi0 if kind in ("z", "ng") else u_hi_mix if kind in ("mg0", "mg1") else u_hi
                return (lambda k: hi[:, k, :]), (lambda k: uT_r[:, k, :])

            def norm(n):
                pr, use = pair_of[("norm", n)], use_of[("norm", n)]
                if use > 1:
                    eng.wait_ge(taken[pr], use - 1)
                for k in range(KC):
                    eng.wait_ge(S["squares"], KC * n + k + 1)
                    for h in range(2):
                        ins = eng.matmul(pair[pr][:, h, 0:HT], ones, uT[:, k, h * HT:(h + 1) * HT], start=k == 0, stop=k == KC - 1)
                ins.then_inc(sum_done[pr], 1)

            normed = lambda n: lambda k: (S["normed"], KC * n + k + 1)

            def ssm_maps():
                eng.wait_ge(S["bd_ready"], 4)
                for q, src in enumerate((bdr, bdi)):
                    for k in range(4):
                        ins = eng.transpose(bank(4 + q)[:, k * P:(k + 1) * P], src[:, 4 * k:4 * k + 4, :].rearrange("p a b -> p (a b)"), ident)
                    ins.then_inc(S["bd_turned"], 1)
                eng.wait_ge(S["ssm_in"], 16 * 8)
                for q in range(2):
                    for k in range(4):
                        ins = eng.transpose(bank(6 + q)[:, k * P:(k + 1) * P], cnat[:, q, k, :], ident)
                    ins.then_inc(S["c_turned"], 1)
                eng.wait_ge(S["bd_copied"], 1)
                for q in range(2):
                    ins = eng.transpose(bank(4)[:, q * P:(q + 1) * P], h0nat[:, q, :], ident)
                ins.then_inc(S["h0_turned"], 1)

            eng.wait_ge(S["const_in"], 16)
            eng.wait_ge(S["nat_in"], 16 * 10)
            eng.transpose(bank(2)[:, 0:104], nat[0:104, :], ident[0:104, 0:104]).then_inc(S["vec_turned"], 1)
            eng.wait_ge(S["spread_ready"], 3)
            for q, rows in enumerate((8, 4, 16)):
                ins = eng.transpose(bank(3)[:, 16 * q:16 * q + rows], spread[0:rows, q, :], ident[0:rows, 0:rows])
            ins.then_inc(S["spread_turned"], 1)
            eng.wait_ge(S["x0"], 16 * 5)
            for q in range(10):
                t, kk = q // 2, q % 2
                n = P if t < 4 else NS
                if q >= 2:
                    eng.wait_ge(S["copied_x"], q - 1)
                for c in range(4):
                    k = 4 * kk + c
                    ins = eng.transpose(bank(q % 2)[:, c * P:c * P + n], xtok[0:n, t, k * P:(k + 1) * P], ident[0:n, 0:n])
                ins.then_inc(S["turned_x"], 1)
            eng.wait_ge(S["hot_in"], 32)
            eng.wait_ge(S["ones_set"], 3)
            n = LINE // 4
            for q in range(4):
                eng.matmul(bank(4 + q)[0:HEADS, 0:n], relb, hot[:, q * n:(q + 1) * n], start=True, stop=True).then_inc(S["line_done"], 1)
            eng.wait_ge(S["copied_x"], 10)
            norm(0)
            eng.wait_ge(S["vec_copied"], 1)
            for m in range(14):
                if m == 1:
                    eng.wait_ge(S["line_copied"], 4)
                gemm(("z", m), normed(0) if m == 0 else None)
            gemm(("ng", 0))
            for t in range(5):
                n = P if t < 4 else NS
                if t == 0:
                    for m in range(10, 14):
                        eng.wait_ge(*out_of(("z", m)))
                    eng.wait_ge(*out_of(("ng", 0)))
                if t >= 2:
                    eng.wait_ge(S["tokst_copied"], t - 1)
                    eng.wait_ge(S["vtok_copied"], t - 1)
                for q, slot in enumerate((0, 1, KS, KW)):
                    ins = eng.transpose(bank(2 * (t % 2))[0:n, q * P:(q + 1) * P], zkv[:, slot, t * P:t * P + n], ident)
                ins.then_inc(S["kvt_done"], 1)
                for q, slot in enumerate((2, 3)):
                    ins = eng.transpose(bank(2 * (t % 2) + 1)[0:n, q * P:(q + 1) * P], zkv[:, slot, t * P:t * P + n], ident)
                ins.then_inc(S["kvt_done"], 1)
                if t == 0:
                    ssm_maps()
            eng.wait_ge(S["bd_copied"], 2)
            for t in range(TILES):
                eng.transpose(bank(5)[:, 32 * t:32 * t + 24], zng[:, t * P:(t + 1) * P], ident[0:24, 0:24])
            ins = eng.transpose(bank(5)[0:NS, 32 * TILES:32 * TILES + 24], zng[:, T:TT], ident[0:24, 0:24])
            ins.then_inc(S["gates_turned"], 1)
            eng.wait_ge(S["h0_copied"], 1)
            eng.wait_ge(S["gates_copied"], TILES + 1)
            for rg in range(4):
                r = slice(32 * rg, 32 * rg + 32)
                for c in range(2):
                    for j in range(rg, 16, 4):
                        ins = eng.matmul(bank(4 + c)[:, j * NS:(j + 1) * NS], BT[r, c, j // 4, :], zsu[r, j // 4, T:TT], start=True, stop=True)
                ins.then_inc(S["xs_done"], 1)
                if rg < 3:
                    eng.wait_ge(S["xs_done"], rg + 1)
            eng.wait_ge(S["samples_done"], 1)
            eng.wait_ge(S["c_copied"], 4)
            for cg in range(4):
                for j in range(cg, 16, 4):
                    for c in range(2):
                        ins = eng.matmul(bank(7)[32 * cg:32 * cg + 32, NS * (j // 4):NS * (j // 4) + NS], CT[:, c, j, :], Hs[:, c, j, :], start=c == 0, stop=c == 1)
            ins.then_inc(S["ys_done"], 1)
            turn = hid = c2 = 0

            def x_in(j):
                if j:
                    eng.wait_ge(S["x_taken"], j)
                r = slice(32 * (j % 4), 32 * (j % 4) + 32)
                for c in range(2):
                    ins = eng.matmul(bank(4 + c), BT[r, c, j // 4, :], zsu[r, j // 4, 0:T], start=True, stop=True)
                ins.then_inc(S["x_done"], 1)

            def y_sum(j):
                eng.wait_ge(S["h_ready"], j + 1)
                if j >= 4 and j % 4 == 0:
                    eng.wait_ge(S["y_taken"], j // 4)
                for c in range(2):
                    ins = eng.matmul(bank(6)[32 * (j % 4):32 * (j % 4) + 32, :], CT[:, c, j, :], Hp[:, j % 2, c, :], start=c == 0, stop=c == 1)
                ins.then_inc(S["y_done"], 1)

            def turns():
                nonlocal turn
                eng.wait_ge(S["raw_copied"], turn // 4 + 1)
                for q in range(4):
                    ckv, ph = q // 2, q % 2
                    if turn >= 2:
                        eng.wait_ge(S["turn_copied"], turn - 1)
                    for c in range(4):
                        col = (4 * ph + c) * 256 + ckv * P
                        ins = eng.transpose(bank(2 + turn % 2)[:, c * P:(c + 1) * P], raw2[:, col:col + P], ident)
                    ins.then_inc(S["raw_turned"], 1)
                    turn += 1

            def hidden(h, half, batch):
                nonlocal hid
                if half == 0 and hid >= 2:
                    eng.wait_ge(S["hid_taken"], hid - 1)
                if half == 0 and h == 0:
                    eng.wait_ge(S["turn_copied"], 8 * (batch + 1))
                out = bank(hid % 2)[:, 0:504].rearrange("p (k b c) -> p k b c", k=KV, c=CB_S)
                for q in range(8):
                    rhs = XT[:, q, :, :].rearrange("p k (b c) -> p k b c", c=64)[:, :, :, half:half + CB_S]
                    ins = eng.matmul(out, w1[:, 8 * half + q, h * P:(h + 1) * P], rhs, start=half == 0 and q == 0, stop=half == 1 and q == 7)
                if half:
                    ins.then_inc(S["hid_done"], 1)
                    hid += 1

            def second(kv):
                nonlocal c2
                eng.wait_ge(S["hid_taken"], hid)
                if c2:
                    eng.wait_ge(S["c2_taken"], c2)
                if c2 % 3 == 0:
                    for quad in range(2 if kv == 0 else 4):
                        for h in range(2):
                            k = quad % 2
                            x = Hq[:, h, CB_P * k:CB_P * (k + 1)]
                            if kv == 0:
                                ins = eng.matmul(bank(7)[64 * k:64 * k + 64, 0:CB_P], w2[:, 0, h, :], x, start=h == 0, stop=h == 1)
                            else:
                                ins = eng.matmul(bank(7)[32 * quad:32 * quad + CB_P, 0:HD], x, w2[:, 1, h, :], start=h == 0, stop=h == 1)
                elif kv == 0:
                    for k in range(KV):
                        for h in range(2):
                            ins = eng.matmul(bank(7)[64 * k:64 * k + 64, 0:252], w2[:, 0, h, :], Hh[:, h, 252 * k:252 * k + 252], start=h == 0, stop=h == 1)
                else:
                    for b in range(4):
                        for k in range(KV):
                            for h in range(2):
                                x = Hh[:, h, 252 * k + CB_S * b:252 * k + CB_S * (b + 1)]
                                ins = eng.matmul(bank(7)[0:CB_S, P * b + HD * k:P * b + HD * (k + 1)], x, w2[:, 1, h, :], start=h == 0, stop=h == 1)
                ins.then_inc(S["c2_done"], 1)
                c2 += 1

            def prompt_hidden(kv):
                nonlocal hid
                eng.wait_ge(S["w1_in"], 16 * (kv + 1))
                eng.wait_ge(S["xp_ready"], kv + 1)
                for h in range(2):
                    if hid >= 2:
                        eng.wait_ge(S["hid_taken"], hid - 1)
                    for q in range(16):
                        ins = eng.matmul(bank(hid % 2)[:, 0:63], w1[:, q, h * P:(h + 1) * P], XP[:, q, 0:63], start=q == 0, stop=q == 15)
                    ins.then_inc(S["hid_done"], 1)
                    hid += 1
                eng.wait_ge(S["w2_in"], 32)
                second(kv)

            eng.wait_ge(S["ys_taken"], 4)
            eng.wait_ge(S["tokst_copied"], 5)
            eng.wait_ge(S["vtok_copied"], 5)
            for j in range(16):
                if j:
                    y_sum(j - 1)
                x_in(j)
                batch = j // 4
                if j % 4 == 0:
                    if batch % 2 == 0:
                        prompt_hidden(batch // 2)
                    turns()
                    turns()
                hidden(j // 2 % 2, j % 2, batch)
                if j % 4 == 3:
                    second(batch // 2)
            y_sum(15)
            eng.wait_ge(S["fin_ready"], 3)
            eng.wait_ge(S["y_taken"], 4)
            for q in range(2):
                eng.transpose(bank(6)[0:16, q * P:(q + 1) * P], hfin[:, q, :], ident).then_inc(S["fin_turned"], 1)
            for q in range(2):
                eng.transpose(bank(6)[:, (2 + q) * P:(3 + q) * P], hfin_s[:, q, :], ident).then_inc(S["fin_turned"], 1)
            eng.wait_ge(S["hid_taken"], 12)
            eng.wait_ge(S["fin_copied"], 4)
            eng.wait_ge(S["c2_taken"], 6)
            eng.wait_ge(S["x_taken"], 16)
            for m in range(4):
                gemm(("glu", m), (lambda k: (S["z_ready"], k + 1)) if m == 0 else None)
            for m in range(4):
                eng.wait_ge(*out_of(("glu", m)))
            for k in range(KV):
                if k:
                    link(ins)
                for i in range(TILES):
                    for g in range(G):
                        h = KV * g + k
                        r = slice(64 * k, 64 * k + 64)
                        c0 = 248 * (i % 2) + h * CB_P
                        ins = eng.matmul(bank(6 + i // 2)[:, c0:c0 + CB_P], zq[r, g, i * P:(i + 1) * P], kcT_p[r, 0:CB_P], start=True, stop=True)
            ins.then_inc(S["cs_done"], 1)
            eng.wait_ge(S["fix_ready"], 1)
            for half in range(2):
                eng.wait_ge(S["cnorm_done"], half + 1)
                for q in range(4):
                    h0 = 16 * half + 4 * q
                    ins = eng.transpose(bank(4 + half)[:, q * P:(q + 1) * P], ce[:, h0:h0 + 4, :].rearrange("p a b -> p (a b)"), ident)
                ins.then_inc(S["cpt_done"], 1)

            def scores(n):
                i, h = n // 8, n % 8
                g, k, W = h // KV, h % KV, P * (i + 1)
                r = slice(64 * k, 64 * k + 64)
                for br in range(2):
                    if n >= 2:
                        eng.wait_ge(S["s_taken"], 2 * (n - 2) + br + 1)
                    eng.matmul(bank(2 * (n % 2) + br)[:, 0:W], zq[r, g, i * P:(i + 1) * P], zkv[r, (KS, KW)[br], 0:W], start=True, stop=True).then_inc(S["s_done"], 1)

            def turn_probs(n):
                i = n // 8
                for br in range(2):
                    q = 2 * (n % 3) + br
                    eng.wait_ge(S["diag_ready"], 2 * n + br + 1)
                    if n:
                        eng.wait_ge(S["pt_copied"], 2 * (n - 1) + br + 1)
                    for c in range(i + 1):
                        ins = eng.matmul(bank(4 + br)[:, c * P:(c + 1) * P], Psb[q][:, c * P:(c + 1) * P], dg[q], start=True, stop=True)
                    ins.then_inc(S["pt_done"], 1)

            def values(n):
                i, h = n // 8, n % 8
                g, k = h // KV, h % KV
                if n % 8 == 0 and i:
                    eng.wait_ge(S["o_taken"], i)
                out = bank(6)[64 * k:64 * k + 64, g * P:(g + 1) * P]
                quad = (g % 2) * 2 + k
                r = slice(32 * quad, 32 * quad + CB_P)
                eng.wait_ge(S["cpt_copied"], 2)
                if n >= 2:
                    eng.wait_ge(S["o_done"], n - 1)
                eng.matmul(out, vc_p[r, :], PTc[r, i, g // 2, :], start=True, stop=False)
                eng.wait_ge(S["pt_copied"], 2 * n + 2)
                for br in range(2):
                    for c in range(i + 1):
                        last = br == 1 and c == i
                        ins = eng.matmul(out, vtok[:, c, br, 64 * k:64 * k + 64], PTs[:, 2 * (n % 2) + br, c * P:(c + 1) * P], start=False, stop=last)
                ins.then_inc(S["o_done"], 1)

            scores(0)
            scores(1)
            for n in range(32):
                if n + 2 < 32:
                    scores(n + 2)
                turn_probs(n)
                if n:
                    values(n - 1)
            values(31)
            tb = 0

            def tb_bank():
                if tb >= 2:
                    eng.wait_ge(S["tb_copied"], tb - 1)
                return bank(4 + tb % 2)

            eng.wait_ge(S["qb_ready"], 2)
            eng.wait_ge(S["pt_copied"], 64)
            eng.wait_ge(S["o_taken"], 4)

            def keys(tile):
                nonlocal tb
                if tile:
                    eng.wait_ge(S["pc_copied"], tile)
                for b in range(4):
                    ins = eng.matmul(bank(6)[32 * b:32 * b + 32, 0:CB_S], Qb[:, 4 * tile + b, :], kcT_s[:, tile, CB_S * b:CB_S * (b + 1)], start=True, stop=True)
                ins.then_inc(S["sc_done"], 1)
                eng.wait_ge(S["kwin_in"], 16 * (tile + 1))
                for b in range(4 * tile, 4 * tile + 4):
                    eng.wait_ge(ksel_in[b % 2], 16 * (b // 2 + 1))
                    for j0 in (0, 4):
                        bk = tb_bank()
                        for c in range(4):
                            ins = eng.transpose(bk[:, c * P:(c + 1) * P], ksel[:, b % 2, (j0 + c) * P:(j0 + c + 1) * P], ident)
                        ins.then_inc(S["tb_done"], 1)
                        tb += 1
                    bk = tb_bank()
                    for c in range(4):
                        ins = eng.transpose(bk[:, c * P:(c + 1) * P], kwin[:, b % 4, c * P:(c + 1) * P], ident)
                    ins.then_inc(S["tb_done"], 1)
                    tb += 1
                    eng.wait_ge(S["tb_copied"], tb)
                    if tile and b == 4:
                        eng.wait_ge(S["ss_taken"], 2)
                    r = slice(32 * (b % 4), 32 * (b % 4) + 32)
                    q = Qb[:, b, :]
                    eng.matmul(bank(0)[r, :], q, KT[:, b % 2, 0:512], start=True, stop=True)
                    eng.matmul(bank(1)[r, :], q, KT[:, b % 2, 512:1024], start=True, stop=True)
                    eng.matmul(bank(2)[r, :], q, KTw[:, b % 2, :], start=True, stop=True)
                    eng.matmul(bank(3)[r, 0:NS], q, zkv[:, KS, T:TT], start=True, stop=True)
                    eng.matmul(bank(3)[r, NS:2 * NS], q, zkv[:, KW, T:TT], start=True, stop=True).then_inc(S["ss_done"], 1)
                    if b % 4 == 0:
                        eng.wait_ge(S["impsum_ready"], tile + 1)
                        eng.matmul(bank(6)[:, 64:78], kc_[:, K_G:K_G + P], small[:, 40:54], start=True, stop=True).then_inc(S["imp_done"], 1)
                    if b % 4 == 1:
                        eng.wait_ge(S["pc_ready"], tile + 1)
                        eng.wait_ge(S["bd_seen"], tile + 1)
                        eng.transpose(bank(6)[0:CB_S, P:2 * P], cc[:, 0, 0:CB_S], ident).then_inc(S["pc_done"], 1)

            def outputs(tile):
                nonlocal tb
                eng.wait_ge(S["sdiag"], 2 * tile + 2)
                for j0 in (0, 4):
                    bk = tb_bank()
                    for c in range(4):
                        ins = eng.matmul(bk[:, c * P:(c + 1) * P], PS_[:, j0 + c:j0 + c + 8 * (P - 1) + 1:8], dgs[:, 0, :], start=True, stop=True)
                    ins.then_inc(S["tb_done"], 1)
                    tb += 1
                bk = tb_bank()
                for c in range(4):
                    ins = eng.matmul(bk[:, c * P:(c + 1) * P], PW[:, c:c + 4 * (P - 1) + 1:4], dgs[:, 1, :], start=True, stop=True)
                ins.then_inc(S["tb_done"], 1)
                tb += 1
                bk = tb_bank()
                eng.matmul(bk[0:NS, 0:P], PS_[:, PAST:PAST + NS], dgs[:, 0, :], start=True, stop=True)
                eng.matmul(bk[0:NS, P:2 * P], PW[:, WIN:WIN + NS], dgs[:, 1, :], start=True, stop=True).then_inc(S["tb_done"], 1)
                tb += 1
                eng.wait_ge(S["tb_copied"], tb)
                eng.wait_ge(S["pc_copied"], tile + 1)
                eng.wait_ge(S["vwin_in"], 16 * (tile + 1))
                if tile:
                    eng.wait_ge(S["so_taken"], 2)
                for b in range(4 * tile, 4 * tile + 4):
                    bl = b % 4
                    c = slice(32 * bl, 32 * bl + 32)
                    out = bank(7)[:, 32 * b:32 * b + 32]
                    eng.wait_ge(vsel_in[b % 4], 16 * (b // 4 + 1))
                    eng.matmul(out, vc_s[0:CB_S, b, :], PTS[0:CB_S, 14 + tile, c], start=True, stop=False)
                    for j in range(8):
                        eng.matmul(out, vsel[:, bl, j * P:(j + 1) * P], PTS[:, j, c], start=False, stop=False)
                    for j in range(4):
                        eng.matmul(out, vwin[:, bl, j * P:(j + 1) * P], PTS[:, 9 + j, c], start=False, stop=False)
                    eng.matmul(out, vtok[0:NS, 4, 0, :], PTS[0:NS, 8, c], start=False, stop=False)
                    eng.matmul(out, vtok[0:NS, 4, 1, :], PTS[0:NS, 13, c], start=False, stop=True).then_inc(S["so_done"], 1)

            keys(0)
            keys(1)
            outputs(0)
            outputs(1)
            eng.wait_ge(S["so_taken"], 4)
            eng.wait_ge(S["glu_ready"], 4)
            for c in range(KC):
                for nm in ("mg0", "mg1", "att", "ssm"):
                    gemm((nm, c), (lambda k: (S["u_returned"], k + 1)) if (nm, c) == ("mg0", 0) else None)
            for c in range(KC):
                gemm(("wo", c), (lambda k: (S["mix_split"], k + 1)) if c == 0 else None)
            norm(1)
            for c in range(FC):
                gemm(("gate", c), normed(1) if c == 0 else None)
                gemm(("up", c))
            for c in range(KC):
                gemm(("down", c), (lambda k: (S["mid_split"], k + 1)) if c == 0 else None)
            norm(2)
            eng.wait_ge(S["p_in"], 32)
            for k in range(2):
                pr, use = pair_of[("pt", k)], use_of[("pt", k)]
                eng.wait_ge(taken[pr], use - 1)
                flat = pair[pr][:, :, :].rearrange("p a b -> p (a b)")
                for t in range(5):
                    n = P if t < 4 else NS
                    ins = eng.transpose(flat[:, t * P:t * P + n], ptok[0:n, t, k * P:(k + 1) * P], ident[0:n, 0:n])
                ins.then_inc(sum_done[pr], 1)
            eng.wait_ge(S["wple_in"], 16)
            for c in range(KC):
                gemm(("pg", c), normed(2) if c == 0 else None)
                if c == 0:
                    for k in range(2):
                        eng.wait_ge(*out_of(("pt", k)))
                gemm(("ple", c))
            norm(3)
            eng.wait_ge(*out_of(("norm", 3)))
            eng.wait_ge(*out_of(("ple", KC - 1)))
            for t in range(5):
                n = P if t < 4 else NS
                if t == 0:
                    eng.wait_ge(S["u_new"], 4 * KC)
                for half in range(2):
                    if t >= 2:
                        eng.wait_ge(S["y_copied_a" if half else "y_copied_v"], t - 1)
                    for c in range(4):
                        ins = eng.transpose(bank(2 * (t % 2) + half)[0:n, c * P:(c + 1) * P], uT[:, 4 * half + c, t * P:t * P + n], ident)
                    ins.then_inc(S["y_turned"], 1)


_INS = """x_prompt x_sample cache_k_cmp cache_v_cmp cache_k_sel cache_v_sel cache_k_win cache_v_win state_ssm_re state_ssm_im
page_table p_prompt p_sample rel_bias final_norm attn_norm w_in cmp_pe_k cmp_w1_k cmp_w2_k cmp_pe_v cmp_w1_v cmp_w2_v ssm_a_re
ssm_a_im ssm_log_dt ssm_b_re ssm_b_im ssm_c_re ssm_c_im ssm_d w_glu b_glu w_att_br w_ssm_br w_o ffn_norm w_ffn_gate w_ffn_up
w_ffn_down ple_norm w_ple_gate w_ple""".split()
_KVP, _KVS, _WINS = (1, 1, T, KV, HD), (1, DB, DT, KV, HD), (1, DB, WIN, KV, HD)
_OUTS = [("y_prompt", (1, T, D)), ("y_sample", (DB, DT, D)),
         ("nk_cmp_p", _KVP), ("nv_cmp_p", _KVP), ("nk_sel_p", _KVP), ("nv_sel_p", _KVP), ("nk_win_p", _KVP), ("nv_win_p", _KVP),
         ("ns_re_p", (1, 1, SG, SP_)), ("ns_im_p", (1, 1, SG, SP_)),
         ("nk_cmp_s", _KVS), ("nv_cmp_s", _KVS), ("nk_sel_s", _KVS), ("nv_sel_s", _KVS), ("nk_win_s", _WINS), ("nv_win_s", _WINS),
         ("ns_re_s", (1, DB, SG, SP_)), ("ns_im_s", (1, DB, SG, SP_))]


def kernel(**inputs):
    import concourse.bacc as bacc
    from concourse.bass_utils import run_bass_kernel_spmd

    nc = bacc.Bacc("TRN2", target_bir_lowering=False, num_devices=1)
    arrays = {n: np.ascontiguousarray(inputs[n]) for n in _INS}
    arrays["consts"] = constants()
    arrays["buckets"] = bucket_table()
    a = {n: nc.dram_tensor("in_" + n, v.shape, mybir.dt.from_np(v.dtype), kind="ExternalInput").ap() for n, v in arrays.items()}
    for n, shape in _OUTS:
        a[n] = nc.dram_tensor("out_" + n, shape, F32, kind="ExternalOutput").ap()
    build(nc, a)
    r = run_bass_kernel_spmd(nc, [{"in_" + n: v for n, v in arrays.items()}], core_ids=[0])
    return tuple(r.results[0]["out_" + n] for n, _ in _OUTS)
```

```python
import math
from contextlib import ExitStack

import numpy as np

import concourse.bass as bass
from concourse import mybir

F32 = mybir.dt.float32
F32R = mybir.dt.float32r
I32 = mybir.dt.int32
U32 = mybir.dt.uint32
ALU = mybir.AluOpType
ACT = mybir.ActivationFunctionType
AX = mybir.AxisListType

P = 128
D = 1024
T = 512
DB, DT = 8, 4
NS = DB * DT
TT = T + NS
HT = TT // 2
PAST = 1024
PAGE = 128
NPAGES = PAST // PAGE
HEADS, KV, HD = 8, 2, 64
G = HEADS // KV
WIN = 512
SEL = 64
NSEL = PAST // SEL + 1
CH = 16
CB_P = T // CH - 1
CB_S = PAST // CH - 1
HID = 256
SG, SC, SP_ = 32, 16, 64
FF = 2816
PLE = 256
NBUCKET = 32
KC = D // P
FC = FF // P
EPS = 1e-6
MASK = -1e30
TILES = T // P
DMAX = PAST + DT - 1
TW = 912
TBASE = DMAX - 3 * P
LINE = TBASE + TW + 1
SHIFTS = 16
LPITCH = LINE + SHIFTS
SLAB = 1024
RING = 5
HI_RING = 3
C_Q, C_KV, C_NG, C_SU, C_MG = 0, 512, 1280, 1304, 1816
W_IN = C_MG + 2 * D
MAGIC = 12582912.0
TWO_PI = 2.0 * math.pi
TP_HI = float(np.float32(6.28125))
TP_LO = float(np.float32(TWO_PI - 6.28125))
K_ID, K_G, K_SM, K_WM, K_IO, K_MOD = 0, 128, 256, 320, 324, 338
K_N = 340


def bucket_table():
    n = np.arange(LINE)
    dist = DMAX - n
    d = np.maximum(dist, 0)
    exact = NBUCKET // 2
    nf = np.maximum(d, 1).astype(np.float32)
    large = exact + (np.log(nf / np.float32(exact)) / np.float32(math.log(128 / exact)) * np.float32(NBUCKET - exact)).astype(np.int32)
    b = np.where(d < exact, d, np.minimum(large, NBUCKET - 1))
    out = np.zeros((NBUCKET + 1, LINE), np.float32)
    out[b[dist >= 0], n[dist >= 0]] = 8.0
    out[NBUCKET, dist < 0] = MASK
    return out


def constants():
    c = np.zeros((P, K_N), np.float32)
    r = np.arange(P)
    c[:, K_ID:K_ID + P] = np.eye(P)
    b, kv, g, t = r // 32, r // 16 % 2, r // 4 % 4, r % 4
    same = (b[:, None] == b) & (kv[:, None] == kv) & (t[:, None] == t)
    c[:, K_G:K_G + P] = same
    for tile in range(2):
        for col in range(NS):
            c[:, K_SM + tile * NS + col] = np.where(4 * tile + b == col // DT, 0.0, MASK)
    for u in range(DT):
        c[:, K_WM + u] = np.where(u <= t, MASK, 0.0)
    c[:, K_IO:K_IO + NSEL - 3] = np.arange(1, NSEL - 2)
    c[:, K_MOD] = r % 16
    c[:, K_MOD + 1] = r % 8
    return c


def at(ap, offset, dims):
    return bass.AP(ap.tensor, ap.offset + offset, [list(ap.ap[0])] + dims)


def wide(ap, n, axis=None):
    dims = [list(x) for x in ap.ap]
    dims.insert(len(dims) if axis is None else axis, [0, n])
    return bass.AP(ap.tensor, ap.offset, dims)


Z_BLOCK = [10, 11, 12, 13] + list(range(10))


def plan_gemms():
    groups, slabs = [], []

    def slab(kind, n, split=True):
        slabs.append((kind, n, split))
        return len(slabs) - 1

    def group(name, steps):
        groups.append((name, steps))

    def plain_steps(w, count, k0=0, m=P):
        return [(w, k * m, m, k0 + k) for k in range(count)]

    for m in range(14):
        group(("z", m), plain_steps(slab("z", m), KC))
        if m == 0:
            group(("norm", 0), None)
    group(("ng", 0), plain_steps(slab("ng", 0), KC, m=24))
    for s in range(2):
        w = slab("glu", s, False)
        for m in range(2):
            group(("glu", 2 * s + m), [(w, k * 256 + m * P, P, k) for k in range(4)])
    for c in range(KC):
        for kind in ("mg0", "mg1"):
            group((kind, c), plain_steps(slab(kind, c), KC))
        w = slab("att", c)
        group(("att", c), plain_steps(w, 4))
        group(("ssm", c), [(w, 512 + k * P, P, k) for k in range(4)])
    for c in range(KC):
        group(("wo", c), plain_steps(slab("wo", c), KC))
    for c in range(FC):
        for kind in ("gate", "up"):
            group((kind, c), plain_steps(slab(kind, c), KC))
            if (kind, c) == ("gate", 0):
                group(("norm", 1), None)
    for m in range(KC):
        steps = []
        for part in range(3):
            k0 = KC * part
            steps += plain_steps(slab("down", 3 * m + part), min(KC, FC - k0), k0)
        group(("down", m), steps)
    for k in range(2):
        group(("pt", k), None)
    for c in range(KC):
        group(("pg", c), plain_steps(slab("pg", c), KC))
        if c == 0:
            group(("norm", 2), None)
        group(("ple", c), [(None, k * D + c * P, P, k) for k in range(2)])
    return groups, slabs


def build(nc, a):
    groups, slabs = plan_gemms()
    pair_of, use_of, count = {}, {}, [0] * 4
    last_use = {}
    landed_at, total = [], [0] * RING
    split_index = {}
    for n, (kind, m, split) in enumerate(slabs):
        total[n % RING] += 16 * (3 if kind == "att" else 2 if kind == "z" and Z_BLOCK[m] < 4 else 1)
        if split:
            split_index[n] = len(split_index)
        landed_at.append(total[n % RING])
    split_slab = list(split_index)
    for n, (name, steps) in enumerate(groups):
        pair = n % 2 if name[0] == "ng" or name[0] == "z" and name[1] >= 4 else name[1] % 3 if name[0] == "glu" else n % 4
        count[pair] += 1
        pair_of[name], use_of[name] = pair, count[pair]
        for st in steps or []:
            if st[0] is not None:
                last_use[st[0]] = name

    bias_line = nc.dram_tensor("bias_line", (HEADS, SHIFTS, LPITCH), F32, kind="Internal").ap()
    gate_rows = nc.dram_tensor("gate_rows", (NS, 24), F32, kind="Internal").ap()
    u_spill = nc.dram_tensor("u_spill", (P, KC * TT), F32, kind="Internal").ap()
    h_spill = nc.dram_tensor("h_spill", (P, KC * TT), F32, kind="Internal").ap()

    AR = 28400
    with ExitStack() as ctx:
        def sb(name, shape, dt=F32):
            return ctx.enter_context(nc.sbuf_tensor(name, shape, dt))

        def sem(name):
            return ctx.enter_context(nc.semaphore(name))

        kc_ = sb("consts", [P, K_N])[:, :]
        ident = kc_[:, K_ID:K_ID + P]
        ones = sb("ones", [P, P])[:, :]
        vec = sb("vec", [P, 120])[:, :]
        sp = sb("ssm_params", [P, 34, 16])
        shapes = [("uT", [P, KC, TT]), ("zT", [P, 14, TT]), ("ring", [P, RING + HI_RING, SLAB]), ("arena", [P, AR])]
        with ExitStack() as plain:
            uT, zT, ring, arena = [plain.enter_context(nc.sbuf_tensor(n, sh, F32)) for n, sh in shapes]
        uT_r, zT_r, ring_r = [sb(n + "_r", sh, F32R) for n, sh in shapes[:3]]
        cuts = [0, 10880, 22848, AR]
        pieces = [sb(f"arena_r{i}", [P, cuts[i + 1] - cuts[i]], F32R) for i in range(3)]
        zq = zT[:, 0:4, :]
        zkv = zT[:, 4:10, :]
        zsu = zT[:, 10:14, :]
        vtok = sb("vtok", [P, 5, 2, P])
        kcT_s = sb("kcT_s", [P, 2, 252])
        kcT_p = sb("kcT_p", [P, 32])
        vc_s = sb("vc_s", [64, DB, P])
        vc_p = sb("vc_p", [P, HD])
        gates = sb("gates", [P, TILES + 1, 24])
        gates_s = sb("gates_s", [P, 2, 3])
        small = sb("small", [P, 96])
        idx = sb("idx", [P, 16], I32)
        pages = sb("page_rows", [16, 32], I32)
        log_dt = sb("log_dt", [16, 2])
        eps_t = sb("eps_t", [P, 1])
        oT = zkv[:, 0:4, :]
        KS, KW = 4, 5
        ZSLOT = [0, 1, 4, 2, 5, 3]

        def ar(off, *dims):
            n = int(np.prod(dims))
            assert off + n <= AR
            v = arena[:, off:off + n]
            if len(dims) == 2:
                return v.rearrange("p (a b) -> p a b", b=dims[1])
            if len(dims) == 3:
                return v.rearrange("p (a b c) -> p a b c", b=dims[1], c=dims[2])
            if len(dims) == 4:
                return v.rearrange("p (a b c d) -> p a b c d", b=dims[1], c=dims[2], d=dims[3])
            return v

        def ar_r(off, a_, b_):
            i = max(i for i in range(3) if cuts[i] <= off)
            assert off + a_ * b_ <= cuts[i + 1]
            off -= cuts[i]
            return pieces[i][:, off:off + a_ * b_].rearrange("p (a b) -> p a b", b=b_)

        u_hi0 = ar_r(10880, KC, TT)
        xtok = ar(0, 5, D)
        hT0 = ar(5120, KC, TT)
        hot = arena[0:33, 20480:20480 + LINE]
        relb = arena[0:33, 22100:22100 + HEADS]
        line = arena[0:HEADS, 22120:22120 + LINE]
        nat = ar(23700, 256)[:, 0:P]
        spread = ar(25500, 3, P)
        zng = arena[0:24, 24900:24900 + TT]
        tmp = ar(23840, 4, 16, 16)
        br_, bi_ = ar(16384, 16, 16), ar(16640, 16, 16)
        bbr, bbi = ar(16896, 16, 16), ar(17152, 16, 16)
        bt_ = ar(17408, 16, 16)
        bdr, bdi = ar(17664, 16, 32), ar(18176, 16, 32)
        cnat = ar(18688, 2, 4, P)
        h0nat = ar(19712, 2, P)
        tokst = ar(9472, 5, 512)
        BT = ar(0, 2, 4, P)
        CT = ar(1024, 2, 16, 32)
        Jt = ar(2048, 2, 16, 32)
        St = ar(3072, 2, 16, 16)
        Hs = ar(3584, 2, 16, NS)
        h0T = ar(4608, 2, P)
        rot = ar(5120, 6, T)
        Et = ar(8192, 2, 2, T)
        Hp = ar(10240, 2, 2, T)
        e_part = ar(27136, T)
        hfin = sb("hfin", [P, 2, 16])
        hfin_s = ar(26752, 2, P)
        hout = ar(27136, 4, P)
        glu_sig = ar(10240, 4, TT)
        w1 = ar(12288, 16, HID)
        XT = ar(16384, 8, KV, 256)
        raw = ar(20480, 2048)
        raw2 = ar(22528, 2048)
        Hh = ar(24576, 2, 504)
        XP = ar(25600, 16, 64)
        Hq = ar(26624, 2, 62)
        w2 = sb("w2", [P, 2, 2, HD])
        pb = sb("pe_bias", [P, 4])
        TZ = ar(0, HEADS, TW)
        Ssb = ar(7304, 4, T)
        Psb = [ar(9352, 4, T)[:, q, :] for q in range(4)] + [ar(15048, 2, T)[:, q, :] for q in range(2)]
        PTs = ar(11400, 4, T)
        PTc = ar(13960, TILES, 2, P)
        cs, ce = ar(7304, TILES * HEADS, 32), ar(8328, TILES * HEADS, 32)
        csum = ar(14984, 64)
        ksel = ar(16384, 2, 1024)
        vsel = ar(18432, 4, 1024)
        kwin = ar(22528, 4, 512)
        vwin = ar(24576, 4, 512)
        biasS = ar(26624, 1056)
        KT = ar(0, 2, 1024)
        KTw = ar(2048, 2, 512)
        bd = ar(3072, 1056)
        bw = ar(4128, 544)
        SS = ar(4672, 1056)
        SW = ar(5728, 544)
        PS_ = ar(6272, 1056)
        PW = ar(7328, 544)
        cc = ar(7872, 3, 64)
        PTS = ar(8064, 16, P)
        dgs = ar(10112, 2, P)
        Qb = ar(10368, DB, 32)
        hT = ar(0, KC, TT)
        mT = ar(KC * TT, KC, TT)
        sig = ar(8704, 4, TT)
        mid = ar(10880, FC, TT)
        sil = ar(22848, 2, TT)
        u_back = ar(10880, KC, TT)
        u_hi_mix = ar_r(10880, KC, TT)
        u_hi = zT_r[:, 0:KC, :]
        mT_lo, mT_hi = ar_r(KC * TT, KC, TT), ar_r(15232, KC, TT)
        mixed_in = [oT[:, k, :] for k in range(4)] + [zsu[:, k, :] for k in range(4)]
        mixed_lo = [zT_r[:, 4 + k, :] for k in range(4)] + [zT_r[:, 10 + k, :] for k in range(4)]
        mixed_hi = [ar_r(19584, 6, TT)[:, k, :] for k in range(6)] + [ar_r(22848, 2, TT)[:, k, :] for k in range(2)]
        mid_lo = ar_r(10880, FC, TT)
        mid_hi = [mT_lo[:, c, :] for c in range(KC)] + [zT_r[:, c, :] for c in range(KC, 14)] + [ar_r(8704, 4, TT)[:, c, :] for c in range(4)] + \
                 [ar_r(23936, 4, TT)[:, c, :] for c in range(4)]
        sq_of = {0: ar(0, KC, TT), 1: ar(19584, KC, TT), 2: ar(14016, KC, TT)}
        pT = ar(10880, 2, TT)
        wple = ar(11968, 2048)
        rt, rs = ar(27136, TT), ar(27680, TT)
        ptok = vtok[:, :, :, :].rearrange("p t a b -> p t (a b)")
        g_final = ar(23936, D)
        ytok = [ar(KC * TT, 4, D)[:, t, :] for t in range(4)] + [ar(24960, D)]
        y_squares = ar(14016, 5, D)

        pair = [ctx.enter_context(nc.psum_tensor(f"pair{i}", [P, 2, 512], F32)) for i in range(4)]

        def bank(b):
            return pair[b // 2][:, b % 2, :]

        slab_landed = [sem(f"slab_landed{i}") for i in range(RING)]
        sum_done = [sem(f"sum_done{i}") for i in range(4)]
        taken = [sem(f"taken{i}") for i in range(4)]
        names = """x0 const_in hot_in nat_in ssm_in ones_set line_done line_copied line_out turned_x copied_x vec_turned
            vec_copied squares normed h_out kvt_done tokst_copied vtok_copied kv_out v_step a_step g_step p_step ldt
            theta_ready sin_done bd_ready bd_turned bd_copied c_turned c_copied h0_turned h0_copied gate_out gate_in
            gates_turned gates_copied rows_in spread_ready spread_turned idx_ready w1_in w2_in raw_in raw_copied
            raw_turned turn_copied hid_done hid_taken c2_done c2_taken xp_ready xs_done samples_done ys_done ys_taken
            x_done x_taken E_ready E_used h_ready y_done y_taken z_ready fin_ready fin_turned fin_copied fin_out
            glu_ready toep_in cs_done cmax_done cexp_done cnorm_done cpt_done cpt_copied s_done s_taken exp_done
            probs_ready pt_done pt_copied o_done o_taken kwin_in vwin_in biasS_in tb_done tb_copied qb_ready sc_done
            cmin_done cexps impsum_ready imp_done bd_seen pc_ready pc_done pc_copied ss_done ss_taken sexp sdiag
            so_done so_taken h_in p_in wple_in mixed h_new y_turned y_root y_made y_out g_in win_out slab_high
            slab_split part_done u_new u_high uhi_out uhi_in u_returned mix_high mix_split z_scaled ng_done mg_done
            in_high in_split mid_new silu_done gate_done mid_high mid_split""".split()
        S = {n: sem(n) for n in names}
        ksel_in = [sem(f"ksel_in{i}") for i in range(2)]
        vsel_in = [sem(f"vsel_in{i}") for i in range(4)]

        xp_t = a["x_prompt"].rearrange("b (t p) d -> p (b t) d", p=P)
        w_in = a["w_in"].rearrange("l (k p) n -> p (l k) n", p=P)

        def done(name):
            return sum_done[pair_of[name]], use_of[name]

        def slab_size(n):
            kind, m, _ = slabs[n]
            return KC * 24 if kind == "ng" else P * min(KC, FC - KC * (m % 3)) if kind == "down" else SLAB

        def used(n):
            kind, m, _ = slabs[n]
            if kind == "down" and m % 3 < 2:
                return S["part_done"], 2 * (m // 3) + m % 3 + 1
            return done(last_use[n])

        def out_of(name):
            return taken[pair_of[name]], use_of[name]

        def keys_turned(b):
            return 3 * (b + 1)

        def both(pr):
            return pair[pr][:, :, 0:HT]

        def whole(pr):
            return pair[pr][:, :, :].rearrange("p a b -> p (a b)")

        def halves(v):
            return v.rearrange("p (h n) -> p h n", h=2)

        block = ctx.enter_context(nc.Block())

        @block.sync
        def _(eng):
            gate_w = a["w_ffn_gate"].rearrange("l (k p) n -> p (l k) n", p=P)
            up_w = a["w_ffn_up"].rearrange("l (k p) n -> p (l k) n", p=P)
            down_w = a["w_ffn_down"].rearrange("l (k p) n -> p (l k) n", p=P)
            o_w = a["w_o"].rearrange("l (k p) n -> p (l k) n", p=P)
            glu_w = a["w_glu"].rearrange("l (k p) n -> p (l k) n", p=P)
            pg_w = a["w_ple_gate"].rearrange("l (k p) n -> p (l k) n", p=P)
            ssm_w = a["w_ssm_br"].rearrange("l (k p) n -> p (l k) n", p=P)

            def load_slab(n):
                kind, s, _ = slabs[n]
                s = Z_BLOCK[s] if kind == "z" else s
                slot = n % RING
                if n >= RING:
                    eng.wait_ge(*used(n - RING))
                dst = ring[:, slot, :]
                landed = slab_landed[slot]
                by_chunk = dst.rearrange("p (k n) -> p k n", k=KC)
                if kind == "z" and s < 4:
                    for h in range(2):
                        c0 = (s + G * h) * HD
                        eng.dma_start(by_chunk[:, :, HD * h:HD * h + HD], w_in[:, :, c0:c0 + HD]).then_inc(landed, 16)
                elif kind == "z":
                    c0 = C_KV + P * (s - 4) if s < 10 else C_SU + P * (s - 10)
                    eng.dma_start(by_chunk, w_in[:, :, c0:c0 + P]).then_inc(landed, 16)
                elif kind in ("mg0", "mg1", "gate", "up", "wo", "pg"):
                    src, c0 = {"mg0": (w_in, C_MG), "mg1": (w_in, C_MG + D), "gate": (gate_w, 0), "up": (up_w, 0),
                               "wo": (o_w, 0), "pg": (pg_w, 0)}[kind]
                    eng.dma_start(by_chunk, src[:, :, c0 + P * s:c0 + P * s + P]).then_inc(landed, 16)
                elif kind == "ng":
                    eng.dma_start(dst[:, 0:KC * 24].rearrange("p (k n) -> p k n", k=KC),
                                  w_in[:, :, C_NG:C_NG + 24]).then_inc(landed, 16)
                elif kind == "glu":
                    eng.dma_start(dst.rearrange("p (k n) -> p k n", k=4), glu_w[:, :, 256 * s:256 * s + 256]).then_inc(landed, 16)
                elif kind == "att":
                    v = dst[:, 0:512].rearrange("p (k n) -> p k n", k=4)
                    for h in range(2):
                        rows = a["w_att_br"][0, h * 256:(h + 1) * 256, P * s:P * s + P]
                        eng.dma_start(v[64 * h:64 * h + 64, :, :],
                                      rows.rearrange("(k p) n -> p k n", p=HD)).then_inc(landed, 16)
                    eng.dma_start(dst[:, 512:1024].rearrange("p (k n) -> p k n", k=4),
                                  ssm_w[:, :, P * s:P * s + P]).then_inc(landed, 16)
                elif kind == "down":
                    m, k0 = s // 3, KC * (s % 3)
                    n_k = min(KC, FC - k0)
                    eng.dma_start(by_chunk[:, 0:n_k, :], down_w[:, k0:k0 + n_k, m * P:(m + 1) * P]).then_inc(landed, 16)

            for t in range(TILES):
                eng.dma_start(xtok[:, t, :], xp_t[:, t, :]).then_inc(S["x0"], 16)
            eng.dma_start(xtok[0:NS, 4, :], a["x_sample"].rearrange("b t d -> (b t) d")).then_inc(S["x0"], 16)
            eng.dma_start(kc_, a["consts"]).then_inc(S["const_in"], 16)
            rows = lambda n, k: a[n].rearrange("l (r p) -> (l r) p", p=P)
            at_row = 0
            for n in ("attn_norm", "ffn_norm", "ple_norm"):
                eng.dma_start(nat[at_row:at_row + KC, :], rows(n, KC)).then_inc(S["nat_in"], 16)
                at_row += KC
            eng.dma_start(nat[24:28, :], rows("b_glu", 4)).then_inc(S["nat_in"], 16)
            eng.dma_start(nat[28:32, :], a["ssm_d"].rearrange("l (r g) c -> (l r) (g c)", r=4)).then_inc(S["nat_in"], 16)
            eng.dma_start(nat[32:48, :], a["ssm_a_re"].rearrange("l (j g) p -> (l j) (g p)", g=2)).then_inc(S["nat_in"], 16)
            eng.dma_start(nat[48:64, :], a["ssm_a_im"].rearrange("l (j g) p -> (l j) (g p)", g=2)).then_inc(S["nat_in"], 16)
            eng.dma_start(nat[64:80, :], a["cmp_pe_k"].rearrange("l (k r) d -> (l k) (r d)", r=2)).then_inc(S["nat_in"], 16)
            eng.dma_start(nat[80:96, :], a["cmp_pe_v"].rearrange("l (k r) d -> (l k) (r d)", r=2)).then_inc(S["nat_in"], 16)
            eng.dma_start(pages[0:8, 0:8], a["page_table"]).then_inc(S["rows_in"], 16)
            eng.dma_start(pages[0:4, 16:32], a["page_table"].rearrange("(a b) n -> a (b n)", b=2)).then_inc(S["rows_in"], 16)
            eng.dma_start(log_dt[:, :], a["ssm_log_dt"].rearrange("l (j g) -> (l j) g", g=2)).then_inc(S["rows_in"], 16)
            eng.dma_start(hot, a["buckets"]).then_inc(S["hot_in"], 16)
            eng.dma_start(relb[0:NBUCKET, :], a["rel_bias"]).then_inc(S["hot_in"], 16)
            load_slab(0)
            load_slab(1)
            for q, (src, dst) in enumerate((("ssm_b_re", br_), ("ssm_b_im", bi_))):
                eng.dma_start(dst, a[src].rearrange("l (j g) p c -> (g p) (l j) c", g=2)).then_inc(S["ssm_in"], 16)
            for q, src in enumerate(("ssm_c_re", "ssm_c_im")):
                v = a[src].rearrange("l (k g) c p -> (g c) (l k) p", k=4)
                for half in range(2):
                    eng.dma_start(cnat[:, q, :, 64 * half:64 * half + 64], v).then_inc(S["ssm_in"], 16)
            for q, src in enumerate(("state_ssm_re", "state_ssm_im")):
                eng.dma_start(h0nat[:, q, :], a[src].rearrange("l b (j g) p -> (l b j) (g p)", g=2)).then_inc(S["ssm_in"], 16)
            for n in range(2, RING):
                load_slab(n)
            rest = (WIN - DT) * KV * HD // 16
            for src, dst in (("cache_k_win", "nk_win_s"), ("cache_v_win", "nv_win_s")):
                dims = [[rest, 16], [WIN * KV * HD, DB], [1, rest]]
                eng.dma_start(bass.AP(a[dst].tensor, 0, dims),
                              bass.AP(a[src].tensor, DT * KV * HD, dims)).then_inc(S["win_out"], 16)
            eng.wait_ge(S["copied_x"], 10)
            eng.dma_start(h_spill, arena[:, 5120:5120 + KC * TT]).then_inc(S["h_out"], 16)
            eng.wait_ge(S["line_copied"], 4)
            eng.dma_start(bass.AP(bias_line.tensor, 0, [[SHIFTS * LPITCH, HEADS], [LPITCH + 1, SHIFTS], [1, LINE]]),
                          wide(line, SHIFTS, 1)).then_inc(S["line_out"], 16)
            for n in range(RING, 7):
                load_slab(n)
            eng.wait_ge(S["u_high"], KC)
            eng.dma_start(u_spill, u_hi0.rearrange("p a b -> p (a b)").bitcast(F32)).then_inc(S["uhi_out"], 16)
            for n in range(7, 20):
                load_slab(n)
            eng.wait_ge(*done(("ng", 0)))
            eng.wait_ge(S["uhi_out"], 16)
            eng.dma_start(w1, a["cmp_w1_k"].rearrange("l (k p) n -> p (l k) n", p=P)).then_inc(S["w1_in"], 16)
            for q, src in enumerate(("cmp_w2_k", "cmp_w2_v")):
                eng.dma_start(w2[:, q, :, :], a[src].rearrange("l (k p) n -> p (l k) n", p=P)).then_inc(S["w2_in"], 16)
            eng.wait_ge(S["gates_copied"], TILES + 1)
            eng.dma_start(gate_rows, gates[0:NS, TILES, :]).then_inc(S["gate_out"], 16)
            eng.wait_ge(S["gate_out"], 16)
            for b in range(DB):
                eng.dma_start(gates_s[32 * (b % 4):32 * (b % 4) + 32, b // 4, :],
                              bass.AP(gate_rows.tensor, DT * 24 * b, [[3, HEADS], [24, DT], [1, 3]])).then_inc(S["gate_in"], 16)
            eng.wait_ge(S["tokst_copied"], 5)
            eng.wait_ge(S["vtok_copied"], 5)
            stores = [("nk_cmp", 0, None), ("nv_cmp", 1, None), ("nk_sel", 2, None), ("nk_win", 3, None),
                      ("nv_sel", None, 0), ("nv_win", None, 1)]
            for n, q, v in stores:
                src = tokst[:, 0:4, q * P:(q + 1) * P] if v is None else vtok[:, 0:4, v, :]
                eng.dma_start(a[n + "_p"].rearrange("l b (t p) k d -> p (l b t) (k d)", p=P), src).then_inc(S["kv_out"], 16)
                src = tokst[0:NS, 4, q * P:(q + 1) * P] if v is None else vtok[0:NS, 4, v, :]
                if n.endswith("win"):
                    o = a[n + "_s"]
                    eng.dma_start(bass.AP(o.tensor, (WIN - DT) * P, [[WIN * P, DB], [P, DT], [1, P]]), src).then_inc(S["kv_out"], 16)
                else:
                    eng.dma_start(a[n + "_s"].rearrange("l b t k d -> (l b t) (k d)"), src).then_inc(S["kv_out"], 16)
            eng.wait_ge(S["hid_done"], 6)
            eng.dma_start(w1, a["cmp_w1_v"].rearrange("l (k p) n -> p (l k) n", p=P)).then_inc(S["w1_in"], 16)
            eng.wait_ge(S["y_done"], 16)
            eng.wait_ge(S["fin_turned"], 4)
            eng.wait_ge(S["line_out"], 16)
            for p0 in range(0, P, SHIFTS):
                for k in range(KV):
                    eng.dma_start(TZ[p0:p0 + SHIFTS, k:HEADS:KV, :],
                                  bass.AP(bias_line.tensor, k * G * SHIFTS * LPITCH + TBASE - p0,
                                          [[LPITCH, SHIFTS], [SHIFTS * LPITCH, G], [1, TW]])).then_inc(S["toep_in"], 16)
            eng.wait_ge(S["fin_copied"], 4)
            for q, n in enumerate(("ns_re", "ns_im")):
                eng.dma_start(a[n + "_p"].rearrange("l b (j g) p -> (l b j) (g p)", g=2), hout[0:16, q, :]).then_inc(S["fin_out"], 16)
                eng.dma_start(a[n + "_s"].rearrange("l b (j g) p -> (l b j) (g p)", g=2), hout[:, 2 + q, :]).then_inc(S["fin_out"], 16)
            eng.wait_ge(S["c2_done"], 6)
            def window(n, dst, tile, s):
                eng.dma_start(dst, a[n][0, 4 * tile:4 * tile + 4].rearrange("b (p j) k d -> p b (j k d)", p=P)).then_inc(S[s], 16)

            window("cache_k_win", kwin, 0, "kwin_in")
            window("cache_v_win", vwin, 0, "vwin_in")
            eng.wait_ge(S["fin_out"], 64)
            for b in range(4):
                eng.dma_start(biasS[32 * b:32 * b + 32, 0:PAST + DT],
                              bass.AP(bias_line.tensor, DT - 1, [[SHIFTS * LPITCH, HEADS], [LPITCH, DT], [1, PAST + DT]])).then_inc(S["biasS_in"], 16)
            load_slab(20)
            load_slab(21)
            eng.wait_ge(S["o_taken"], TILES)
            eng.dma_start(arena[:, 10880:10880 + KC * TT], u_spill).then_inc(S["uhi_in"], 16)
            eng.wait_ge(S["tb_done"], keys_turned(3))
            window("cache_k_win", kwin, 1, "kwin_in")
            eng.wait_ge(S["so_done"], 4)
            window("cache_v_win", vwin, 1, "vwin_in")
            eng.wait_ge(S["so_taken"], 4)
            eng.wait_ge(S["h_out"], 16)
            eng.dma_start(arena[:, 0:KC * TT], h_spill).then_inc(S["h_in"], 16)
            eng.wait_ge(S["kv_out"], 16 * 12)
            eng.dma_start(ptok[:, 0:4, :], a["p_prompt"].rearrange("l b (t p) d -> p (l b t) d", p=P)).then_inc(S["p_in"], 16)
            eng.dma_start(ptok[0:NS, 4, :], a["p_sample"].rearrange("l b t d -> (l b t) d")).then_inc(S["p_in"], 16)
            for n in range(22, len(slabs)):
                load_slab(n)
                if n == len(slabs) - KC + 3:
                    eng.wait_ge(*done(("down", KC - 1)))
                    eng.dma_start(wple.rearrange("p (k n) -> p k n", k=2), a["w_ple"].rearrange("l (k p) n -> p (l k) n", p=P)).then_inc(S["wple_in"], 16)
                    eng.dma_start(g_final, bass.AP(a["final_norm"].tensor, 0, [[0, P], [1, D]])).then_inc(S["g_in"], 16)
            for t in range(5):
                eng.wait_ge(S["y_made"], t + 1)
                dst = a["y_prompt"][0, t * P:(t + 1) * P, :] if t < TILES else a["y_sample"].rearrange("b t d -> (b t) d")
                eng.dma_start(dst, ytok[t][0:P if t < TILES else NS, :]).then_inc(S["y_out"], 16)
            eng.wait_ge(S["y_out"], 16 * 5)
            eng.wait_ge(S["win_out"], 32)
            eng.wait_ge(S["kv_out"], 16 * 12)
            eng.wait_ge(S["fin_out"], 16 * 4)

        @block.gpsimd
        def _(eng):
            steps = [0]

            def link(ins):
                steps[0] += 1
                ins.then_inc(S["g_step"], 1)
                eng.wait_ge(S["g_step"], steps[0])

            pools = {n: a[n] for n in ("cache_k_cmp", "cache_v_cmp", "cache_k_sel", "cache_v_sel")}

            def gather_cmp(n):
                kv, tile = n // 4, n % 4
                if n:
                    eng.wait_ge(S["raw_copied"], n)
                src = pools["cache_k_cmp" if kv == 0 else "cache_v_cmp"].rearrange("l n (c r) k d -> (l n c) (r k d)", r=CH)
                eng.indirect_dma_start(out=raw, out_offset=None, in_=src,
                                       in_offset=bass.IndirectOffsetOnAxis(ap=idx[:, 8 + tile:9 + tile].bitcast(U32), axis=0)).then_inc(S["raw_in"], 16)

            def gather_sel(which, b):
                src = pools["cache_k_sel" if which == 0 else "cache_v_sel"].rearrange("l n (c r) k d -> (l n c) (r k d)", r=8)
                dst = ksel[:, b % 2, :] if which == 0 else vsel[:, b % 4, :]
                eng.indirect_dma_start(out=dst, out_offset=None, in_=src,
                                       in_offset=bass.IndirectOffsetOnAxis(ap=idx[:, b:b + 1].bitcast(U32), axis=0)).then_inc(ksel_in[b % 2] if which == 0 else vsel_in[b % 4], 16)

            def split(n):
                q = split_index[n]
                eng.wait_ge(S["slab_high"], q + 1)
                hi = ring_r[:, RING + q % HI_RING, 0:slab_size(n)].bitcast(F32)
                eng.tensor_tensor(ring_r[:, n % RING, 0:slab_size(n)], ring[:, n % RING, 0:slab_size(n)], hi, ALU.subtract).then_inc(S["slab_split"], 1)

            for n in range(15):
                split(n)
            eng.wait_ge(S["idx_ready"], 2)
            eng.wait_ge(S["line_out"], 16)
            eng.wait_ge(S["vec_turned"], 1)
            gather_cmp(0)
            gather_cmp(1)
            eng.wait_ge(S["theta_ready"], 1)
            eng.wait_ge(S["kv_out"], 16 * 12)
            eng.wait_ge(S["h_out"], 16)
            raws = 2
            for j in range(16):
                if j:
                    eng.wait_ge(S["E_ready"], j)
                if j >= 2:
                    eng.wait_ge(S["E_used"], j - 1)
                J = lambda c: wide(Jt[:, c, j, :], 16)
                Sx = lambda c: wide(St[:, c, j, :], 32, 1)
                part = e_part.rearrange("p (a b) -> p a b", b=16)
                E = lambda c: Et[:, j % 2, c, :].rearrange("p (a b) -> p a b", b=16)
                eng.tensor_tensor(E(0), J(0), Sx(0), ALU.mult)
                link(eng.tensor_tensor(part, J(1), Sx(1), ALU.mult))
                link(eng.tensor_tensor(E(0), E(0), part, ALU.subtract))
                eng.tensor_tensor(E(1), J(0), Sx(1), ALU.mult)
                link(eng.tensor_tensor(part, J(1), Sx(0), ALU.mult))
                eng.tensor_tensor(E(1), E(1), part, ALU.add).then_inc(S["E_ready"], 1)
                if j % 2 == 0 and raws < 8:
                    gather_cmp(raws)
                    raws += 1
            while raws < 8:
                gather_cmp(raws)
                raws += 1
            for n in (17, 18, 19):
                split(n)
            eng.wait_ge(S["c2_done"], 6)
            eng.wait_ge(S["toep_in"], 16 * KV * P // SHIFTS)
            for which, b in [(0, 0), (0, 1)] + [(1, b) for b in range(4)] + [(0, b) for b in range(2, DB)] + [(1, b) for b in range(4, DB)]:
                if which == 0 and b >= 2:
                    eng.wait_ge(S["tb_done"], keys_turned(b - 2))
                if which == 1 and b >= 4:
                    eng.wait_ge(S["so_done"], b - 3)
                gather_sel(which, b)
            for n in range(20, len(slabs)):
                if n in split_index:
                    split(n)

        def pt_copy(eng, n):
            W = P * (n // 8 + 1)
            for br in range(2):
                eng.wait_ge(S["pt_done"], 2 * n + br + 1)
                if n >= 2:
                    eng.wait_ge(S["o_done"], n - 1)
                eng.activation(PTs[:, 2 * (n % 2) + br, 0:W], bank(4 + br)[:, 0:W], ACT.Copy).then_inc(S["pt_copied"], 1)

        @block.scalar
        def _(eng):
            steps = [0]

            def link(ins):
                steps[0] += 1
                ins.then_inc(S["a_step"], 1)
                eng.wait_ge(S["a_step"], steps[0])

            def squares(n, src, gate=lambda k: None):
                for k in range(KC):
                    gate(k)
                    eng.activation(sq_of[n][:, k, :], src[:, k, :], ACT.Square).then_inc(S["squares"], 1)

            def root(n, dst):
                eng.wait_ge(*done(("norm", n)))
                eng.activation(halves(dst), both(pair_of[("norm", n)]), ACT.Sqrt, bias=eps_t[:, :], scale=1.0 / D).then_inc(taken[pair_of[("norm", n)]], 1)

            def high_after(name, part=2):
                slab = [st[0] for st in dict(groups)[name]][KC * part if name[0] == "down" else 0]
                weights_high(split_index[slab] + HI_RING)

            def weights_high(q):
                if q >= len(split_slab):
                    return
                n = split_slab[q]
                if q >= HI_RING:
                    eng.wait_ge(*used(split_slab[q - HI_RING]))
                eng.wait_ge(slab_landed[n % RING], landed_at[n])
                eng.activation(ring_r[:, RING + q % HI_RING, 0:slab_size(n)], ring[:, n % RING, 0:slab_size(n)], ACT.Copy).then_inc(S["slab_high"], 1)

            def high(n, dst, before=lambda k: None, after=lambda k: None):
                for k in range(KC):
                    before(k)
                    eng.wait_ge(S["u_new"], KC * n + k + 1)
                    eng.activation(dst[:, k, :], uT[:, k, :], ACT.Copy).then_inc(S["u_high"], 1)
                    after(k)

            for q in range(HI_RING):
                weights_high(q)
            eng.wait_ge(S["ones_set"], 2)
            high(0, u_hi0)
            squares(0, hT0)
            root(0, rt)
            ldt, ar_, dt, mag = vec[:, 96:112], vec[:, 32:48], sp[:, 0, :], sp[:, 1, :]
            eng.wait_ge(S["vec_copied"], 1)
            eng.activation(dt, ldt, ACT.Exp).then_inc(S["ldt"], 1)
            eng.wait_ge(S["ldt"], 2)
            eng.activation(mag, sp[:, 2, :], ACT.Exp).then_inc(S["sin_done"], 1)
            eng.wait_ge(S["ldt"], 4)
            eng.activation(sp[:, 5, :], sp[:, 3, :], ACT.Sin).then_inc(S["sin_done"], 1)
            eng.activation(sp[:, 6, :], sp[:, 4, :], ACT.Sin).then_inc(S["sin_done"], 1)
            for m in range(14):
                name = ("z", m)
                eng.wait_ge(*done(name))
                z = Z_BLOCK[m]
                dst = zq[:, z, :] if z < 4 else zkv[:, ZSLOT[z - 4], :] if z < 10 else zsu[:, z - 10, :]
                eng.activation(halves(dst), both(pair_of[name]), ACT.Copy).then_inc(taken[pair_of[name]], 1)
                if m < 12:
                    high_after(name)
            eng.wait_ge(*out_of(("ng", 0)))
            eng.activation(zng, zng, ACT.Sigmoid).then_inc(S["ng_done"], 1)
            eng.wait_ge(S["uhi_out"], 16)
            for t in range(5):
                n = P if t < 4 else NS
                eng.wait_ge(S["kvt_done"], 2 * t + 1)
                eng.activation(tokst[0:n, t, :], bank(2 * (t % 2))[0:n, :], ACT.Copy).then_inc(S["tokst_copied"], 1)
            high_after(("z", 12))
            high_after(("z", 13))
            high_after(("ng", 0))
            eng.wait_ge(S["gate_out"], 16)
            eng.wait_ge(S["gates_turned"], 1)
            turn = hid = c2 = 0

            def turns_out(tt):
                nonlocal turn
                for q in range(4):
                    ckv, ph = q // 2, q % 2
                    eng.wait_ge(S["raw_turned"], turn + 1)
                    eng.activation(XT[:, 4 * ph:4 * ph + 4, ckv, tt * P:(tt + 1) * P],
                                   bank(2 + turn % 2).rearrange("p (a b) -> p a b", b=P), ACT.Copy).then_inc(S["turn_copied"], 1)
                    turn += 1

            def prompt_blocks(kv):
                nonlocal hid, c2
                for h in range(2):
                    eng.wait_ge(S["hid_done"], hid + 1)
                    b, bias = bank(hid % 2), pb[:, 2 * kv + h:2 * kv + h + 1]
                    link(eng.activation(bias, b[:, 62:63], ACT.Copy))
                    eng.activation(Hq[:, h, :], b[:, 0:62], ACT.Gelu_apprx_tanh, bias=bias).then_inc(S["hid_taken"], 1)
                    hid += 1
                eng.wait_ge(S["c2_done"], c2 + 1)
                if kv == 0:
                    eng.activation(kcT_p[:, 0:CB_P], bank(7)[:, 0:CB_P], ACT.Copy).then_inc(S["c2_taken"], 1)
                else:
                    for q in range(4):
                        r = slice(32 * q, 32 * q + CB_P)
                        ins = eng.activation(vc_p[r, :], bank(7)[r, 0:HD], ACT.Copy)
                    ins.then_inc(S["c2_taken"], 1)
                c2 += 1

            for kv in range(2):
                for bg in range(2):
                    turns_out(0)
                    if bg == 0:
                        prompt_blocks(kv)
                    turns_out(1)
                    for h in range(2):
                        eng.wait_ge(S["hid_done"], hid + 1)
                        eng.activation(Hh[:, h, :], bank(hid % 2)[:, 0:504], ACT.Gelu_apprx_tanh,
                                       bias=pb[:, 2 * kv + h:2 * kv + h + 1]).then_inc(S["hid_taken"], 1)
                        hid += 1
                    eng.wait_ge(S["c2_done"], c2 + 1)
                    if kv == 0:
                        eng.activation(kcT_s[:, bg, :], bank(7)[:, 0:252], ACT.Copy).then_inc(S["c2_taken"], 1)
                    else:
                        eng.activation(vc_s[0:CB_S, 4 * bg:4 * bg + 4, :], bank(7)[0:CB_S, :].rearrange("p (a b) -> p a b", b=P), ACT.Copy).then_inc(S["c2_taken"], 1)
                    c2 += 1
            for c in range(4):
                eng.wait_ge(S["y_taken"], c + 1)
                eng.activation(zsu[:, c, :], zsu[:, c, :], ACT.Gelu_apprx_tanh).then_inc(S["z_ready"], 1)
            for m in range(4):
                if m == 2:
                    eng.wait_ge(S["cmax_done"], 1)
                    eng.activation(ce[:, :, 0:CB_P], cs[:, :, 0:CB_P], ACT.Exp, scale=0.125).then_inc(S["cexp_done"], 1)
                name = ("glu", m)
                eng.wait_ge(*done(name))
                eng.activation(halves(glu_sig[:, m, :]), both(pair_of[name]), ACT.Sigmoid, bias=vec[:, 24 + m:25 + m]).then_inc(taken[pair_of[name]], 1)
            for half in range(2):
                eng.wait_ge(S["cpt_done"], half + 1)
                eng.activation(PTc[:, 2 * half:2 * half + 2, :, :].rearrange("p i a b -> p (i a) b"),
                               bank(4 + half).rearrange("p (a b) -> p a b", b=P), ACT.Copy).then_inc(S["cpt_copied"], 1)
            n = 0
            for i in range(TILES):
                W = P * (i + 1)
                for g in range(G):
                    for kv in range(KV):
                        for br in range(2):
                            q = 2 * (n % 3) + br
                            eng.wait_ge(S["s_taken"], 2 * n + br + 1)
                            if n >= 3:
                                eng.wait_ge(S["pt_done"], 2 * (n - 3) + br + 1)
                            eng.activation(Psb[q][:, 0:W], Ssb[:, 2 * (n % 2) + br, 0:W], ACT.Exp, bias=small[:, q:q + 1], scale=-1.0,
                                           accum_out=small[:, 24 + q:25 + q]).then_inc(S["exp_done"], 1)
                        if n >= 2:
                            pt_copy(eng, n - 2)
                        n += 1
            pt_copy(eng, n - 2)
            pt_copy(eng, n - 1)
            tb = 0

            def tb_copy(dst, src):
                nonlocal tb
                eng.wait_ge(S["tb_done"], tb + 1)
                ins = eng.activation(dst, src(bank(4 + tb % 2)), ACT.Copy)
                ins.then_inc(S["tb_copied"], 1)
                tb += 1

            by4 = lambda x: x.rearrange("p (a b) -> p a b", b=P)

            def keys_out(tile):
                eng.wait_ge(S["cmin_done"], tile + 1)
                eng.activation(cc[:, 1, 0:CB_S], cc[:, 0, 0:CB_S], ACT.Exp, bias=small[:, 16:17], scale=-1.0, accum_out=small[:, 17:18]).then_inc(S["cexps"], 1)
                for b in range(4 * tile, 4 * tile + 4):
                    for j0 in (0, 4):
                        tb_copy(at(KT[:, b % 2, :], j0, [[1, 4], [8, P]]), by4)
                    tb_copy(at(KTw[:, b % 2, :], 0, [[1, 4], [4, P]]), by4)

            def exps(tile):
                eng.wait_ge(S["ss_taken"], 2 * tile + 1)
                eng.activation(PS_, SS, ACT.Exp, bias=small[:, 18:19], scale=-1.0, accum_out=small[:, 20:21]).then_inc(S["sexp"], 1)
                eng.wait_ge(S["ss_taken"], 2 * tile + 2)
                eng.activation(PW, SW, ACT.Exp, bias=small[:, 19:20], scale=-1.0, accum_out=small[:, 21:22]).then_inc(S["sexp"], 1)

            def probs_out():
                tb_copy(PTS[:, 0:4, :], by4)
                tb_copy(PTS[:, 4:8, :], by4)
                tb_copy(PTS[:, 9:13, :], by4)
                tb_copy(at(PTS[0:NS, 8, :], 0, [[5 * P, 2], [1, P]]), lambda x: x[0:NS, 0:256].rearrange("p (a b) -> p a b", b=P))

            keys_out(0)
            exps(0)
            keys_out(1)
            probs_out()
            exps(1)
            eng.wait_ge(S["so_done"], 4)
            probs_out()
            def mix_high(c):
                eng.wait_ge(S["mixed"], c + 1)
                eng.activation(mT_hi[:, c, :], mT[:, c, :], ACT.Copy).then_inc(S["mix_high"], 1)

            def mid_part(c):
                eng.wait_ge(S["mid_new"], c + 1)
                eng.activation(mid_hi[c], mid[:, c, :], ACT.Copy).then_inc(S["mid_high"], 1)

            eng.wait_ge(S["uhi_in"], 16)
            for k in range(KC):
                eng.activation(u_hi_mix[:, k, :], u_back[:, k, :], ACT.Copy).then_inc(S["u_returned"], 1)
            for k in range(KC):
                if k == 0:
                    eng.wait_ge(S["so_taken"], 4)
                    eng.wait_ge(S["glu_ready"], 4)
                eng.activation(mixed_hi[k], mixed_in[k], ACT.Copy).then_inc(S["in_high"], 1)
            for c in range(KC):
                if c:
                    high_after(("ssm", c - 1))
                    mix_high(c - 1)
                for q, nm in enumerate(("mg0", "mg1")):
                    name = (nm, c)
                    eng.wait_ge(*out_of(name))
                    x = sig[:, 2 * (c % 2) + q, :]
                    eng.activation(x, x, ACT.Sigmoid).then_inc(S["mg_done"], 1)
                    high_after(name)
            high_after(("ssm", KC - 1))
            mix_high(KC - 1)
            high(1, u_hi, after=lambda k: high_after(("wo", k)))
            squares(1, hT)
            root(1, rt)
            for c in range(FC):
                name = ("gate", c)
                eng.wait_ge(*out_of(name))
                eng.activation(sil[:, c % 2, :], sil[:, c % 2, :], ACT.Silu).then_inc(S["silu_done"], 1)
                if c:
                    mid_part(c - 1)
                    high_after(("up", c - 1))
                high_after(name)
            mid_part(FC - 1)
            high_after(("up", FC - 1))

            def down_parts(k):
                high_after(("down", k), 0)
                high_after(("down", k), 1)

            high(2, u_hi, down_parts, lambda k: high_after(("down", k)))
            squares(2, hT)
            root(2, rt)
            for c in range(KC):
                name = ("pg", c)
                eng.wait_ge(*out_of(name))
                eng.activation(sig[:, c % 2, :], sig[:, c % 2, :], ACT.Sigmoid).then_inc(S["gate_done"], 1)
                high_after(name)
            for t in range(5):
                n = P if t < 4 else NS
                eng.wait_ge(S["y_turned"], t + 1)
                link(eng.activation(y_squares[0:n, t, :], whole(t % 4)[0:n, :], ACT.Square, accum_out=small[0:n, 80 + t:81 + t]))
                eng.activation(small[0:n, 85 + t:86 + t], small[0:n, 80 + t:81 + t], ACT.Sqrt, bias=eps_t[0:n, :], scale=1.0 / D).then_inc(S["y_root"], 1)

        @block.vector
        def _(eng):
            steps = [0]

            def link(ins):
                steps[0] += 1
                ins.then_inc(S["v_step"], 1)
                eng.wait_ge(S["v_step"], steps[0])

            def f32(x):
                return x.bitcast(F32)

            def tt(o, x, y, op):
                return eng.tensor_tensor(o, x, y, op)

            def low(n, k, hi):
                eng.wait_ge(S["u_high"], KC * n + k + 1)
                tt(uT_r[:, k, :], uT[:, k, :], f32(hi[:, k, :]), ALU.subtract).then_inc(S["normed"], 1)

            def weigh(n, k, col, src, hi):
                eng.tensor_scalar(uT[:, k, :], src[:, k, :], vec[:, col + k:col + k + 1], None, ALU.mult).then_inc(S["u_new"], 1)
                if k:
                    low(n, k - 1, hi)

            def inverse(n):
                eng.wait_ge(*out_of(("norm", n)))
                link(eng.reciprocal(rs, rt))

            def scaled(dst, name):
                eng.wait_ge(*done(name))
                eng.tensor_tensor(halves(dst), both(pair_of[name]), halves(rs), ALU.mult).then_inc(taken[pair_of[name]], 1)

            def z_scale(ms):
                for m in ms:
                    z = Z_BLOCK[m]
                    x = zq[:, z, :] if z < 4 else zkv[:, ZSLOT[z - 4], :] if z < 10 else zsu[:, z - 10, :]
                    eng.wait_ge(*out_of(("z", m)))
                    tt(x, x, rs, ALU.mult).then_inc(S["z_scaled"], 1)

            def mix_low(c):
                eng.wait_ge(S["mix_high"], c + 1)
                tt(mT_lo[:, c, :], mT[:, c, :], f32(mT_hi[:, c, :]), ALU.subtract).then_inc(S["mix_split"], 1)

            def mid_low(c):
                eng.wait_ge(S["mid_high"], c + 1)
                tt(mid_lo[:, c, :], mid[:, c, :], f32(mid_hi[c]), ALU.subtract).then_inc(S["mid_split"], 1)

            def xp_fill(kv):
                if kv:
                    eng.wait_ge(S["hid_done"], 2)
                for par in range(2):
                    for k in range(KV):
                        src = zkv[64 * k:64 * k + 64, ZSLOT[kv], 0:T].rearrange("p (c q r) -> p q c r", q=8, r=2)[:, :, :, par]
                        for half in range(2):
                            eng.tensor_copy(XP[64 * par:64 * par + 64, 8 * half:8 * half + 8, CB_P * k:CB_P * (k + 1)],
                                            src[:, :, half:half + CB_P])
                eng.tensor_copy(XP[:, :, 62:63], vec[:, 64 + 16 * kv:80 + 16 * kv].rearrange("p (a b) -> p a b", b=1)).then_inc(S["xp_ready"], 1)

            def raw_copy(n):
                eng.wait_ge(S["raw_in"], 16 * (n + 1))
                if n:
                    eng.wait_ge(S["raw_turned"], 4 * n)
                for par in range(2):
                    ins = eng.tensor_copy(raw2.rearrange("p (q k r d) -> p q k r d", k=KV, r=2, d=HD)[:, :, :, par, :],
                                          raw.rearrange("p (q r k d) -> p q r k d", r=2, k=KV, d=HD)[:, :, par, :, :])
                ins.then_inc(S["raw_copied"], 1)

            def y_out(c):
                eng.wait_ge(S["y_done"], 4 * c + 4)
                eng.scalar_tensor_tensor(zsu[:, c, 0:T], zsu[:, c, 0:T], vec[:, 28 + c:29 + c], bank(6), ALU.mult, ALU.add).then_inc(S["y_taken"], 1)

            def scale_probs(n):
                q0, i, h = 2 * (n % 3), n // 8, n % 8
                head = (h % KV) * G + h // KV
                inv = small[:, 32 + q0:34 + q0]
                eng.wait_ge(S["exp_done"], 2 * n + 2)
                link(eng.tensor_scalar(inv, small[:, 24 + q0:26 + q0], 1e-30, None, ALU.max))
                link(eng.reciprocal(inv, inv))
                for br in range(2):
                    gc = 3 * head + 1 + br
                    x = Psb[q0 + br][:, 0:P * (i + 1)]
                    eng.tensor_scalar(x, x, inv[:, br:br + 1], gates[:, i, gc:gc + 1], ALU.mult, ALU.mult).then_inc(S["probs_ready"], 1)

            def take_o(i):
                eng.tensor_copy(oT[:, :, i * P:(i + 1) * P], bank(6).rearrange("p (a b) -> p a b", b=P)).then_inc(S["o_taken"], 1)

            eng.memset(ones, 1.0).then_inc(S["ones_set"], 1)
            eng.memset(eps_t[:, :], EPS).then_inc(S["ones_set"], 1)
            eng.memset(relb[NBUCKET:NBUCKET + 1, :], 1.0).then_inc(S["ones_set"], 1)
            eng.wait_ge(S["rows_in"], 48)
            for q, (src, n) in enumerate(((pages[0:8, 0:8], 16), (pages[0:4, 16:32], 8), (log_dt[:, :], SP_))):
                rows = src.ap[0][1]
                eng.tensor_copy(spread[0:rows, q, :].rearrange("p (a b) -> p a b", b=n), wide(src, n)).then_inc(S["spread_ready"], 1)
            eng.wait_ge(S["vec_turned"], 1)
            eng.tensor_copy(vec[:, 0:96], bank(2)[:, 0:96])
            eng.wait_ge(S["spread_turned"], 1)
            eng.tensor_copy(vec[:, 96:112], bank(3)[:, 32:48]).then_inc(S["vec_copied"], 1)
            eng.tensor_scalar(idx[:, 0:8], bank(3)[:, 0:8], 16.0, kc_[:, K_MOD:K_MOD + 1], ALU.mult, ALU.add).then_inc(S["idx_ready"], 1)
            eng.tensor_scalar(idx[:, 8:12], bank(3)[:, 16:20], 8.0, kc_[:, K_MOD + 1:K_MOD + 2], ALU.mult, ALU.add).then_inc(S["idx_ready"], 1)
            for q in range(10):
                t, kk = q % 5, q // 5
                n = P if t < 4 else NS
                eng.wait_ge(S["turned_x"], q + 1)
                eng.tensor_copy(hT0[:, 4 * kk:4 * kk + 4, t * P:t * P + n],
                                bank(q % 2).rearrange("p (a b) -> p a b", b=P)[:, :, 0:n]).then_inc(S["copied_x"], 1)
            eng.wait_ge(S["copied_x"], 10)
            eng.wait_ge(S["vec_copied"], 1)
            for k in range(KC):
                weigh(0, k, 0, hT0, u_hi0)
            low(0, KC - 1, u_hi0)
            for q in range(4):
                eng.wait_ge(S["line_done"], q + 1)
                n = LINE // 4
                eng.tensor_copy(line[:, q * n:(q + 1) * n], bank(4 + q)[0:HEADS, 0:n]).then_inc(S["line_copied"], 1)
            v = lambda q: sp[:, q, :]
            are, aim = vec[:, 32:48], vec[:, 48:64]
            DTc, MAG, AD, TH, TH2, SN, CS, ABR, ABI, FR, FI, T0, T1, T2, T3 = range(15)
            eng.wait_ge(S["ldt"], 1)
            tt(v(AD), are, v(DTc), ALU.mult).then_inc(S["ldt"], 1)
            link(tt(v(T0), aim, v(DTc), ALU.mult))
            for q, shift in ((TH, 0.0), (TH2, math.pi / 2)):
                link(eng.tensor_scalar(v(T1), v(T0), shift, None, ALU.add))
                link(eng.tensor_scalar(v(T2), v(T1), 1.0 / TWO_PI, MAGIC, ALU.mult, ALU.add))
                link(eng.tensor_scalar(v(T2), v(T2), -MAGIC, None, ALU.add))
                link(eng.scalar_tensor_tensor(v(T3), v(T2), -TP_HI, v(T1), ALU.mult, ALU.add))
                link(eng.scalar_tensor_tensor(v(T3), v(T2), -TP_LO, v(T3), ALU.mult, ALU.add))
                eng.tensor_scalar(v(q), v(T3), math.pi * (1 - 1e-7), -math.pi * (1 - 1e-7), ALU.min, ALU.max).then_inc(S["ldt"], 1)
            eng.wait_ge(S["sin_done"], 3)
            tt(v(ABR), v(MAG), v(CS), ALU.mult)
            tt(v(ABI), v(MAG), v(SN), ALU.mult)
            tt(v(T0), are, are, ALU.mult)
            link(tt(v(T1), aim, aim, ALU.mult))
            link(tt(v(T0), v(T0), v(T1), ALU.add))
            link(eng.reciprocal(v(T1), v(T0)))
            link(eng.tensor_scalar(v(T0), v(ABR), -1.0, None, ALU.add))
            tt(v(T2), v(T0), are, ALU.mult)
            link(tt(v(T3), v(ABI), aim, ALU.mult))
            link(tt(v(T2), v(T2), v(T3), ALU.add))
            link(tt(v(FR), v(T2), v(T1), ALU.mult))
            tt(v(T2), v(ABI), are, ALU.mult)
            link(tt(v(T3), v(T0), aim, ALU.mult))
            link(tt(v(T2), v(T2), v(T3), ALU.subtract))
            link(tt(v(FI), v(T2), v(T1), ALU.mult))
            eng.wait_ge(S["ssm_in"], 16 * 8)
            eng.memset(bdr, 0.0)
            eng.memset(bdi, 0.0)
            fr, fi = wide(v(FR), 16), wide(v(FI), 16)
            link(tt(bbr, br_, fr, ALU.mult))
            link(tt(bt_, bi_, fi, ALU.mult))
            link(tt(bbr, bbr, bt_, ALU.subtract))
            link(tt(bbi, bi_, fr, ALU.mult))
            link(tt(bt_, br_, fi, ALU.mult))
            link(tt(bbi, bbi, bt_, ALU.add))
            for src, dst in ((bbr, bdr), (bbi, bdi)):
                for half in range(2):
                    r = slice(64 * half, 64 * half + 64)
                    eng.tensor_copy(dst[r, :, 16 * half:16 * half + 16], src[r, :, :]).then_inc(S["bd_ready"], 1)
            eng.wait_ge(S["turned_x"], 10)

            def cmul(o, x, y, n):
                t = [tmp[:, q, :, 0:n] for q in range(4)]
                link(tt(t[0], x[0], y[0], ALU.mult))
                tt(t[1], x[1], y[1], ALU.mult)
                tt(t[2], x[0], y[1], ALU.mult)
                link(tt(t[3], x[1], y[0], ALU.mult))
                tt(o[0], t[0], t[1], ALU.subtract)
                link(tt(o[1], t[2], t[3], ALU.add))

            col = lambda q: [sp[:, 16 + 2 * q + c, :] for c in range(2)]
            flat = lambda c: at(c, 0, [list(c.ap[-1]), [1, 1]])
            eng.tensor_copy(col(0)[0], v(CS))
            link(eng.tensor_copy(col(0)[1], v(SN)))
            cur = 0
            for table, top in ((St, 16), (Jt, 32)):
                eng.memset(table[:, 0, :, 0:1], 1.0)
                link(eng.memset(table[:, 1, :, 0:1], 0.0))
                n = 1
                while n < top:
                    p_ = [wide(c, n) for c in col(cur)]
                    cmul([table[:, c, :, n:2 * n] for c in range(2)], [table[:, c, :, 0:n] for c in range(2)], p_, n)
                    if (table is St) or n * 2 < top:
                        x = [flat(c) for c in col(cur)]
                        cmul([flat(c) for c in col(1 - cur)], x, x, 1)
                        cur = 1 - cur
                    n *= 2
            link(eng.memset(Hs[:, :, :, :].rearrange("p a b c -> p (a b c)"), 0.0))
            eng.memset(CT[:, :, :, :].rearrange("p a b c -> p (a b c)"), 0.0).then_inc(S["theta_ready"], 1)
            inverse(0)
            z_scale(range(4))
            for q in range(2):
                eng.wait_ge(S["bd_turned"], q + 1)
                eng.tensor_copy(BT[:, q, :, :], bank(4 + q).rearrange("p (a b) -> p a b", b=P)).then_inc(S["bd_copied"], 1)
            eng.wait_ge(S["theta_ready"], 1)
            for q in range(2):
                eng.wait_ge(S["c_turned"], q + 1)
                for half in range(2):
                    r = slice(64 * half, 64 * half + 64)
                    src = bank(6 + q)[r, :].rearrange("p (j g c) -> p j g c", g=2, c=16)[:, :, half, :]
                    eng.tensor_scalar(CT[r, q, :, 16 * half:16 * half + 16], src, -1.0 if q else 1.0, None, ALU.mult).then_inc(S["c_copied"], 1)
            eng.wait_ge(S["h0_turned"], 1)
            eng.tensor_copy(h0T[:, :, :], bank(4)[:, 0:256].rearrange("p (a b) -> p a b", b=P)).then_inc(S["h0_copied"], 1)
            z_scale(range(4, 10))
            eng.wait_ge(S["h_out"], 16)
            eng.wait_ge(S["xs_done"], 4)
            eng.wait_ge(S["h0_copied"], 1)
            abr, abi = wide(v(ABR), DB), wide(v(ABI), DB)
            rx = [at(rot, q * T, [[8, 16], [1, 8]]) for q in range(4)]
            for t in range(DT):
                if t == 0:
                    hr, hi = [h0T[:, c, :].rearrange("p (b j) -> p j b", j=16) for c in range(2)]
                else:
                    hr, hi = [Hs[:, c, :, :].rearrange("p j (b t) -> p j b t", t=DT)[:, :, :, t - 1] for c in range(2)]
                xr, xi = [bank(4 + c).rearrange("p (j b t) -> p j b t", b=DB, t=DT)[:, :, :, t] for c in range(2)]
                orr, oii = [Hs[:, c, :, :].rearrange("p j (b t) -> p j b t", t=DT)[:, :, :, t] for c in range(2)]
                tt(rx[0], hr, abr, ALU.mult)
                tt(rx[1], hi, abi, ALU.mult)
                tt(rx[2], hi, abr, ALU.mult)
                link(tt(rx[3], hr, abi, ALU.mult))
                tt(rx[0], rx[0], rx[1], ALU.subtract)
                link(tt(rx[2], rx[2], rx[3], ALU.add))
                tt(orr, rx[0], xr, ALU.add)
                ins = tt(oii, rx[2], xi, ALU.add)
                if t < DT - 1:
                    link(ins)
                else:
                    ins.then_inc(S["samples_done"], 1)
            eng.wait_ge(S["samples_done"], 1)
            for c in range(2):
                eng.tensor_copy(hfin_s[:, c, :].rearrange("p (b j) -> p b j", j=16),
                                Hs[:, c, :, :].rearrange("p j (b t) -> p b j t", t=DT)[:, :, :, DT - 1]).then_inc(S["fin_ready"], 1)
            eng.wait_ge(S["ys_done"], 1)
            eng.wait_ge(S["z_scaled"], 4)
            for c in range(4):
                eng.scalar_tensor_tensor(zsu[:, c, T:TT], zsu[:, c, T:TT], vec[:, 28 + c:29 + c], bank(7)[:, c * NS:(c + 1) * NS], ALU.mult, ALU.add).then_inc(S["ys_taken"], 1)
            z_scale(range(10, 14))
            eng.wait_ge(*done(("ng", 0)))
            tt(halves(zng), pair[pair_of[("ng", 0)]][0:24, :, 0:HT], halves(rs[0:24, :]), ALU.mult).then_inc(taken[pair_of[("ng", 0)]], 1)
            for t in range(5):
                n = P if t < 4 else NS
                eng.wait_ge(S["kvt_done"], 2 * t + 2)
                eng.tensor_copy(vtok[0:n, t, :, :], bank(2 * (t % 2) + 1)[0:n, 0:256].rearrange("p (a b) -> p a b", b=P)).then_inc(S["vtok_copied"], 1)
            eng.wait_ge(S["gates_turned"], 1)
            for t in range(TILES + 1):
                n = P if t < TILES else NS
                eng.tensor_copy(gates[0:n, t, :], bank(5)[0:n, 32 * t:32 * t + 24]).then_inc(S["gates_copied"], 1)
            raw_copy(0)
            eng.wait_ge(S["z_scaled"], 14)
            xp_fill(0)
            raw_copy(1)
            for j in range(16):
                e = [Et[:, j % 2, c, :] for c in range(2)]
                R = [rot[:, q, :] for q in range(6)]
                eng.wait_ge(S["E_ready"], j + 1)
                eng.wait_ge(S["x_done"], j + 1)
                xr, xi = bank(4), bank(5)
                tt(R[0], xr, e[0], ALU.mult)
                tt(R[1], xi, e[1], ALU.mult)
                tt(R[2], xi, e[0], ALU.mult)
                ins = tt(R[3], xr, e[1], ALU.mult)
                ins.then_inc(S["x_taken"], 1)
                eng.wait_ge(S["x_taken"], j + 1)
                tt(R[0], R[0], R[1], ALU.add)
                link(tt(R[2], R[2], R[3], ALU.subtract))
                decay = at(v(MAG), j, [[0, T]])
                eng.tensor_tensor_scan(R[1], decay, R[0], 0.0, ALU.mult, ALU.add)
                link(eng.tensor_tensor_scan(R[3], decay, R[2], 0.0, ALU.mult, ALU.add))
                tt(R[0], R[1], e[0], ALU.mult)
                tt(R[2], R[3], e[1], ALU.mult)
                tt(R[4], R[1], e[1], ALU.mult)
                ins = tt(R[5], R[3], e[0], ALU.mult)
                ins.then_inc(S["E_used"], 1)
                eng.wait_ge(S["E_used"], j + 1)
                if j >= 2:
                    eng.wait_ge(S["y_done"], j - 1)
                tt(Hp[:, j % 2, 0, :], R[0], R[2], ALU.subtract)
                tt(Hp[:, j % 2, 1, :], R[4], R[5], ALU.add).then_inc(S["h_ready"], 1)
                eng.wait_ge(S["h_ready"], j + 1)
                eng.tensor_copy(hfin[:, 0, j:j + 1], Hp[:, j % 2, 0, T - 1:T])
                ins = eng.tensor_copy(hfin[:, 1, j:j + 1], Hp[:, j % 2, 1, T - 1:T])
                if j == 15:
                    ins.then_inc(S["fin_ready"], 1)
                if j % 4 == 0 and j:
                    y_out(j // 4 - 1)
                if j % 4 == 1 and j < 13:
                    raw_copy((j + 3) // 2)
                if j % 4 == 3 and j < 15:
                    raw_copy((j + 3) // 2)
                if j == 3:
                    xp_fill(1)
            y_out(3)
            eng.wait_ge(S["fin_turned"], 4)
            for q in range(4):
                n = 16 if q < 2 else P
                eng.tensor_copy(hout[0:n, q, :], bank(6)[0:n, q * P:(q + 1) * P]).then_inc(S["fin_copied"], 1)
            eng.memset(ce[:, :, CB_P:32], 0.0)
            eng.wait_ge(S["toep_in"], 16 * KV * P // SHIFTS)
            mx, sm = csum[:, 0:32], csum[:, 32:64]
            eng.wait_ge(S["cs_done"], 1)
            for i in range(TILES):
                c0 = 3 * P - P * i + 2 * CH - 1
                src = bank(6 + i // 2)[:, 248 * (i % 2):248 * (i % 2) + 248]
                ins = tt(cs[:, HEADS * i:HEADS * (i + 1), 0:CB_P], src.rearrange("p (a b) -> p a b", b=CB_P),
                         TZ[:, :, c0:c0 + CH * (CB_P - 1) + 1:CH], ALU.add)
            link(ins)
            link(eng.tensor_reduce(mx, cs[:, :, 0:CB_P], AX.X, ALU.max))
            link(eng.tensor_scalar(mx, mx, 0.1 * MASK, None, ALU.max))
            tt(cs[:, :, 0:CB_P], cs[:, :, 0:CB_P], wide(mx, CB_P), ALU.subtract).then_inc(S["cmax_done"], 1)
            eng.wait_ge(S["cexp_done"], 1)
            link(eng.tensor_reduce(sm, ce[:, :, 0:CB_P], AX.X, ALU.add))
            link(eng.tensor_scalar(sm, sm, 1e-30, None, ALU.max))
            link(eng.reciprocal(sm, sm))
            for i in range(TILES):
                by_head = sm[:, HEADS * i:HEADS * (i + 1)].rearrange("p (g k) -> p g k", k=KV)
                ins = tt(by_head, by_head, gates[:, i, :].rearrange("p (k g r) -> p g k r", k=KV, r=3)[:, :, :, 0], ALU.mult)
            link(ins)
            for half in range(2):
                hs = slice(16 * half, 16 * half + 16)
                tt(ce[:, hs, 0:CB_P], ce[:, hs, 0:CB_P], wide(sm[:, hs], CB_P), ALU.mult).then_inc(S["cnorm_done"], 1)
            eng.wait_ge(*done(("glu", 3)))
            for m in range(4):
                eng.wait_ge(*out_of(("glu", m)))
                eng.tensor_tensor(zsu[:, m, :], zsu[:, m, :], glu_sig[:, m, :], ALU.mult).then_inc(S["glu_ready"], 1)
            eng.wait_ge(S["cpt_done"], 2)
            n = 0
            for i in range(TILES):
                W = P * (i + 1)
                for g in range(G):
                    for kv in range(KV):
                        for br in range(2):
                            q = 2 * (n % 2) + br
                            eng.wait_ge(S["s_done"], 2 * n + br + 1)
                            if n >= 2:
                                eng.wait_ge(S["exp_done"], 2 * (n - 2) + br + 1)
                            eng.tensor_tensor_reduce(Ssb[:, q, 0:W], bank(q)[:, 0:W], TZ[:, 2 * g + kv, (3 - i) * P:T], -0.125, 3e38,
                                                     ALU.add, ALU.min, small[:, 2 * (n % 3) + br:2 * (n % 3) + br + 1]).then_inc(S["s_taken"], 1)
                        if n:
                            scale_probs(n - 1)
                        if n % 8 == 1 and n > 1:
                            eng.wait_ge(S["o_done"], n - 1)
                            take_o(i - 1)
                        n += 1
            scale_probs(n - 1)
            eng.wait_ge(S["o_done"], 32)
            take_o(TILES - 1)
            eng.memset(Qb[:, :, :].rearrange("p a b -> p (a b)"), 0.0).then_inc(S["v_step"], 1)
            steps[0] += 1
            eng.wait_ge(S["v_step"], steps[0])
            for kv in range(KV):
                r = slice(64 * kv, 64 * kv + 64)
                eng.tensor_copy(Qb[r, :, 16 * kv:16 * kv + 16].rearrange("p b (g t) -> p b g t", t=DT),
                                zq[r, :, T:TT].rearrange("p g (b t) -> p b g t", t=DT)).then_inc(S["qb_ready"], 1)
            eng.wait_ge(S["biasS_in"], 64)
            eng.wait_ge(S["gate_in"], 16 * DB)
            link(eng.memset(cc[:, 2, CB_S:64], 0.0))
            IO = kc_[:, K_IO:K_IO + NSEL - 3]

            def sample_scores(tile):
                eng.wait_ge(S["sc_done"], tile + 1)
                eng.tensor_tensor_reduce(cc[:, 0, 0:CB_S], bank(6)[:, 0:CB_S], biasS[:, 2 * CH - 1:2 * CH - 1 + CH * (CB_S - 1) + 1:CH], -0.125, 3e38,
                                         ALU.add, ALU.min, small[:, 16:17]).then_inc(S["cmin_done"], 1)
                eng.wait_ge(S["cexps"], tile + 1)
                link(eng.tensor_scalar(small[:, 76:77], small[:, 17:18], 1e-30, None, ALU.max))
                link(eng.reciprocal(small[:, 76:77], small[:, 76:77]))
                link(eng.tensor_scalar(cc[:, 2, 0:CB_S], cc[:, 1, 0:CB_S], small[:, 76:77], None, ALU.mult))
                link(eng.tensor_reduce(small[:, 40:54], cc[:, 2, 4:60].rearrange("p (a b) -> p a b", b=4), AX.X, ALU.add))
                tt(small[:, 40:54], small[:, 40:54], cc[:, 2, 3:56:4], ALU.add).then_inc(S["impsum_ready"], 1)
                eng.tensor_scalar(cc[:, 0, 0:CB_S], cc[:, 2, 0:CB_S], gates_s[:, tile, 0:1], None, ALU.mult).then_inc(S["pc_ready"], 1)
                eng.wait_ge(S["imp_done"], tile + 1)
                eng.tensor_copy(small[:, 40:54], bank(6)[:, 64:78]).then_inc(S["bd_seen"], 1)
                eng.wait_ge(S["bd_seen"], tile + 1)
                link(eng.tensor_reduce(small[:, 72:73], small[:, 40:54], AX.X, ALU.min))
                link(eng.scalar_tensor_tensor(small[:, 56:70], small[:, 40:54], small[:, 72:73], IO, ALU.is_equal, ALU.mult))
                link(eng.tensor_reduce(small[:, 73:74], small[:, 56:70], AX.X, ALU.max))
                link(eng.tensor_scalar(small[:, 56:70], IO, small[:, 73:74], MASK, ALU.is_equal, ALU.mult))
                tt(bd[:, SEL:PAST - SEL].rearrange("p (a b) -> p a b", b=SEL), biasS[:, SEL:PAST - SEL].rearrange("p (a b) -> p a b", b=SEL),
                   wide(small[:, 56:70], SEL), ALU.add)
                eng.tensor_copy(bd[:, 0:SEL], biasS[:, 0:SEL])
                eng.tensor_copy(bd[:, PAST - SEL:PAST], biasS[:, PAST - SEL:PAST])
                own = kc_[:, K_SM + NS * tile:K_SM + NS * tile + NS].rearrange("p (b t) -> p b t", t=DT)
                tt(bd[:, PAST:PAST + NS].rearrange("p (b t) -> p b t", t=DT), wide(biasS[:, PAST:PAST + DT], DB, 1), own, ALU.add)
                tt(bw[:, WIN:WIN + NS].rearrange("p (b t) -> p b t", t=DT), wide(biasS[:, PAST:PAST + DT], DB, 1), own, ALU.add)
                eng.tensor_copy(bw[:, DT:WIN], biasS[:, PAST - WIN + DT:PAST])
                link(tt(bw[:, 0:DT], biasS[:, PAST - WIN:PAST - WIN + DT], kc_[:, K_WM:K_WM + DT], ALU.add))
                eng.wait_ge(S["pc_done"], tile + 1)
                eng.tensor_copy(PTS[0:CB_S, 14 + tile, :], bank(6)[0:CB_S, P:2 * P]).then_inc(S["pc_copied"], 1)
                eng.wait_ge(S["ss_done"], 4 * tile + 4)
                sel = pair[0][:, :, :].rearrange("p a b -> p (a b)")
                link(eng.tensor_tensor_reduce(SS[:, 0:PAST], sel, bd[:, 0:PAST], -0.125, 3e38, ALU.add, ALU.min, small[:, 77:78]))
                eng.tensor_tensor_reduce(SS[:, PAST:PAST + NS], bank(3)[:, 0:NS], bd[:, PAST:PAST + NS], -0.125, small[:, 77:78],
                                         ALU.add, ALU.min, small[:, 18:19]).then_inc(S["ss_taken"], 1)
                link(eng.tensor_tensor_reduce(SW[:, 0:WIN], bank(2), bw[:, 0:WIN], -0.125, 3e38, ALU.add, ALU.min, small[:, 78:79]))
                eng.tensor_tensor_reduce(SW[:, WIN:WIN + NS], bank(3)[:, NS:2 * NS], bw[:, WIN:WIN + NS], -0.125, small[:, 78:79],
                                         ALU.add, ALU.min, small[:, 19:20]).then_inc(S["ss_taken"], 1)

            def sample_sums(tile):
                eng.wait_ge(S["sexp"], 2 * tile + 2)
                if tile:
                    eng.wait_ge(S["tb_done"], 28)
                link(eng.tensor_scalar(small[:, 74:76], small[:, 20:22], 1e-30, None, ALU.max))
                link(eng.reciprocal(small[:, 74:76], small[:, 74:76]))
                for br in range(2):
                    eng.tensor_scalar(dgs[:, br, :], ident, small[:, 74 + br:75 + br], gates_s[:, tile, 1 + br:2 + br], ALU.mult, ALU.mult).then_inc(S["sdiag"], 1)

            def sample_out(tile):
                eng.wait_ge(S["so_done"], 4 * tile + 4)
                for kv in range(KV):
                    r = slice(64 * kv, 64 * kv + 64)
                    src = bank(7)[r, P * tile:P * tile + P].rearrange("p (b k g t) -> p b k g t", k=KV, g=G, t=DT)[:, :, kv, :, :]
                    dst = oT[r, :, T + 16 * tile:T + 16 * tile + 16].rearrange("p g (b t) -> p b g t", t=DT)
                    eng.tensor_copy(dst, src).then_inc(S["so_taken"], 1)

            sample_scores(0)
            sample_sums(0)
            sample_scores(1)
            sample_out(0)
            sample_sums(1)
            sample_out(1)
            for k in range(KC):
                eng.wait_ge(S["in_high"], k + 1)
                tt(mixed_lo[k], mixed_in[k], f32(mixed_hi[k]), ALU.subtract).then_inc(S["in_split"], 1)
            for c in range(KC):
                if c >= 2:
                    eng.wait_ge(S["mixed"], c - 1)
                for q in range(2):
                    scaled(sig[:, 2 * (c % 2) + q, :], (("mg0", "mg1")[q], c))
                for q, nm in enumerate(("att", "ssm")):
                    eng.wait_ge(S["mg_done"], 2 * c + q + 1)
                    eng.wait_ge(*done((nm, c)))
                    eng.tensor_tensor(halves(sig[:, 2 * (c % 2) + q, :]), halves(sig[:, 2 * (c % 2) + q, :]), both(pair_of[(nm, c)]), ALU.mult).then_inc(taken[pair_of[(nm, c)]], 1)
                eng.wait_ge(*out_of(("ssm", c)))
                tt(mT[:, c, :], sig[:, 2 * (c % 2), :], sig[:, 2 * (c % 2) + 1, :], ALU.add).then_inc(S["mixed"], 1)
                if c:
                    mix_low(c - 1)
            mix_low(KC - 1)
            eng.wait_ge(S["h_in"], 16)
            for c in range(KC):
                eng.wait_ge(*done(("wo", c)))
                eng.tensor_tensor(halves(hT[:, c, :]), halves(hT[:, c, :]), both(pair_of[("wo", c)]), ALU.add).then_inc(taken[pair_of[("wo", c)]], 1)
                eng.wait_ge(*out_of(("wo", c)))
                weigh(1, c, 8, hT, u_hi)
            low(1, KC - 1, u_hi)
            inverse(1)
            for c in range(FC):
                if c >= 2:
                    eng.wait_ge(S["mid_new"], c - 1)
                scaled(sil[:, c % 2, :], ("gate", c))
                scaled(mid[:, c, :], ("up", c))
                eng.wait_ge(S["silu_done"], c + 1)
                eng.wait_ge(*out_of(("up", c)))
                tt(mid[:, c, :], mid[:, c, :], sil[:, c % 2, :], ALU.mult).then_inc(S["mid_new"], 1)
                if c:
                    mid_low(c - 1)
            mid_low(FC - 1)
            for c in range(KC):
                eng.wait_ge(*done(("down", c)))
                eng.tensor_tensor(halves(hT[:, c, :]), halves(hT[:, c, :]), both(pair_of[("down", c)]), ALU.add).then_inc(taken[pair_of[("down", c)]], 1)
                eng.wait_ge(*out_of(("down", c)))
                weigh(2, c, 16, hT, u_hi)
            low(2, KC - 1, u_hi)
            for k in range(2):
                eng.wait_ge(*done(("pt", k)))
                eng.tensor_copy(pT[:, k, :], pair[pair_of[("pt", k)]][:, :, :].rearrange("p a b -> p (a b)")[:, 0:TT]).then_inc(taken[pair_of[("pt", k)]], 1)
            inverse(2)
            for c in range(KC):
                if c >= 2:
                    eng.wait_ge(S["h_new"], c - 1)
                scaled(sig[:, c % 2, :], ("pg", c))
                eng.wait_ge(S["gate_done"], c + 1)
                eng.wait_ge(*done(("ple", c)))
                eng.tensor_tensor(halves(sig[:, c % 2, :]), halves(sig[:, c % 2, :]), both(pair_of[("ple", c)]), ALU.mult).then_inc(taken[pair_of[("ple", c)]], 1)
                eng.wait_ge(*out_of(("ple", c)))
                tt(hT[:, c, :], hT[:, c, :], sig[:, c % 2, :], ALU.add).then_inc(S["h_new"], 1)
            eng.wait_ge(S["g_in"], 16)
            for t in range(5):
                n = P if t < 4 else NS
                eng.wait_ge(S["y_root"], t + 1)
                link(eng.reciprocal(small[0:n, 90 + t:91 + t], small[0:n, 85 + t:86 + t]))
                eng.scalar_tensor_tensor(ytok[t][0:n, :], whole(t % 4)[0:n, :], small[0:n, 90 + t:91 + t], g_final[0:n, :], ALU.mult, ALU.mult).then_inc(S["y_made"], 1)

        @block.tensor
        def _(eng):
            rhs_of = {"z": uT, "ng": uT, "mg0": uT, "mg1": uT, "glu": zsu, "att": oT, "ssm": zsu, "wo": mT,
                      "gate": uT, "up": uT, "down": mid, "pg": uT, "ple": pT}
            step_of = dict(groups)
            steps_p = [0]

            def link(ins):
                steps_p[0] += 1
                ins.then_inc(S["p_step"], 1)
                eng.wait_ge(S["p_step"], steps_p[0])

            def gemm(name, ready=None):
                pr, use = pair_of[name], use_of[name]
                if use > 1:
                    eng.wait_ge(taken[pr], use - 1)
                steps = step_of[name]
                src = rhs_of[name[0]]
                seen = set()
                for n, (w, off, m, k) in enumerate(steps):
                    if w is None:
                        lhsT = wple[:, off:off + m]
                    else:
                        if w not in seen:
                            if w in split_index:
                                eng.wait_ge(S["slab_split"], split_index[w] + 1)
                            else:
                                eng.wait_ge(slab_landed[w % RING], landed_at[w])
                            seen.add(w)
                        lhsT = ring[:, w % RING, off:off + m]
                    if ready:
                        eng.wait_ge(*ready(k))
                    if w in split_index:
                        w_hi = ring_r[:, RING + split_index[w] % HI_RING, off:off + m]
                        w_lo = ring_r[:, w % RING, off:off + m]
                        x_hi, x_lo = parts_of(name)
                        for h in range(2):
                            out, cols = pair[pr][0:m, h, 0:HT], slice(h * HT, (h + 1) * HT)
                            eng.matmul(out, w_hi, x_hi(k)[:, cols], start=n == 0, stop=False)
                            eng.matmul(out, w_hi, x_lo(k)[:, cols], start=False, stop=False)
                            ins = eng.matmul(out, w_lo, x_hi(k)[:, cols], start=False, stop=n == len(steps) - 1)
                        if n < len(steps) - 1 and steps[n + 1][0] != w:
                            ins.then_inc(S["part_done"], 1)
                        continue
                    for h in range(2):
                        ins = eng.matmul(pair[pr][0:m, h, 0:HT], lhsT, src[:, k, h * HT:(h + 1) * HT], start=n == 0, stop=n == len(steps) - 1)
                ins.then_inc(sum_done[pr], 1)

            def parts_of(name):
                kind = name[0]
                if kind == "wo":
                    return (lambda k: mT_hi[:, k, :]), (lambda k: mT_lo[:, k, :])
                if kind == "down":
                    return (lambda k: mid_hi[k]), (lambda k: mid_lo[:, k, :])
                if kind in ("att", "ssm"):
                    k0 = 4 if kind == "ssm" else 0
                    return (lambda k: mixed_hi[k0 + k]), (lambda k: mixed_lo[k0 + k])
                hi = u_hi0 if kind in ("z", "ng") else u_hi_mix if kind in ("mg0", "mg1") else u_hi
                return (lambda k: hi[:, k, :]), (lambda k: uT_r[:, k, :])

            def norm(n):
                pr, use = pair_of[("norm", n)], use_of[("norm", n)]
                if use > 1:
                    eng.wait_ge(taken[pr], use - 1)
                for k in range(KC):
                    eng.wait_ge(S["squares"], KC * n + k + 1)
                    for h in range(2):
                        ins = eng.matmul(pair[pr][:, h, 0:HT], ones, sq_of[n][:, k, h * HT:(h + 1) * HT], start=k == 0, stop=k == KC - 1)
                ins.then_inc(sum_done[pr], 1)

            normed = lambda n: lambda k: (S["normed"], KC * n + k + 1)

            def sample_inputs():
                eng.wait_ge(S["h0_copied"], 1)
                for rg in range(4):
                    r = slice(32 * rg, 32 * rg + 32)
                    for c in range(2):
                        for j in range(rg, 16, 4):
                            ins = eng.matmul(bank(4 + c)[:, j * NS:(j + 1) * NS], BT[r, c, j // 4, :], zsu[r, j // 4, T:TT], start=True, stop=True)
                    ins.then_inc(S["xs_done"], 1)
                    if rg < 3:
                        eng.wait_ge(S["xs_done"], rg + 1)

            def sample_outputs():
                eng.wait_ge(S["samples_done"], 1)
                eng.wait_ge(S["c_copied"], 4)
                for cg in range(4):
                    for j in range(cg, 16, 4):
                        for c in range(2):
                            ins = eng.matmul(bank(7)[32 * cg:32 * cg + 32, NS * (j // 4):NS * (j // 4) + NS], CT[:, c, j, :], Hs[:, c, j, :], start=c == 0, stop=c == 1)
                ins.then_inc(S["ys_done"], 1)

            def ssm_maps():
                eng.wait_ge(S["bd_ready"], 4)
                for q, src in enumerate((bdr, bdi)):
                    for k in range(4):
                        ins = eng.transpose(bank(4 + q)[:, k * P:(k + 1) * P], src[:, 4 * k:4 * k + 4, :].rearrange("p a b -> p (a b)"), ident)
                    ins.then_inc(S["bd_turned"], 1)
                eng.wait_ge(S["ssm_in"], 16 * 8)
                for q in range(2):
                    for k in range(4):
                        ins = eng.transpose(bank(6 + q)[:, k * P:(k + 1) * P], cnat[:, q, k, :], ident)
                    ins.then_inc(S["c_turned"], 1)
                eng.wait_ge(S["bd_copied"], 1)
                for q in range(2):
                    ins = eng.transpose(bank(4)[:, q * P:(q + 1) * P], h0nat[:, q, :], ident)
                ins.then_inc(S["h0_turned"], 1)

            eng.wait_ge(S["const_in"], 16)
            eng.wait_ge(S["nat_in"], 16 * 9)
            eng.transpose(bank(2)[:, 0:96], nat[0:96, :], ident[0:96, 0:96]).then_inc(S["vec_turned"], 1)
            eng.wait_ge(S["spread_ready"], 3)
            for q, rows in enumerate((8, 4, 16)):
                ins = eng.transpose(bank(3)[:, 16 * q:16 * q + rows], spread[0:rows, q, :], ident[0:rows, 0:rows])
            ins.then_inc(S["spread_turned"], 1)
            eng.wait_ge(S["x0"], 16 * 5)
            for q in range(10):
                t, kk = q % 5, q // 5
                n = P if t < 4 else NS
                if q >= 2:
                    eng.wait_ge(S["copied_x"], q - 1)
                for c in range(4):
                    k = 4 * kk + c
                    ins = eng.transpose(bank(q % 2)[:, c * P:c * P + n], xtok[0:n, t, k * P:(k + 1) * P], ident[0:n, 0:n])
                ins.then_inc(S["turned_x"], 1)
            eng.wait_ge(S["hot_in"], 32)
            eng.wait_ge(S["ones_set"], 3)
            n = LINE // 4
            for q in range(4):
                eng.matmul(bank(4 + q)[0:HEADS, 0:n], relb, hot[:, q * n:(q + 1) * n], start=True, stop=True).then_inc(S["line_done"], 1)
            for m in range(14):
                if m == 0:
                    eng.wait_ge(S["copied_x"], 10)
                if m == 1:
                    norm(0)
                    eng.wait_ge(S["line_copied"], 4)
                gemm(("z", m), normed(0) if m == 0 else None)
                if m == 8:
                    for q in range(4):
                        eng.wait_ge(*out_of(("z", q)))
                    ssm_maps()
                if m == 10:
                    eng.wait_ge(S["z_scaled"], 4)
                    sample_inputs()
                if m == 13:
                    sample_outputs()
            gemm(("ng", 0))
            for t in range(5):
                n = P if t < 4 else NS
                if t == 0:
                    for m in (12, 13):
                        eng.wait_ge(*out_of(("z", m)))
                    eng.wait_ge(*out_of(("ng", 0)))
                    eng.wait_ge(S["z_scaled"], 14)
                if t >= 2:
                    eng.wait_ge(S["tokst_copied"], t - 1)
                    eng.wait_ge(S["vtok_copied"], t - 1)
                for q, slot in enumerate((0, 1, KS, KW)):
                    ins = eng.transpose(bank(2 * (t % 2))[0:n, q * P:(q + 1) * P], zkv[:, slot, t * P:t * P + n], ident)
                ins.then_inc(S["kvt_done"], 1)
                for q, slot in enumerate((2, 3)):
                    ins = eng.transpose(bank(2 * (t % 2) + 1)[0:n, q * P:(q + 1) * P], zkv[:, slot, t * P:t * P + n], ident)
                ins.then_inc(S["kvt_done"], 1)
            eng.wait_ge(S["samples_done"], 1)
            eng.wait_ge(S["ng_done"], 1)
            for t in range(TILES):
                eng.transpose(bank(5)[:, 32 * t:32 * t + 24], zng[:, t * P:(t + 1) * P], ident[0:24, 0:24])
            ins = eng.transpose(bank(5)[0:NS, 32 * TILES:32 * TILES + 24], zng[:, T:TT], ident[0:24, 0:24])
            ins.then_inc(S["gates_turned"], 1)
            eng.wait_ge(S["gates_copied"], TILES + 1)
            turn = hid = c2 = 0

            def x_in(j):
                if j:
                    eng.wait_ge(S["x_taken"], j)
                r = slice(32 * (j % 4), 32 * (j % 4) + 32)
                for c in range(2):
                    ins = eng.matmul(bank(4 + c), BT[r, c, j // 4, :], zsu[r, j // 4, 0:T], start=True, stop=True)
                ins.then_inc(S["x_done"], 1)

            def y_sum(j):
                eng.wait_ge(S["h_ready"], j + 1)
                if j >= 4 and j % 4 == 0:
                    eng.wait_ge(S["y_taken"], j // 4)
                for c in range(2):
                    ins = eng.matmul(bank(6)[32 * (j % 4):32 * (j % 4) + 32, :], CT[:, c, j, :], Hp[:, j % 2, c, :], start=c == 0, stop=c == 1)
                ins.then_inc(S["y_done"], 1)

            def turns():
                nonlocal turn
                eng.wait_ge(S["raw_copied"], turn // 4 + 1)
                for q in range(4):
                    ckv, ph = q // 2, q % 2
                    if turn >= 2:
                        eng.wait_ge(S["turn_copied"], turn - 1)
                    for c in range(4):
                        col = (4 * ph + c) * 256 + ckv * P
                        ins = eng.transpose(bank(2 + turn % 2)[:, c * P:(c + 1) * P], raw2[:, col:col + P], ident)
                    ins.then_inc(S["raw_turned"], 1)
                    turn += 1

            def hidden(h, half, batch):
                nonlocal hid
                if half == 0 and hid >= 2:
                    eng.wait_ge(S["hid_taken"], hid - 1)
                if half == 0 and h == 0:
                    eng.wait_ge(S["turn_copied"], 8 * (batch + 1))
                out = bank(hid % 2)[:, 0:504].rearrange("p (k b c) -> p k b c", k=KV, c=CB_S)
                for q in range(8):
                    rhs = XT[:, q, :, :].rearrange("p k (b c) -> p k b c", c=64)[:, :, :, half:half + CB_S]
                    ins = eng.matmul(out, w1[:, 8 * half + q, h * P:(h + 1) * P], rhs, start=half == 0 and q == 0, stop=half == 1 and q == 7)
                if half:
                    ins.then_inc(S["hid_done"], 1)
                    hid += 1

            def second(kv):
                nonlocal c2
                eng.wait_ge(S["hid_taken"], hid)
                if c2:
                    eng.wait_ge(S["c2_taken"], c2)
                if c2 % 3 == 0:
                    for quad in range(2 if kv == 0 else 4):
                        for h in range(2):
                            k = quad % 2
                            x = Hq[:, h, CB_P * k:CB_P * (k + 1)]
                            if kv == 0:
                                ins = eng.matmul(bank(7)[64 * k:64 * k + 64, 0:CB_P], w2[:, 0, h, :], x, start=h == 0, stop=h == 1)
                            else:
                                ins = eng.matmul(bank(7)[32 * quad:32 * quad + CB_P, 0:HD], x, w2[:, 1, h, :], start=h == 0, stop=h == 1)
                elif kv == 0:
                    for k in range(KV):
                        for h in range(2):
                            ins = eng.matmul(bank(7)[64 * k:64 * k + 64, 0:252], w2[:, 0, h, :], Hh[:, h, 252 * k:252 * k + 252], start=h == 0, stop=h == 1)
                else:
                    for b in range(4):
                        for k in range(KV):
                            for h in range(2):
                                x = Hh[:, h, 252 * k + CB_S * b:252 * k + CB_S * (b + 1)]
                                ins = eng.matmul(bank(7)[0:CB_S, P * b + HD * k:P * b + HD * (k + 1)], x, w2[:, 1, h, :], start=h == 0, stop=h == 1)
                ins.then_inc(S["c2_done"], 1)
                c2 += 1

            def prompt_hidden(kv):
                nonlocal hid
                eng.wait_ge(S["w1_in"], 16 * (kv + 1))
                eng.wait_ge(S["xp_ready"], kv + 1)
                for h in range(2):
                    if hid >= 2:
                        eng.wait_ge(S["hid_taken"], hid - 1)
                    for q in range(16):
                        ins = eng.matmul(bank(hid % 2)[:, 0:63], w1[:, q, h * P:(h + 1) * P], XP[:, q, 0:63], start=q == 0, stop=q == 15)
                    ins.then_inc(S["hid_done"], 1)
                    hid += 1
                eng.wait_ge(S["w2_in"], 32)
                second(kv)

            eng.wait_ge(S["ys_taken"], 4)
            eng.wait_ge(S["tokst_copied"], 5)
            eng.wait_ge(S["vtok_copied"], 5)
            for j in range(16):
                if j:
                    y_sum(j - 1)
                x_in(j)
                batch = j // 4
                if j % 4 == 0:
                    turns()
                    if batch % 2 == 0:
                        prompt_hidden(batch // 2)
                    turns()
                hidden(j // 2 % 2, j % 2, batch)
                if j % 4 == 3:
                    second(batch // 2)
            y_sum(15)
            eng.wait_ge(S["fin_ready"], 3)
            eng.wait_ge(S["y_taken"], 4)
            for q in range(2):
                eng.transpose(bank(6)[0:16, q * P:(q + 1) * P], hfin[:, q, :], ident).then_inc(S["fin_turned"], 1)
            for q in range(2):
                eng.transpose(bank(6)[:, (2 + q) * P:(3 + q) * P], hfin_s[:, q, :], ident).then_inc(S["fin_turned"], 1)
            eng.wait_ge(S["hid_taken"], 12)
            eng.wait_ge(S["fin_copied"], 4)
            eng.wait_ge(S["c2_taken"], 6)
            eng.wait_ge(S["x_taken"], 16)
            for m in range(4):
                gemm(("glu", m), (lambda k: (S["z_ready"], k + 1)) if m == 0 else None)
                if m >= KV:
                    continue
                for i in range(TILES):
                    for g in range(G):
                        h = KV * g + m
                        r = slice(64 * m, 64 * m + 64)
                        c0 = 248 * (i % 2) + h * CB_P
                        ins = eng.matmul(bank(6 + i // 2)[:, c0:c0 + CB_P], zq[r, g, i * P:(i + 1) * P], kcT_p[r, 0:CB_P], start=True, stop=True)
                if m == KV - 1:
                    ins.then_inc(S["cs_done"], 1)
                else:
                    link(ins)
            for m in range(4):
                eng.wait_ge(*out_of(("glu", m)))
            for half in range(2):
                eng.wait_ge(S["cnorm_done"], half + 1)
                for q in range(4):
                    h0 = 16 * half + 4 * q
                    ins = eng.transpose(bank(4 + half)[:, q * P:(q + 1) * P], ce[:, h0:h0 + 4, :].rearrange("p a b -> p (a b)"), ident)
                ins.then_inc(S["cpt_done"], 1)

            def scores(n):
                i, h = n // 8, n % 8
                g, k, W = h // KV, h % KV, P * (i + 1)
                r = slice(64 * k, 64 * k + 64)
                for br in range(2):
                    if n >= 2:
                        eng.wait_ge(S["s_taken"], 2 * (n - 2) + br + 1)
                    eng.matmul(bank(2 * (n % 2) + br)[:, 0:W], zq[r, g, i * P:(i + 1) * P], zkv[r, (KS, KW)[br], 0:W], start=True, stop=True).then_inc(S["s_done"], 1)

            def turn_probs(n):
                i = n // 8
                for br in range(2):
                    q = 2 * (n % 3) + br
                    eng.wait_ge(S["probs_ready"], 2 * n + br + 1)
                    if n:
                        eng.wait_ge(S["pt_copied"], 2 * (n - 1) + br + 1)
                    for c in range(i + 1):
                        ins = eng.transpose(bank(4 + br)[:, c * P:(c + 1) * P], Psb[q][:, c * P:(c + 1) * P], ident)
                    ins.then_inc(S["pt_done"], 1)

            def values(n):
                i, h = n // 8, n % 8
                g, k = h // KV, h % KV
                if n % 8 == 0 and i:
                    eng.wait_ge(S["o_taken"], i)
                out = bank(6)[64 * k:64 * k + 64, g * P:(g + 1) * P]
                quad = (g % 2) * 2 + k
                r = slice(32 * quad, 32 * quad + CB_P)
                eng.wait_ge(S["cpt_copied"], 2)
                if n >= 2:
                    eng.wait_ge(S["o_done"], n - 1)
                eng.matmul(out, vc_p[r, :], PTc[r, i, g // 2, :], start=True, stop=False)
                eng.wait_ge(S["pt_copied"], 2 * n + 2)
                for br in range(2):
                    for c in range(i + 1):
                        last = br == 1 and c == i
                        ins = eng.matmul(out, vtok[:, c, br, 64 * k:64 * k + 64], PTs[:, 2 * (n % 2) + br, c * P:(c + 1) * P], start=False, stop=last)
                ins.then_inc(S["o_done"], 1)

            scores(0)
            scores(1)
            for n in range(32):
                if n + 2 < 32:
                    scores(n + 2)
                turn_probs(n)
                if n:
                    values(n - 1)
            values(31)
            tb = 0

            def tb_bank():
                if tb >= 2:
                    eng.wait_ge(S["tb_copied"], tb - 1)
                return bank(4 + tb % 2)

            eng.wait_ge(S["qb_ready"], 2)
            eng.wait_ge(S["pt_copied"], 64)
            eng.wait_ge(S["o_taken"], 4)

            def turn_keys(b):
                nonlocal tb
                eng.wait_ge(ksel_in[b % 2], 16 * (b // 2 + 1))
                for j0 in (0, 4):
                    bk = tb_bank()
                    for c in range(4):
                        ins = eng.transpose(bk[:, c * P:(c + 1) * P], ksel[:, b % 2, (j0 + c) * P:(j0 + c + 1) * P], ident)
                    ins.then_inc(S["tb_done"], 1)
                    tb += 1
                bk = tb_bank()
                for c in range(4):
                    ins = eng.transpose(bk[:, c * P:(c + 1) * P], kwin[:, b % 4, c * P:(c + 1) * P], ident)
                ins.then_inc(S["tb_done"], 1)
                tb += 1

            def keys(tile):
                if tile:
                    eng.wait_ge(S["pc_copied"], tile)
                for b in range(4):
                    ins = eng.matmul(bank(6)[32 * b:32 * b + 32, 0:CB_S], Qb[:, 4 * tile + b, :], kcT_s[:, tile, CB_S * b:CB_S * (b + 1)], start=True, stop=True)
                ins.then_inc(S["sc_done"], 1)
                eng.wait_ge(S["kwin_in"], 16 * (tile + 1))
                first = 4 * tile
                turn_keys(first)
                for b in range(first, first + 4):
                    if b < first + 3:
                        turn_keys(b + 1)
                    eng.wait_ge(S["tb_copied"], keys_turned(b))
                    if tile and b == first:
                        eng.wait_ge(S["ss_taken"], 2)
                    r = slice(32 * (b % 4), 32 * (b % 4) + 32)
                    q = Qb[:, b, :]
                    eng.matmul(bank(0)[r, :], q, KT[:, b % 2, 0:512], start=True, stop=True)
                    eng.matmul(bank(1)[r, :], q, KT[:, b % 2, 512:1024], start=True, stop=True)
                    eng.matmul(bank(2)[r, :], q, KTw[:, b % 2, :], start=True, stop=True)
                    eng.matmul(bank(3)[r, 0:NS], q, zkv[:, KS, T:TT], start=True, stop=True)
                    eng.matmul(bank(3)[r, NS:2 * NS], q, zkv[:, KW, T:TT], start=True, stop=True).then_inc(S["ss_done"], 1)
                    if b == first + 1:
                        eng.wait_ge(S["impsum_ready"], tile + 1)
                        eng.matmul(bank(6)[:, 64:78], kc_[:, K_G:K_G + P], small[:, 40:54], start=True, stop=True).then_inc(S["imp_done"], 1)
                    if b == first + 2:
                        eng.wait_ge(S["pc_ready"], tile + 1)
                        eng.wait_ge(S["bd_seen"], tile + 1)
                        eng.transpose(bank(6)[0:CB_S, P:2 * P], cc[:, 0, 0:CB_S], ident).then_inc(S["pc_done"], 1)

            def outputs(tile):
                nonlocal tb
                eng.wait_ge(S["sdiag"], 2 * tile + 2)
                for j0 in (0, 4):
                    bk = tb_bank()
                    for c in range(4):
                        ins = eng.matmul(bk[:, c * P:(c + 1) * P], PS_[:, j0 + c:j0 + c + 8 * (P - 1) + 1:8], dgs[:, 0, :], start=True, stop=True)
                    ins.then_inc(S["tb_done"], 1)
                    tb += 1
                bk = tb_bank()
                for c in range(4):
                    ins = eng.matmul(bk[:, c * P:(c + 1) * P], PW[:, c:c + 4 * (P - 1) + 1:4], dgs[:, 1, :], start=True, stop=True)
                ins.then_inc(S["tb_done"], 1)
                tb += 1
                bk = tb_bank()
                eng.matmul(bk[0:NS, 0:P], PS_[:, PAST:PAST + NS], dgs[:, 0, :], start=True, stop=True)
                eng.matmul(bk[0:NS, P:2 * P], PW[:, WIN:WIN + NS], dgs[:, 1, :], start=True, stop=True).then_inc(S["tb_done"], 1)
                tb += 1
                eng.wait_ge(S["tb_copied"], tb)
                eng.wait_ge(S["pc_copied"], tile + 1)
                eng.wait_ge(S["vwin_in"], 16 * (tile + 1))
                if tile:
                    eng.wait_ge(S["so_taken"], 2)
                for b in range(4 * tile, 4 * tile + 4):
                    bl = b % 4
                    c = slice(32 * bl, 32 * bl + 32)
                    out = bank(7)[:, 32 * b:32 * b + 32]
                    eng.wait_ge(vsel_in[b % 4], 16 * (b // 4 + 1))
                    eng.matmul(out, vc_s[0:CB_S, b, :], PTS[0:CB_S, 14 + tile, c], start=True, stop=False)
                    for j in range(8):
                        eng.matmul(out, vsel[:, bl, j * P:(j + 1) * P], PTS[:, j, c], start=False, stop=False)
                    for j in range(4):
                        eng.matmul(out, vwin[:, bl, j * P:(j + 1) * P], PTS[:, 9 + j, c], start=False, stop=False)
                    eng.matmul(out, vtok[0:NS, 4, 0, :], PTS[0:NS, 8, c], start=False, stop=False)
                    eng.matmul(out, vtok[0:NS, 4, 1, :], PTS[0:NS, 13, c], start=False, stop=True).then_inc(S["so_done"], 1)

            keys(0)
            keys(1)
            outputs(0)
            outputs(1)
            eng.wait_ge(S["so_taken"], 4)
            eng.wait_ge(S["glu_ready"], 4)
            for c in range(KC):
                for nm in ("mg0", "mg1", "att", "ssm"):
                    if (nm, c) == ("att", 0):
                        eng.wait_ge(S["in_split"], KC)
                    gemm((nm, c), (lambda k: (S["u_returned"], k + 1)) if (nm, c) == ("mg0", 0) else None)
            for c in range(KC):
                gemm(("wo", c), (lambda k: (S["mix_split"], k + 1)) if c == 0 else None)
            for c in range(FC):
                gemm(("gate", c), normed(1) if c == 0 else None)
                if c == 0:
                    norm(1)
                gemm(("up", c))
            for c in range(KC):
                gemm(("down", c), (lambda k: (S["mid_split"], k + 1)) if c == 0 else None)
            eng.wait_ge(S["p_in"], 32)
            for k in range(2):
                pr, use = pair_of[("pt", k)], use_of[("pt", k)]
                eng.wait_ge(taken[pr], use - 1)
                flat = pair[pr][:, :, :].rearrange("p a b -> p (a b)")
                for t in range(5):
                    n = P if t < 4 else NS
                    ins = eng.transpose(flat[:, t * P:t * P + n], ptok[0:n, t, k * P:(k + 1) * P], ident[0:n, 0:n])
                ins.then_inc(sum_done[pr], 1)
            for c in range(KC):
                gemm(("pg", c), normed(2) if c == 0 else None)
                if c == 0:
                    norm(2)
                    eng.wait_ge(S["wple_in"], 16)
                    for k in range(2):
                        eng.wait_ge(*out_of(("pt", k)))
                gemm(("ple", c))
            for name in (("pg", KC - 2), ("ple", KC - 2), ("pg", KC - 1), ("ple", KC - 1)):
                eng.wait_ge(*out_of(name))
            for t in range(5):
                n = P if t < 4 else NS
                if t == 4:
                    eng.wait_ge(S["y_made"], 1)
                for k in range(KC):
                    if t == 0:
                        eng.wait_ge(S["h_new"], k + 1)
                    ins = eng.transpose(whole(t % 4)[0:n, k * P:(k + 1) * P], hT[:, k, t * P:t * P + n], ident)
                ins.then_inc(S["y_turned"], 1)


_INS = """x_prompt x_sample cache_k_cmp cache_v_cmp cache_k_sel cache_v_sel cache_k_win cache_v_win state_ssm_re state_ssm_im
page_table p_prompt p_sample rel_bias final_norm attn_norm w_in cmp_pe_k cmp_w1_k cmp_w2_k cmp_pe_v cmp_w1_v cmp_w2_v ssm_a_re
ssm_a_im ssm_log_dt ssm_b_re ssm_b_im ssm_c_re ssm_c_im ssm_d w_glu b_glu w_att_br w_ssm_br w_o ffn_norm w_ffn_gate w_ffn_up
w_ffn_down ple_norm w_ple_gate w_ple""".split()
_KVP, _KVS, _WINS = (1, 1, T, KV, HD), (1, DB, DT, KV, HD), (1, DB, WIN, KV, HD)
_OUTS = [("y_prompt", (1, T, D)), ("y_sample", (DB, DT, D)),
         ("nk_cmp_p", _KVP), ("nv_cmp_p", _KVP), ("nk_sel_p", _KVP), ("nv_sel_p", _KVP), ("nk_win_p", _KVP), ("nv_win_p", _KVP),
         ("ns_re_p", (1, 1, SG, SP_)), ("ns_im_p", (1, 1, SG, SP_)),
         ("nk_cmp_s", _KVS), ("nv_cmp_s", _KVS), ("nk_sel_s", _KVS), ("nv_sel_s", _KVS), ("nk_win_s", _WINS), ("nv_win_s", _WINS),
         ("ns_re_s", (1, DB, SG, SP_)), ("ns_im_s", (1, DB, SG, SP_))]


def kernel(**inputs):
    import concourse.bacc as bacc
    from concourse.bass_utils import run_bass_kernel_spmd

    nc = bacc.Bacc("TRN2", target_bir_lowering=False, num_devices=1)
    arrays = {n: np.ascontiguousarray(inputs[n]) for n in _INS}
    arrays["consts"] = constants()
    arrays["buckets"] = bucket_table()
    a = {n: nc.dram_tensor("in_" + n, v.shape, mybir.dt.from_np(v.dtype), kind="ExternalInput").ap() for n, v in arrays.items()}
    for n, shape in _OUTS:
        a[n] = nc.dram_tensor("out_" + n, shape, F32, kind="ExternalOutput").ap()
    build(nc, a)
    r = run_bass_kernel_spmd(nc, [{"in_" + n: v for n, v in arrays.items()}], core_ids=[0])
    return tuple(r.results[0]["out_" + n] for n, _ in _OUTS)
```
